# Optimizing a Trainium2 kernel written in Bass

```python
import math
import jax
import jax.numpy as jnp
from jax import lax
import numpy as np

D_MODEL = 1024
BATCH = 1
SEQ = 256
DEPTH = 2

HEAD_DIM = 64
DIL_GROUPS = ((128, 1), (512, 4), (2048, 16))
HEADS_PER_DIL_GROUP = 4
N_HEADS_A = HEADS_PER_DIL_GROUP * len(DIL_GROUPS)
N_HEADS_B = 6
N_HEADS_C = 6
N_HEADS = N_HEADS_A + N_HEADS_B + N_HEADS_C
MIX_WIDTH = N_HEADS * HEAD_DIM
WIDTH_A = HEADS_PER_DIL_GROUP * HEAD_DIM
WIDTH_B = N_HEADS_B * HEAD_DIM
WIDTH_C = N_HEADS_C * HEAD_DIM
ROPE_DIM = HEAD_DIM // 4
ROPE_THETA = 500000.0
MOBA_BLOCK = 256
MOBA_TOPK = 3
MOBA_QCHUNK = 32
SB_QBLOCK = 128
D_FF = 4 * D_MODEL
N_BRANCHES = 3
NORM_EPS = 1e-6
IN_COLS = 3 * MIX_WIDTH + N_BRANCHES * D_MODEL


def rmsnorm(x, g):
    xf = x.astype(jnp.float32)
    y = xf * lax.rsqrt(jnp.mean(xf * xf, axis=-1, keepdims=True) + NORM_EPS)
    return (y * g.astype(jnp.float32)).astype(x.dtype)

def partial_rope(t, pos):
    inv_freq = jnp.exp(-math.log(ROPE_THETA) * jnp.arange(0, ROPE_DIM, 2, dtype=jnp.float32) / ROPE_DIM)
    ang = pos[:, None] * inv_freq[None, :]
    cos, sin = jnp.cos(ang), jnp.sin(ang)
    half = ROPE_DIM // 2
    x1, x2, rest = t[..., :half], t[..., half:ROPE_DIM], t[..., ROPE_DIM:]
    return jnp.concatenate([x1 * cos - x2 * sin, x2 * cos + x1 * sin, rest], axis=-1)

def dilated_window_attention(q, k, v, window, dilation):
    B, H, S, Dh = q.shape
    span = window // dilation
    blk = span
    unit = dilation * blk
    L = -(-S // unit) * unit
    nb = L // unit
    pad = ((0, 0), (0, 0), (0, L - S), (0, 0))

    def split(t):
        t = jnp.pad(t, pad).reshape(B, H, L // dilation, dilation, Dh)
        return jnp.swapaxes(t, 2, 3).reshape(B, H, dilation, nb, blk, Dh)

    def with_prev(t):
        prev = jnp.concatenate([jnp.zeros_like(t[:, :, :, :1]), t[:, :, :, :-1]], axis=3)
        return jnp.concatenate([prev, t], axis=4)

    qb = split(q)
    kc, vc = with_prev(split(k)), with_prev(split(v))
    s = jnp.einsum('bhrnqd,bhrnkd->bhrnqk', qb, kc) * (Dh ** -0.5)
    qi = jnp.arange(blk)[:, None]
    kj = jnp.arange(2 * blk)[None, :]
    dist = qi + blk - kj
    band = (dist >= 0) & (dist <= span)
    first = (jnp.arange(nb) == 0)[:, None, None]
    mask = band[None] & ~(first & (kj < blk)[None])
    s = jnp.where(mask, s, -jnp.inf)
    m = jnp.max(s, axis=-1, keepdims=True)
    p = jnp.exp(s - m)
    l = jnp.sum(p, axis=-1, keepdims=True)
    o = jnp.einsum('bhrnqk,bhrnkd->bhrnqd', p, vc) / l
    lse = (m + jnp.log(l))[..., 0]

    def merge(t):
        tail = t.shape[5:]
        t = t.reshape((B, H, dilation, L // dilation) + tail)
        return jnp.swapaxes(t, 2, 3).reshape((B, H, L) + tail)[:, :, :S]

    return merge(o), merge(lse)

def dilated_mixture(q, k, v):
    outs, lses = [], []
    for g, (w, d) in enumerate(DIL_GROUPS):
        sl = slice(g * HEADS_PER_DIL_GROUP, (g + 1) * HEADS_PER_DIL_GROUP)
        o, lse = dilated_window_attention(q[:, sl], k[:, sl], v[:, sl], w, d)
        outs.append(o)
        lses.append(lse)
    o = jnp.stack(outs, axis=0)
    wgt = jax.nn.softmax(jnp.stack(lses, axis=0), axis=0)
    return jnp.sum(wgt[..., None] * o, axis=0)

def moba_attention(q, k, v):
    B, H, S, Dh = q.shape
    L = -(-S // MOBA_BLOCK) * MOBA_BLOCK
    nblk = L // MOBA_BLOCK
    topk = min(MOBA_TOPK, nblk)
    pad = ((0, 0), (0, 0), (0, L - S), (0, 0))
    qp, kp, vp = jnp.pad(q, pad), jnp.pad(k, pad), jnp.pad(v, pad)
    kblocks = kp.reshape(B, H, nblk, MOBA_BLOCK, Dh)
    vblocks = vp.reshape(B, H, nblk, MOBA_BLOCK, Dh)
    kmean = jnp.mean(kblocks, axis=3)
    scale = Dh ** -0.5
    gather = jax.vmap(jax.vmap(lambda blocks, idx: blocks[idx]))

    def chunk(c):
        start = c * MOBA_QCHUNK
        qc = lax.dynamic_slice_in_dim(qp, start, MOBA_QCHUNK, axis=2)
        qpos = start + jnp.arange(MOBA_QCHUNK)
        own = start // MOBA_BLOCK
        gate = jnp.einsum('bhqd,bhnd->bhqn', qc, kmean)
        gate = jnp.where((jnp.arange(nblk) < own)[None, None, None, :], gate, -jnp.inf)
        _, idx = lax.top_k(gate, topk)
        valid = idx < own
        ksel = gather(kblocks, idx)
        vsel = gather(vblocks, idx)
        s_sel = jnp.einsum('bhqd,bhqjkd->bhqjk', qc, ksel) * scale
        s_sel = jnp.where(valid[..., None], s_sel, -jnp.inf).reshape(B, H, MOBA_QCHUNK, topk * MOBA_BLOCK)
        kown = lax.dynamic_index_in_dim(kblocks, own, axis=2, keepdims=False)
        vown = lax.dynamic_index_in_dim(vblocks, own, axis=2, keepdims=False)
        s_own = jnp.einsum('bhqd,bhkd->bhqk', qc, kown) * scale
        kpos = own * MOBA_BLOCK + jnp.arange(MOBA_BLOCK)
        s_own = jnp.where(kpos[None, :] <= qpos[:, None], s_own, -jnp.inf)
        p = jax.nn.softmax(jnp.concatenate([s_own, s_sel], axis=-1), axis=-1)
        p_own = p[..., :MOBA_BLOCK]
        p_sel = p[..., MOBA_BLOCK:].reshape(B, H, MOBA_QCHUNK, topk, MOBA_BLOCK)
        return (jnp.einsum('bhqk,bhkd->bhqd', p_own, vown)
                + jnp.einsum('bhqjk,bhqjkd->bhqd', p_sel, vsel))

    o = lax.map(chunk, jnp.arange(L // MOBA_QCHUNK))
    return jnp.moveaxis(o, 0, 2).reshape(B, H, L, Dh)[:, :, :S]

def stick_breaking_attention(q, k, v):
    B, H, S, Dh = q.shape
    scale = Dh ** -0.5
    outs = []
    for start in range(0, S, SB_QBLOCK):
        end = min(start + SB_QBLOCK, S)
        z = jnp.einsum('bhqd,bhkd->bhqk', q[:, :, start:end], k[:, :, :end]) * scale
        causal = jnp.arange(end)[None, :] < jnp.arange(start, end)[:, None]
        log_1m = jnp.where(causal, jax.nn.log_sigmoid(-z), 0.0)
        suffix = lax.cumsum(log_1m, axis=3, reverse=True) - log_1m
        a = jnp.where(causal, jnp.exp(jax.nn.log_sigmoid(z) + suffix), 0.0)
        outs.append(jnp.einsum('bhqk,bhkd->bhqd', a, v[:, :, :end]))
    return jnp.concatenate(outs, axis=2)

def hybrid_layer(x, norm_mix, w_in, w_out_a, w_out_b, w_out_c, w_o, norm_mlp, w_up, w_down, pos):
    B, S, D = x.shape
    h = rmsnorm(x, norm_mix)
    proj = h @ w_in

    def heads(t):
        return t.reshape(B, S, N_HEADS, HEAD_DIM).transpose(0, 2, 1, 3).astype(jnp.float32)

    q = heads(proj[..., :MIX_WIDTH])
    k = heads(proj[..., MIX_WIDTH:2 * MIX_WIDTH])
    v = heads(proj[..., 2 * MIX_WIDTH:3 * MIX_WIDTH])
    gates = jax.nn.sigmoid(proj[..., 3 * MIX_WIDTH:]).reshape(B, S, N_BRANCHES, D)

    n_rot = N_HEADS_A + N_HEADS_B
    q = jnp.concatenate([partial_rope(q[:, :n_rot], pos), q[:, n_rot:]], axis=1)
    k = jnp.concatenate([partial_rope(k[:, :n_rot], pos), k[:, n_rot:]], axis=1)

    a_sl = slice(0, N_HEADS_A)
    b_sl = slice(N_HEADS_A, N_HEADS_A + N_HEADS_B)
    c_sl = slice(N_HEADS_A + N_HEADS_B, N_HEADS)
    o_a = dilated_mixture(q[:, a_sl], k[:, a_sl], v[:, a_sl])
    o_b = moba_attention(q[:, b_sl], k[:, b_sl], v[:, b_sl])
    o_c = stick_breaking_attention(q[:, c_sl], k[:, c_sl], v[:, c_sl])

    def flat(o):
        return o.transpose(0, 2, 1, 3).reshape(B, S, -1).astype(x.dtype)

    y_a = flat(o_a) @ w_out_a
    y_b = flat(o_b) @ w_out_b
    y_c = flat(o_c) @ w_out_c
    merged = gates[:, :, 0] * y_a + gates[:, :, 1] * y_b + gates[:, :, 2] * y_c
    x = x + merged @ w_o

    h = rmsnorm(x, norm_mlp)
    return x + jnp.square(jax.nn.relu(h @ w_up)) @ w_down

def first_inputs(seed: int = 0) -> dict:
    key = jax.random.key(seed)
    ks = jax.random.split(key, 12)
    f32 = jnp.float32

    def nrm(k, shape, fan_in):
        return jax.random.normal(k, shape, f32) * (fan_in ** -0.5)

    x = jax.random.normal(ks[0], (BATCH, SEQ, D_MODEL), f32)
    norm_mix = 1.0 + 0.05 * jax.random.normal(ks[1], (DEPTH, D_MODEL), f32)
    w_in = nrm(ks[2], (DEPTH, D_MODEL, IN_COLS), D_MODEL)
    w_out_a = nrm(ks[3], (DEPTH, WIDTH_A, D_MODEL), WIDTH_A)
    w_out_b = nrm(ks[4], (DEPTH, WIDTH_B, D_MODEL), WIDTH_B)
    w_out_c = nrm(ks[5], (DEPTH, WIDTH_C, D_MODEL), WIDTH_C)
    w_o = nrm(ks[6], (DEPTH, D_MODEL, D_MODEL), D_MODEL)
    norm_mlp = 1.0 + 0.05 * jax.random.normal(ks[7], (DEPTH, D_MODEL), f32)
    w_up = nrm(ks[8], (DEPTH, D_MODEL, D_FF), D_MODEL)
    w_down = nrm(ks[9], (DEPTH, D_FF, D_MODEL), D_FF)
    norm_final = 1.0 + 0.05 * jax.random.normal(ks[10], (D_MODEL,), f32)
    return {"x": x, "norm_mix": norm_mix, "w_in": w_in, "w_out_a": w_out_a,
            "w_out_b": w_out_b, "w_out_c": w_out_c, "w_o": w_o, "norm_mlp": norm_mlp,
            "w_up": w_up, "w_down": w_down, "norm_final": norm_final}

def first_block(x, norm_mix, w_in, w_out_a, w_out_b, w_out_c, w_o, norm_mlp, w_up, w_down, norm_final):
    pos = jnp.arange(x.shape[1], dtype=jnp.float32)
    for layer in range(DEPTH):
        x = hybrid_layer(x, norm_mix[layer], w_in[layer], w_out_a[layer], w_out_b[layer],
                         w_out_c[layer], w_o[layer], norm_mlp[layer], w_up[layer],
                         w_down[layer], pos)
    return rmsnorm(x, norm_final)


GRID_W = 64
CTX_LEN = 256
MIX_WIDTH_2 = D_MODEL
GROUP_WIDTH = MIX_WIDTH_2 // 2
N_Q_HEADS = GROUP_WIDTH // HEAD_DIM
N_KV_HEADS = N_Q_HEADS // 4
KV_WIDTH = N_KV_HEADS * HEAD_DIM
HYENA_WIDTH = GROUP_WIDTH
HYENA_ORDER = 2
HYENA_SHORT_CONV = 3
HYENA_EMB = 33
HYENA_HIDDEN = 64
HYENA_DECAY_TARGET = 1e-2
HYENA_SHORT_DECAY_PCT = 0.3
HYENA_LONG_DECAY_PCT = 1.5
Q_BLOCK = 128
WINDOW = 128
NA_ROWS = 8
NA_COLS = 16
ROPE_THETA_2 = 10000.0
EPS = 1e-6
NEG_INF = -1e30
N_EVEN = (DEPTH + 1) // 2
N_ODD = DEPTH // 2
EVEN_SPLITS = (GROUP_WIDTH, KV_WIDTH, KV_WIDTH, (HYENA_ORDER + 1) * HYENA_WIDTH, GROUP_WIDTH, HYENA_WIDTH)
ODD_SPLITS = (GROUP_WIDTH, KV_WIDTH, KV_WIDTH, GROUP_WIDTH, GROUP_WIDTH, GROUP_WIDTH, GROUP_WIDTH, GROUP_WIDTH)
IN_WIDTH = sum(EVEN_SPLITS)


def rms_norm(x, g):
    xf = x.astype(jnp.float32)
    y = xf * lax.rsqrt(jnp.mean(xf * xf, axis=-1, keepdims=True) + EPS)
    return (y * g.astype(jnp.float32)).astype(x.dtype)

def adaln(cond, w, b):
    m = jnp.matmul(jax.nn.silu(cond), w) + b
    return jnp.split(m, 3, axis=-1)

def modulated_norm(x, g, shift, scale):
    return rms_norm(x, g) * (1 + scale) + shift

def split_cols(p, sizes):
    idx = [int(v) for v in np.cumsum(sizes)[:-1]]
    return jnp.split(p, idx, axis=-1)

def heads(t, n):
    return t.reshape(t.shape[0], t.shape[1], n, HEAD_DIM)

def axial_rope_tables(n_tokens):
    t = jnp.arange(n_tokens, dtype=jnp.int32)
    row = (t // GRID_W).astype(jnp.float32)
    col = (t % GRID_W).astype(jnp.float32)
    n_pairs = HEAD_DIM // 4
    inv = ROPE_THETA_2 ** (-jnp.arange(n_pairs, dtype=jnp.float32) / n_pairs)
    ang = jnp.concatenate([row[:, None] * inv, col[:, None] * inv], axis=-1)
    return jnp.cos(ang), jnp.sin(ang)

def apply_rope(x, cos, sin):
    b, n, h, dh = x.shape
    xf = x.astype(jnp.float32).reshape(b, n, h, dh // 2, 2)
    x0, x1 = xf[..., 0], xf[..., 1]
    cs, sn = cos[None, :, None, :], sin[None, :, None, :]
    out = jnp.stack([x0 * cs - x1 * sn, x0 * sn + x1 * cs], axis=-1)
    return out.reshape(b, n, h, dh).astype(x.dtype)

def context_attention(q_ctx, k_ctx, v_ctx, sink_logit=None):
    b, n, h, dh = q_ctx.shape
    kv = k_ctx.shape[2]
    g = h // kv
    qg = q_ctx.reshape(b, n, kv, g, dh)
    sc = jnp.einsum('bqkgd,bckd->bkgqc', qg, k_ctx).astype(jnp.float32) * dh ** -0.5
    if sink_logit is not None:
        sink = jnp.broadcast_to(sink_logit.astype(jnp.float32).reshape(1, kv, g, 1, 1), sc.shape[:-1] + (1,))
        p = jax.nn.softmax(jnp.concatenate([sc, sink], axis=-1), axis=-1)[..., :-1]
    else:
        p = jax.nn.softmax(sc, axis=-1)
    o = jnp.einsum('bkgqc,bckd->bqkgd', p.astype(v_ctx.dtype), v_ctx)
    return o.reshape(b, n, h * dh)

def global_gqa(q, k, v, k_ctx, v_ctx):
    b, s, h, dh = q.shape
    kv = k.shape[2]
    g = h // kv
    nb = s // Q_BLOCK
    k_all = jnp.concatenate([k_ctx, k], axis=1)
    v_all = jnp.concatenate([v_ctx, v], axis=1)
    scale = dh ** -0.5
    qb = q.reshape(b, nb, Q_BLOCK, kv, g, dh).swapaxes(0, 1)

    def one_block(q_blk):
        sc = jnp.einsum('bqkgd,bnkd->bkgqn', q_blk, k_all).astype(jnp.float32) * scale
        p = jax.nn.softmax(sc, axis=-1).astype(v_all.dtype)
        return jnp.einsum('bkgqn,bnkd->bqkgd', p, v_all)

    o = lax.map(one_block, qb)
    return o.swapaxes(0, 1).reshape(b, s, h * dh)

def windowed_gqa(q, k, v, k_ctx, v_ctx, sink_logit):
    b, s, h, dh = q.shape
    kv = k.shape[2]
    g = h // kv
    nb = s // Q_BLOCK
    side = WINDOW // Q_BLOCK
    span = (2 * side + 1) * Q_BLOCK
    n_ctx = k_ctx.shape[1]
    pad = ((0, 0), (side * Q_BLOCK, side * Q_BLOCK), (0, 0), (0, 0))
    kp = jnp.pad(k, pad).reshape(b, nb + 2 * side, Q_BLOCK, kv, dh)
    vp = jnp.pad(v, pad).reshape(b, nb + 2 * side, Q_BLOCK, kv, dh)
    kb = jnp.concatenate([kp[:, j:j + nb] for j in range(2 * side + 1)], axis=2)
    vb = jnp.concatenate([vp[:, j:j + nb] for j in range(2 * side + 1)], axis=2)
    qb = q.reshape(b, nb, Q_BLOCK, kv, g, dh)
    a = jnp.arange(Q_BLOCK)[:, None]
    j = jnp.arange(span)[None, :]
    band = jnp.abs(j - side * Q_BLOCK - a) <= WINDOW
    kpos = jnp.arange(nb)[:, None] * Q_BLOCK - side * Q_BLOCK + jnp.arange(span)[None, :]
    valid = band[None] & ((kpos >= 0) & (kpos < s))[:, None, :]
    sink = sink_logit.astype(jnp.float32).reshape(kv, g, 1, 1)
    scale = dh ** -0.5

    def one_block(args):
        q_blk, k_blk, v_blk, m = args
        s_loc = jnp.einsum('bqkgd,bjkd->bkgqj', q_blk, k_blk).astype(jnp.float32) * scale
        s_loc = jnp.where(m, s_loc, NEG_INF)
        s_ctx = jnp.einsum('bqkgd,bckd->bkgqc', q_blk, k_ctx).astype(jnp.float32) * scale
        s_sink = jnp.broadcast_to(sink, s_loc.shape[:-1] + (1,))
        p = jax.nn.softmax(jnp.concatenate([s_loc, s_ctx, s_sink], axis=-1), axis=-1)
        p_loc = p[..., :span].astype(v.dtype)
        p_ctx = p[..., span:span + n_ctx].astype(v.dtype)
        return (jnp.einsum('bkgqj,bjkd->bqkgd', p_loc, v_blk)
                + jnp.einsum('bkgqc,bckd->bqkgd', p_ctx, v_ctx))

    xs = (qb.swapaxes(0, 1), kb.swapaxes(0, 1), vb.swapaxes(0, 1), valid)
    o = lax.map(one_block, xs)
    return o.swapaxes(0, 1).reshape(b, s, h * dh)

def neighbourhood_attention(q, k, v, k_ctx, v_ctx, rpb):
    b, s, h, dh = q.shape
    rows = s // GRID_W
    kr = min(NA_ROWS, rows)
    kw = min(NA_COLS, GRID_W)
    nk = kr * kw
    t = jnp.arange(s, dtype=jnp.int32)
    r = t // GRID_W
    col = t % GRID_W
    r0 = jnp.clip(r - kr // 2, 0, rows - kr)
    c0 = jnp.clip(col - kw // 2, 0, GRID_W - kw)
    key_r = r0[:, None, None] + jnp.arange(kr, dtype=jnp.int32)[None, :, None]
    key_c = c0[:, None, None] + jnp.arange(kw, dtype=jnp.int32)[None, None, :]
    key_idx = (key_r * GRID_W + key_c).reshape(s, nk)
    rel_idx = ((key_r - r[:, None, None] + NA_ROWS - 1) * (2 * NA_COLS - 1)
               + (key_c - col[:, None, None] + NA_COLS - 1)).reshape(s, nk)
    nb = s // Q_BLOCK
    rpb_flat = rpb.reshape(h, -1).astype(jnp.float32)
    scale = dh ** -0.5
    n_ctx = k_ctx.shape[1]

    def one_block(args):
        q_blk, idx, ridx = args
        kg = jnp.take(k, idx.reshape(-1), axis=1).reshape(b, Q_BLOCK, nk, h, dh)
        vg = jnp.take(v, idx.reshape(-1), axis=1).reshape(b, Q_BLOCK, nk, h, dh)
        s_loc = (jnp.einsum('bqhd,bqnhd->bhqn', q_blk, kg).astype(jnp.float32) * scale
                 + jnp.take(rpb_flat, ridx, axis=1)[None])
        s_ctx = jnp.einsum('bqhd,bchd->bhqc', q_blk, k_ctx).astype(jnp.float32) * scale
        p = jax.nn.softmax(jnp.concatenate([s_loc, s_ctx], axis=-1), axis=-1)
        p_loc = p[..., :nk].astype(v.dtype)
        p_ctx = p[..., nk:nk + n_ctx].astype(v.dtype)
        return (jnp.einsum('bhqn,bqnhd->bqhd', p_loc, vg)
                + jnp.einsum('bhqc,bchd->bqhd', p_ctx, v_ctx))

    xs = (q.reshape(b, nb, Q_BLOCK, h, dh).swapaxes(0, 1),
          key_idx.reshape(nb, Q_BLOCK, nk), rel_idx.reshape(nb, Q_BLOCK, nk))
    o = lax.map(one_block, xs)
    return o.swapaxes(0, 1).reshape(b, s, h * dh)

def hyena_positional_features(n):
    t = jnp.linspace(0.0, 1.0, n, dtype=jnp.float32)[:, None]
    bands = (HYENA_EMB - 1) // 2
    w = 2.0 * math.pi * jnp.arange(n, dtype=jnp.float32)[:, None] / n
    f = jnp.linspace(1e-4, bands - 1, bands, dtype=jnp.float32)[None, :]
    return jnp.concatenate([t, jnp.cos(f * w), -jnp.sin(f * w)], axis=-1)

def hyena_filters(n, w1, b1, w2, b2, freq, w3):
    f32 = jnp.float32
    z = hyena_positional_features(n)
    fr = freq.astype(f32)
    hdn = jnp.sin(fr * (z @ w1.astype(f32) + b1.astype(f32)))
    hdn = jnp.sin(fr * (hdn @ w2.astype(f32) + b2.astype(f32)))
    filt = hdn @ w3.astype(f32)
    t = jnp.linspace(0.0, 1.0, n, dtype=f32)[:, None]
    deltas = jnp.linspace(math.log(HYENA_DECAY_TARGET) / HYENA_LONG_DECAY_PCT,
                          math.log(HYENA_DECAY_TARGET) / HYENA_SHORT_DECAY_PCT, HYENA_WIDTH, dtype=f32)
    decay = jnp.exp(-t * jnp.abs(deltas))
    return filt.reshape(n, HYENA_ORDER, 2, HYENA_WIDTH) * decay[:, None, None, :]

def bidir_long_conv(z, h_fwd, h_bwd, d_skip):
    n = z.shape[1]
    taps = jnp.concatenate([h_fwd, jnp.zeros_like(h_fwd[:1]), h_bwd[:0:-1]], axis=0)
    taps = taps * lax.rsqrt(jnp.sum(taps * taps, axis=0, keepdims=True) + EPS)
    zf = jnp.fft.rfft(z.astype(jnp.float32), n=2 * n, axis=1)
    tf = jnp.fft.rfft(taps, n=2 * n, axis=0)
    y = jnp.fft.irfft(zf * tf[None], n=2 * n, axis=1)[:, :n]
    return (y + z.astype(jnp.float32) * d_skip.astype(jnp.float32)).astype(z.dtype)

def centred_depthwise_conv(u, w, bias):
    pad = w.shape[0] // 2
    y = lax.conv_general_dilated(u, w[:, None, :].astype(u.dtype), window_strides=(1,),
                                 padding=[(pad, pad)], dimension_numbers=('NWC', 'WIO', 'NWC'),
                                 feature_group_count=u.shape[-1])
    return y + bias

def hyena_branch(u, conv_w, conv_b, w1, b1, w2, b2, freq, w3, d_skip):
    n = u.shape[1]
    filt = hyena_filters(n, w1, b1, w2, b2, freq, w3)
    uc = centred_depthwise_conv(u, conv_w, conv_b)
    parts = jnp.split(uc, HYENA_ORDER + 1, axis=-1)
    z = parts[0]
    for o in range(HYENA_ORDER):
        z = parts[o + 1] * bidir_long_conv(z, filt[:, o, 0], filt[:, o, 1], d_skip[o])
    return z

def even_mixer(p, p_ctx, q_norm, k_norm, conv_w, conv_b, w1, b1, w2, b2, freq, w3, d_skip, cos, sin, need_ctx):
    aq, ak, av, hu, ag, hg = split_cols(p, EVEN_SPLITS)
    caq, cak, cav, chu, cag, chg = split_cols(p_ctx, EVEN_SPLITS)
    q = apply_rope(rms_norm(heads(aq, N_Q_HEADS), q_norm), cos, sin)
    k = apply_rope(rms_norm(heads(ak, N_KV_HEADS), k_norm), cos, sin)
    v = heads(av, N_KV_HEADS)
    k_c = rms_norm(heads(cak, N_KV_HEADS), k_norm)
    v_c = heads(cav, N_KV_HEADS)
    y_a = global_gqa(q, k, v, k_c, v_c)
    y_b = hyena_branch(hu, conv_w, conv_b, w1, b1, w2, b2, freq, w3, d_skip)
    y = jnp.concatenate([y_a * jax.nn.silu(ag), y_b * jax.nn.silu(hg)], axis=-1)
    if not need_ctx:
        return y, None
    q_c = rms_norm(heads(caq, N_Q_HEADS), q_norm)
    y_ca = context_attention(q_c, k_c, v_c)
    y_cb = hyena_branch(chu, conv_w, conv_b, w1, b1, w2, b2, freq, w3, d_skip)
    y_c = jnp.concatenate([y_ca * jax.nn.silu(cag), y_cb * jax.nn.silu(chg)], axis=-1)
    return y, y_c

def odd_mixer(p, p_ctx, wq_norm, wk_norm, sink, nq_norm, nk_norm, rpb, cos, sin, need_ctx):
    wq, wk, wv, nq, nk_, nv, wg, ng = split_cols(p, ODD_SPLITS)
    cwq, cwk, cwv, cnq, cnk, cnv, cwg, cng = split_cols(p_ctx, ODD_SPLITS)
    q_w = apply_rope(rms_norm(heads(wq, N_Q_HEADS), wq_norm), cos, sin)
    k_w = apply_rope(rms_norm(heads(wk, N_KV_HEADS), wk_norm), cos, sin)
    v_w = heads(wv, N_KV_HEADS)
    kc_w = rms_norm(heads(cwk, N_KV_HEADS), wk_norm)
    vc_w = heads(cwv, N_KV_HEADS)
    y_w = windowed_gqa(q_w, k_w, v_w, kc_w, vc_w, sink)
    q_n = rms_norm(heads(nq, N_Q_HEADS), nq_norm)
    k_n = rms_norm(heads(nk_, N_Q_HEADS), nk_norm)
    v_n = heads(nv, N_Q_HEADS)
    kc_n = rms_norm(heads(cnk, N_Q_HEADS), nk_norm)
    vc_n = heads(cnv, N_Q_HEADS)
    y_n = neighbourhood_attention(q_n, k_n, v_n, kc_n, vc_n, rpb)
    y = jnp.concatenate([y_w * jax.nn.silu(wg), y_n * jax.nn.silu(ng)], axis=-1)
    if not need_ctx:
        return y, None
    y_cw = context_attention(rms_norm(heads(cwq, N_Q_HEADS), wq_norm), kc_w, vc_w, sink)
    y_cn = context_attention(rms_norm(heads(cnq, N_Q_HEADS), nq_norm), kc_n, vc_n)
    y_c = jnp.concatenate([y_cw * jax.nn.silu(cwg), y_cn * jax.nn.silu(cng)], axis=-1)
    return y, y_c

def second_inputs(seed: int = 0) -> dict:
    key = jax.random.key(seed)
    keys = iter(jax.random.split(key, 32))

    def nrm(shape, std):
        return std * jax.random.normal(next(keys), shape, jnp.float32)

    n_filter_out = HYENA_ORDER * 2 * HYENA_WIDTH
    n_hy_in = (HYENA_ORDER + 1) * HYENA_WIDTH
    return {
        'x': nrm((BATCH, SEQ, D_MODEL), 1.0),
        'c': nrm((BATCH, D_MODEL), 1.0),
        'ctx': nrm((BATCH, CTX_LEN, D_MODEL), 1.0),
        'c_ctx': nrm((D_MODEL,), 1.0),
        'norm_g': 1.0 + nrm((DEPTH, D_MODEL), 0.1),
        'w_ada': nrm((DEPTH, D_MODEL, 3 * D_MODEL), D_MODEL ** -0.5),
        'b_ada': nrm((DEPTH, 3 * D_MODEL), 0.01),
        'w_in': nrm((DEPTH, D_MODEL, IN_WIDTH), D_MODEL ** -0.5),
        'w_out': nrm((DEPTH, MIX_WIDTH_2, D_MODEL), MIX_WIDTH_2 ** -0.5),
        'glob_q_norm': 1.0 + nrm((N_EVEN, HEAD_DIM), 0.1),
        'glob_k_norm': 1.0 + nrm((N_EVEN, HEAD_DIM), 0.1),
        'hy_conv_w': nrm((N_EVEN, HYENA_SHORT_CONV, n_hy_in), HYENA_SHORT_CONV ** -0.5),
        'hy_conv_b': nrm((N_EVEN, n_hy_in), 0.01),
        'hy_w1': nrm((N_EVEN, HYENA_EMB, HYENA_HIDDEN), HYENA_EMB ** -0.5),
        'hy_b1': nrm((N_EVEN, HYENA_HIDDEN), 0.01),
        'hy_w2': nrm((N_EVEN, HYENA_HIDDEN, HYENA_HIDDEN), HYENA_HIDDEN ** -0.5),
        'hy_b2': nrm((N_EVEN, HYENA_HIDDEN), 0.01),
        'hy_freq': 1.0 + nrm((N_EVEN, HYENA_HIDDEN), 0.1),
        'hy_w3': nrm((N_EVEN, HYENA_HIDDEN, n_filter_out), HYENA_HIDDEN ** -0.5),
        'hy_skip': nrm((N_EVEN, HYENA_ORDER, HYENA_WIDTH), 0.5),
        'win_q_norm': 1.0 + nrm((N_ODD, HEAD_DIM), 0.1),
        'win_k_norm': 1.0 + nrm((N_ODD, HEAD_DIM), 0.1),
        'win_sink': nrm((N_ODD, N_Q_HEADS), 0.5),
        'nat_q_norm': 1.0 + nrm((N_ODD, HEAD_DIM), 0.1),
        'nat_k_norm': 1.0 + nrm((N_ODD, HEAD_DIM), 0.1),
        'nat_rpb': nrm((N_ODD, N_Q_HEADS, 2 * NA_ROWS - 1, 2 * NA_COLS - 1), 0.1),
    }

def second_block(x, c, ctx, c_ctx, norm_g, w_ada, b_ada, w_in, w_out,
              glob_q_norm, glob_k_norm, hy_conv_w, hy_conv_b, hy_w1, hy_b1, hy_w2, hy_b2,
              hy_freq, hy_w3, hy_skip, win_q_norm, win_k_norm, win_sink,
              nat_q_norm, nat_k_norm, nat_rpb):
    cos, sin = axial_rope_tables(x.shape[1])
    x_ctx = ctx
    for layer in range(DEPTH):
        need_ctx = layer < DEPTH - 1
        shift, scale, gate = adaln(c, w_ada[layer], b_ada[layer])
        c_shift, c_scale, c_gate = adaln(c_ctx, w_ada[layer], b_ada[layer])
        h = modulated_norm(x, norm_g[layer], shift[:, None], scale[:, None])
        h_ctx = modulated_norm(x_ctx, norm_g[layer], c_shift, c_scale)
        p = jnp.matmul(h, w_in[layer])
        p_ctx = jnp.matmul(h_ctx, w_in[layer])
        i = layer // 2
        if layer % 2 == 0:
            y, y_ctx = even_mixer(p, p_ctx, glob_q_norm[i], glob_k_norm[i], hy_conv_w[i], hy_conv_b[i],
                                  hy_w1[i], hy_b1[i], hy_w2[i], hy_b2[i], hy_freq[i], hy_w3[i], hy_skip[i],
                                  cos, sin, need_ctx)
        else:
            y, y_ctx = odd_mixer(p, p_ctx, win_q_norm[i], win_k_norm[i], win_sink[i],
                                 nat_q_norm[i], nat_k_norm[i], nat_rpb[i], cos, sin, need_ctx)
        x = x + gate[:, None] * jnp.matmul(y, w_out[layer])
        if need_ctx:
            x_ctx = x_ctx + c_gate * jnp.matmul(y_ctx, w_out[layer])
    return x


def setup_inputs(seed=0):
    out = dict(first_inputs(seed))
    for name, value in second_inputs(seed + 1).items():
        if name != "x":
            out[name + "_2"] = value
    return out


def reference(
    x, norm_mix, w_in, w_out_a, w_out_b, w_out_c, w_o, norm_mlp, w_up, w_down, norm_final, c_2,
    ctx_2, c_ctx_2, norm_g_2, w_ada_2, b_ada_2, w_in_2, w_out_2, glob_q_norm_2, glob_k_norm_2,
    hy_conv_w_2, hy_conv_b_2, hy_w1_2, hy_b1_2, hy_w2_2, hy_b2_2, hy_freq_2, hy_w3_2, hy_skip_2,
    win_q_norm_2, win_k_norm_2, win_sink_2, nat_q_norm_2, nat_k_norm_2, nat_rpb_2,
):
    x = first_block(
        x, norm_mix, w_in, w_out_a, w_out_b, w_out_c, w_o, norm_mlp, w_up, w_down, norm_final,
    )
    return second_block(
        x, c_2, ctx_2, c_ctx_2, norm_g_2, w_ada_2, b_ada_2, w_in_2, w_out_2, glob_q_norm_2,
        glob_k_norm_2, hy_conv_w_2, hy_conv_b_2, hy_w1_2, hy_b1_2, hy_w2_2, hy_b2_2, hy_freq_2,
        hy_w3_2, hy_skip_2, win_q_norm_2, win_k_norm_2, win_sink_2, nat_q_norm_2, nat_k_norm_2,
        nat_rpb_2,
    )


_drawn_inputs = setup_inputs


def setup_inputs(seed=0):
    import zlib

    import numpy as np

    out = dict(_drawn_inputs(seed))
    spreads = {}
    factors = {'glob_q_norm_2': 8.0,
     'glob_k_norm_2': 8.0,
     'hy_conv_b_2': 2.932,
     'win_q_norm_2': 8.0,
     'win_k_norm_2': 8.0,
     'win_sink_2': 8.0,
     'nat_q_norm_2': 8.0,
     'nat_k_norm_2': 8.0,
     'nat_rpb_2': 36.111}
    for name, (base, spread) in spreads.items():
        noise = np.random.default_rng([zlib.crc32(name.encode()), seed]).standard_normal(out[name].shape)
        drawn = base * np.exp(spread * noise) if base else spread * noise
        out[name] = jnp.asarray(drawn.astype(out[name].dtype))
    for name, factor in factors.items():
        out[name] = (out[name] * factor).astype(out[name].dtype)
    return out
```

```python
import math
from contextlib import ExitStack

import numpy as np

import concourse.bass as bass
from concourse import mybir

F32 = mybir.dt.float32
ACT = mybir.ActivationFunctionType
ALU = mybir.AluOpType
AX_X = mybir.AxisListType.X

P = 128
SEQ = 256
D = 1024
KD = D // P
TILES = SEQ // P
DH = 64
SCALE = DH ** -0.5
EPS = 1e-6
NEG = -1e30
LAYERS = 2
HEADS = 24
MIX = HEADS * DH
ROT = 18
ROPE = 16
N_A, N_B, N_C = 4, 6, 6
GROUPS_A = ((128, 1), (512, 4), (2048, 16))
G_A = len(GROUPS_A)
FF = 4096
CTX = 256
T4 = (SEQ + CTX) // P
N4 = T4 * P
QH = 8
KVH = 2
GW = QH * DH
IN2 = [(0, 512), (512, 768), (768, 1280), (1280, 1792), (1792, 2304), (2304, 2816), (2816, 3328)]
HY = 512
HY_CH = 3 * HY // P
HID, EMB = 64, 33
NA_ROWS, NA_COLS, GRID_W = 8, 16, 64
ROWS = SEQ // GRID_W
REL_R, REL_C = 2 * NA_ROWS - 1, 2 * NA_COLS - 1
TWO_PI = 2.0 * math.pi
TWO_PI_HI = float(np.float32(6.28125))
TWO_PI_LO = float(np.float32(TWO_PI - 6.28125))
ROUND = 1.5 * 2.0 ** 23
PI_IN = float(np.nextafter(np.float32(math.pi), np.float32(0)))

SLAB = 4096
SLOTS = 4
BANKS = 8
CONSTS = 9 + 6 + 2 + 6 + 4 + 3
LATE0, FILTERS, BIASES = 2, 6, ROWS + 2


def constants():
    f = np.float32
    i = np.arange(P)
    c = {"ident": np.eye(P, dtype=f)}
    c["tri"] = (i[:, None] >= i[None, :]).astype(f)
    off = i[:, None] + P - i[None, :]
    on = i[:, None] - i[None, :]
    mask_a = np.zeros((P, G_A, 2, P), f)
    for g, (w, d) in enumerate(GROUPS_A):
        for b, dist in enumerate((off, on)):
            ok = (dist >= 0) & (dist <= w) & (dist % d == 0)
            mask_a[:, g, b] = np.where(ok, 0, NEG)
    c["mask_a"] = mask_a.reshape(P, -1)
    causal = np.where(on >= 0, 0, NEG)
    c["mask_b"] = np.concatenate([np.zeros((P, P)), causal], 1).astype(f)
    strict = np.where(i[None, :] > i[:, None], 0, NEG)
    c["mask_c"] = np.concatenate([strict, np.zeros((P, P)), strict], 1).astype(f)
    pos = np.arange(SEQ, dtype=f)
    inv = np.exp(f(-math.log(500000.0)) * np.arange(0, ROPE, 2, dtype=f) / f(ROPE)).astype(f)
    ang = (pos[:, None] * inv).astype(f).astype(np.float64)
    table = np.concatenate([np.cos(ang), np.sin(ang)], 1).astype(f)
    c["rope_a"] = np.concatenate([table[:P], table[P:]], 1)
    row, col = (np.arange(SEQ) // GRID_W).astype(f), (np.arange(SEQ) % GRID_W).astype(f)
    inv = (f(10000.0) ** (-np.arange(16, dtype=f) / f(16))).astype(f)
    ang = np.concatenate([row[:, None] * inv, col[:, None] * inv], 1).astype(f).astype(np.float64)
    table = np.concatenate([np.cos(ang), np.sin(ang)], 1).astype(f)
    c["rope_b"] = np.concatenate([table[:P], table[P:]], 1)
    sel = np.zeros((2, 2, P), f)
    sel[0, 0] = sel[1, 1] = 1
    c["select"] = sel.reshape(2, -1)
    near0 = np.where(i[None, :] <= i[:, None], 0, NEG)
    near1 = np.where(i[:, None] <= i[None, :], 0, NEG)
    z = np.zeros((P, P))
    c["mask_w"] = np.concatenate([z, near0, near1, z], 1).astype(f)
    gc = i % GRID_W
    c0 = np.clip(gc - NA_COLS // 2, 0, GRID_W - NA_COLS)
    k = np.arange(GRID_W)
    c["mask_n"] = np.where((k >= c0[:, None]) & (k < c0[:, None] + NA_COLS), 0, NEG).astype(f)
    t = np.arange(SEQ)
    theta = TWO_PI * ((t[:, None] * t[None, :]) % (2 * SEQ)) / (2 * SEQ)
    alt = np.where(t % 2, -1.0, 1.0)
    fc, fs = np.cos(theta), -np.sin(theta)
    fs[:, 0] = alt
    gcos, gsin = 2 * np.cos(theta) / (2 * SEQ), -2 * np.sin(theta) / (2 * SEQ)
    gcos[0] /= 2
    gsin[0] = alt / (2 * SEQ)
    c["fourier"] = np.concatenate([m[h * P:(h + 1) * P] for m in (fc, fs, gcos, gsin) for h in (0, 1)], 1).astype(f)
    tt = np.linspace(0.0, 1.0, SEQ, dtype=f)[:, None]
    bands = (EMB - 1) // 2
    w = (f(TWO_PI) * np.arange(SEQ, dtype=f)[:, None] / f(SEQ)).astype(f)
    fr = np.linspace(1e-4, bands - 1, bands, dtype=f)[None]
    a = (fr * w).astype(f).astype(np.float64)
    c["positions"] = np.ascontiguousarray(np.concatenate([tt, np.cos(a), -np.sin(a)], 1).astype(f).T)
    deltas = np.linspace(math.log(1e-2) / 1.5, math.log(1e-2) / 0.3, HY, dtype=f)
    decay = np.exp((-tt * np.abs(deltas)).astype(f)).astype(f)
    c["decay"] = np.concatenate([decay[:P], decay[P:]], 1)
    return {n: np.ascontiguousarray(a.astype(f)) for n, a in c.items()}


def units_of_block1():
    soft = [("A", s, t) for s in range(N_A) for t in range(TILES)]
    soft += [("B", b, t) for b in range(N_B) for t in range(TILES)]
    return soft + [("C", c, 0) for c in range(N_C)]


def units_of_block2(layer):
    if layer == 0:
        return [("G", h, t) for h in range(QH) for t in range(T4)]
    return [(k, h, t) for k in ("W", "N") for h in range(QH) for t in range(TILES)]


def slab_list():
    out = []
    for l in range(LAYERS):
        out += [("in", l, c) for c in range(15)]
        out += [("out", l, c) for c in range(2)] + [("o", l, c) for c in range(2)]
        out += [("up", l, c) for c in range(8)] + [("down", l, c) for c in range(8)]
    for l in range(LAYERS):
        out += [("ada", l, c) for c in range(6)] + [("in2", l, c) for c in range(7)]
        out += [("out2", l, c) for c in range(2)]
    return out


class Signal:

    def __init__(self, sem, keys):
        self.sem = sem
        self.value = {k: n + 1 for n, k in enumerate(keys)}
        self.count = 0

    def at(self, *key):
        return self.sem, self.value[key]

    def by(self, *key):
        self.count += 1
        assert self.value[key] == self.count, (self.sem, key)
        return self.sem, self.count


class Steps:

    def __init__(self, eng, sem):
        self.eng, self.sem, self.n, self.last = eng, sem, 0, None

    def __call__(self, instruction, signal=None):
        if signal is None:
            self.n += 1
            signal = (self.sem, self.n)
        instruction.then_inc(signal[0], 1)
        self.last = signal

    def settle(self):
        self.eng.wait_ge(*self.last)


def two_blocks(nc, A, C, out):
    ctx = ExitStack()
    with ctx:
        def sb(name, shape):
            return ctx.enter_context(nc.sbuf_tensor(name, shape, F32))

        def sem(name):
            return ctx.enter_context(nc.semaphore(name))

        slabs = sb("slabs", [P, SLOTS, SLAB])
        X = sb("X", [P, T4, D])
        ident = sb("ident", [P, P])
        ones = sb("ones", [P, P])
        rope_a = sb("rope_a", [P, TILES, ROPE])
        g_cols = sb("g_cols", [P, 3, LAYERS, KD])
        stat = sb("stat", [P, 2, 4, 8])
        nstat = sb("nstat", [P, 4, 64])
        small = sb("small", [P, 64])
        rope_b = sb("rope_b", [P, TILES, DH])
        select = sb("select", [2, 2, P])
        eps_col = sb("eps_col", [P, 2])
        ada_t = sb("ada_t", [P, 16, 2])
        gain = sb("gain", [P, KD, 2])
        cond = sb("cond", [P, KD, 2])
        cond_e = sb("cond_e", [P, KD, 2])
        sink = sb("sink", [P, QH])
        head_gain = sb("head_gain", [P, 6, DH])
        conv_w = sb("conv_w", [P, 4, HY_CH])
        hid = sb("hid", [HID, 8])
        arena_cols = 31000
        arena = sb("arena", [P, arena_cols])
        rel_rows = nc.dram_tensor("rel_rows", (GRID_W, QH * REL_R, GRID_W), F32, kind="Internal").ap()

        def carve(at, *shape):
            n = int(np.prod(shape))
            assert at[0] + n <= arena_cols, (at[0] + n)
            v = arena[:, at[0]:at[0] + n]
            at[0] += n
            if len(shape) == 2:
                v = v.rearrange("p (a b) -> p a b", a=shape[0])
            elif len(shape) == 3:
                v = v.rearrange("p (a b c) -> p a b c", a=shape[0], b=shape[1])
            elif len(shape) == 4:
                v = v.rearrange("p (a b c d) -> p a b c d", a=shape[0], b=shape[1], c=shape[2])
            return v

        at = [0]
        S = carve(at, 2, 768)
        PT = carve(at, 2, 768)
        work = arena[:, 0:2048]
        base = at[0]
        hT = carve(at, KD, SEQ)
        oT = carve(at, KD, SEQ)
        qkv_at = at[0]
        qkv = carve(at, 3, TILES, MIX)
        qT_at = at[0]
        qkT = carve(at, 2, MIX // P, SEQ)
        gates = carve(at, TILES, 3, D)
        mask_a = carve(at, G_A, SEQ)
        mask_b = carve(at, SEQ)
        mask_c = carve(at, 3, P)
        tri = carve(at, P)
        uT = carve([qkv_at], FF // P, SEQ)
        merged = carve([qkv_at], TILES, D)
        gated = carve([qkv_at + 2 * D], 2, 512)
        rope_tmp = carve([qT_at + 4 * D], 4, TILES, ROT, ROPE // 2)
        xn1 = carve([qT_at], TILES, D)
        final_g = carve([base + 2 * D], D)
        rel_at = [qT_at + 2 * SEQ * (MIX // P)]
        rel_pad = carve(rel_at, 2 * GRID_W)
        rel_toep = carve(rel_at, GRID_W, GRID_W)
        at = [base]
        hT2 = carve(at, KD, N4)
        gate_b = carve(at, 2, D)
        q_at = at[0]
        q2 = carve(at, T4, GW)
        kv2 = carve(at, T4, 2 * KVH * DH)
        k2d = carve(at, T4, KVH, 2 * DH)
        qT2 = carve(at, QH // 2, N4)
        kT2 = carve(at, KVH, N4)
        oT2 = carve(at, QH // 2, N4)
        uc_at = at[0]
        uc = carve(at, HY_CH, N4)
        ag_at = at[0]
        ag = carve(at, 4, N4)
        hg = carve(at, 4, N4)
        fourier = carve(at, 4, 2, SEQ)
        xn2 = carve([uc_at], T4, D)
        ada_bias = carve([uc_at + 4 * D], 3 * D)
        ada_row = carve([uc_at + 7 * D], 3 * D)
        at = [q_at]
        spec_a = carve(at, 2, 2, HY)
        spec_b = carve(at, 2, 2, HY)
        yTh = carve(at, 4, N4)
        decay = carve(at, 2, HY)
        assert at[0] <= q_at + 7 * D
        hid_at = [q_at + 4 * D]
        positions = carve(hid_at, SEQ)[0:EMB, :]
        hyena_w1 = carve(hid_at, HID)[0:EMB, :]
        hyena_w2 = carve(hid_at, HID)[0:HID, :]
        hidden = carve(hid_at, 2, SEQ)
        w3 = carve([ag_at], 2, 2, HY)
        skip_b = carve([ag_at + 2048], 2, HY)
        spec_c = carve([ag_at + 3072], 2, HY)
        taps = carve([base], 2, 2, HY)
        taps_sd = carve([base + 2048], 2, 2, HY)
        Z = carve([base], T4, HY)
        G1 = carve([base + 2048], T4, HY)
        Y = carve([0], 4, HY)
        rn = carve([2048], 2, HY)
        spec_tmp = carve([2048], 2, HY)
        Y1 = carve([ag_at], 4, HY)

        def spectrum(s):
            return (Y, Y1)[s]

        at = [base + 4096 + 2048]
        wq_at = at[0]
        wq = carve(at, TILES, GW)
        nq = carve(at, TILES, GW)
        kv3 = carve(at, T4, 2 * KVH * DH)
        k3d = carve(at, T4, KVH, 2 * DH)
        nk = carve(at, T4, GW)
        nv = carve(at, T4, GW)
        wqT = carve(at, QH // 2, SEQ)
        nqT = carve(at, QH // 2, SEQ)
        wkT = carve(at, KVH, N4)
        nkT = carve(at, QH // 2, N4)
        wgT = carve(at, 4, SEQ)
        ngT = carve(at, 4, SEQ)
        bias_at = at[0]
        rel_bias = carve(at, TILES, QH, SEQ)
        mask_w = carve(at, TILES, SEQ)
        mask_n = carve(at, GRID_W)
        oT3 = carve([wq_at], 4, SEQ)
        yT3 = carve([wq_at + 1024], 4, SEQ)
        xn3 = carve([bias_at], T4, D)
        nk_at = wq_at + 4096
        ada_row3 = carve([nk_at], 3 * D)
        ada_bias3 = carve([uc_at], 3 * D)

        banks = [ctx.enter_context(nc.psum_tensor(f"bank{b}", [P, 512], F32)) for b in range(BANKS)]

        bank_filled = [sem(f"bank_filled{b}") for b in range(BANKS)]
        bank_emptied = [sem(f"bank_emptied{b}") for b in range(BANKS)]
        slab_loaded = [sem(f"slab_loaded{s}") for s in range(SLOTS)]
        x_loaded = sem("x_loaded")
        consts_loaded = sem("consts_loaded")
        late_loaded = sem("late_loaded")
        final_g_loaded = sem("final_g_loaded")
        filter_loaded = sem("filter_loaded")
        bias_loaded = sem("bias_loaded")
        ada_bias_loaded = sem("ada_bias_loaded")
        rel_loaded = sem("rel_loaded")
        rel_stored = sem("rel_stored")
        out_stored = sem("out_stored")
        vector_step = sem("vector_step")
        scalar_step = sem("scalar_step")
        NORMS = range(7)
        b1u = [(l, u) for l in range(LAYERS) for u in range(len(units_of_block1()))]
        b2u = [(2 + l, u) for l in range(LAYERS) for u in range(len(units_of_block2(l)))]
        kinds = {(l, u): units_of_block1()[u][0] for l, u in b1u}
        kinds |= {(l, u): units_of_block2(l - 2)[u][0] for l, u in b2u}
        softs = [k for k in b1u + b2u if kinds[k] != "C"]
        sticks = [k for k in b1u if kinds[k] == "C"]
        ones_set = sem("ones_set")
        x_added = Signal(sem("x_added"), [(n,) for n in range(8)])
        rstd_ready = Signal(sem("rstd_ready"), [(n,) for n in NORMS])
        xn_by_vector = Signal(sem("xn_by_vector"), [(n,) for n in NORMS if n != 4])
        qk_roped = Signal(sem("qk_roped"), [(l, j) for l in range(LAYERS) for j in range(2)])
        bias_ready = Signal(sem("bias_ready"), softs)
        probs_scaled = Signal(sem("probs_scaled"), softs)
        stick_masked = Signal(sem("stick_masked"), sticks)
        stick_summed = Signal(sem("stick_summed"), sticks)
        merged_ready = Signal(sem("merged_ready"), [(l,) for l in range(LAYERS)])
        heads_squared = Signal(sem("heads_squared"), [(l, j) for l, n in ((0, 2), (1, 4)) for j in range(n)])
        heads_ready = Signal(sem("heads_ready"), [(l, j) for l, n in ((0, 2), (1, 4)) for j in range(n)])
        cond_ready = sem("cond_ready")
        cond_ready_s = Signal(cond_ready, [("sum",), ("done",)])
        ada_ready = Signal(sem("ada_ready"), [(l,) for l in range(LAYERS)])
        gated_ready = Signal(sem("gated_ready"), [(0,), (1,)])
        sin_in_range = Signal(sem("sin_in_range"), [(0,), (1,)])
        taps_squared = Signal(sem("taps_squared"), [(0,), (1,)])
        taps_mixed = Signal(sem("taps_mixed"), [(0,), (1,)])
        stick_argument = Signal(sem("stick_argument"), sticks)
        spectra_ready = Signal(sem("spectra_ready"), [(0,), (1,)])
        silu_used = Signal(sem("silu_used"), [(0,)])
        pool_step = sem("pool_step")
        bias_masked = sem("bias_masked")
        spectrum_ready = Signal(sem("spectrum_ready"), [(o, s) for o in range(2) for s in range(2)])
        rsqrt_guess = Signal(sem("rsqrt_guess"), [(n,) for n in NORMS])
        xn_by_scalar = Signal(sem("xn_by_scalar"), [(n,) for n in NORMS if n != 4])
        probs_ready = Signal(sem("probs_ready"), softs)
        softplus_part = Signal(sem("softplus_part"), sticks)
        stick_weights = Signal(sem("stick_weights"), sticks)
        heads_guess = Signal(sem("heads_guess"), [(l, j) for l, n in ((0, 2), (1, 4)) for j in range(n)])
        cond_exp = Signal(sem("cond_exp"), [(0,)])
        sin_ready = Signal(sem("sin_ready"), [(0,), (1,)])
        taps_guess = Signal(sem("taps_guess"), [(0,), (1,)])
        conv_begun = Signal(sem("conv_begun"), [(c,) for c in range(HY_CH)])
        silu_exp = Signal(sem("silu_exp"), [(l, c) for l in range(LAYERS) for c in range(8)])
        hT_by_scalar = Signal(sem("hT_by_scalar"), [(n, k) for n in (5, 6) for k in range(KD)])
        down_used = Signal(sem("down_used"), [(l, s) for l in range(LAYERS) for s in range(7)])

        number = {}
        SLABS = slab_list()
        slab_at = {k: n for n, k in enumerate(SLABS)}
        slab_dmas = [3 if k[0] == "out" else 1 for k in SLABS]
        last_use = {}
        ended_in = {}

        def bank(*key):
            return banks[number[key] % BANKS]

        def filled(*key):
            n = number[key]
            return bank_filled[n % BANKS], n // BANKS + 1

        def emptied(*key):
            n = number[key]
            return bank_emptied[n % BANKS], n // BANKS + 1

        block = ctx.enter_context(nc.Block())

        @block.tensor
        def _(pe):
            mm, tr = nc.tensor.matmul, nc.tensor.transpose

            def open_bank(*key):
                n = len(number)
                number[key] = n
                if n >= BANKS:
                    pe.wait_ge(bank_emptied[n % BANKS], n // BANKS)
                return banks[n % BANKS]

            def close_bank(ins, *key):
                ins.then_inc(filled(*key)[0], 1)

            def slab(*key):
                n = slab_at[key]
                count = sum(slab_dmas[m] for m in range(n % SLOTS, n + 1, SLOTS))
                pe.wait_ge(slab_loaded[n % SLOTS], 16 * count)
                return slabs[:, n % SLOTS, :]

            def free_slab(key, *group):
                last_use[slab_at[key]] = filled(*group)

            def norm_transposes(n, xn, tiles, per_bank):
                pe.wait_ge(*xn_by_vector.at(n))
                pe.wait_ge(*xn_by_scalar.at(n))
                for b in range(KD // per_bank):
                    o = open_bank("hT", n, b)
                    for kk in range(per_bank):
                        k = b * per_bank + kk
                        for t in range(tiles):
                            c = (kk * tiles + t) * P
                            ins = tr(o[:, c:c + P], xn[:, t, k * P:(k + 1) * P], ident[:, :])
                    close_bank(ins, "hT", n, b)

            def wait_hT(n, per_bank):
                for b in range(KD // per_bank):
                    pe.wait_ge(*emptied("hT", n, b))

            def tokens_by_features(group, w, lhs, ks, width):
                o = open_bank(*group)
                for n, k in enumerate(ks):
                    ins = mm(o[:, 0:width], lhs(k), w[:, k, 0:width], start=n == 0, stop=n == len(ks) - 1)
                    if n < len(ks) - 1:
                        yield
                close_bank(ins, *group)
                if group[0] == "gate":
                    ended_in[(group[1], "at")].append(group)
                yield

            def run(steps):
                for _ in steps:
                    pass

            def advance(steps, n):
                for _ in range(n):
                    if next(steps, "end") == "end":
                        return

            pe.wait_ge(consts_loaded, CONSTS * 16)
            pe.wait_ge(ones_set, 1)
            for l in range(LAYERS):
                norm_transposes(2 * l, xn1, TILES, 2)
                wait_hT(2 * l, 2)
                lhs = lambda k, t=0: hT[:, k, t * P:(t + 1) * P]
                turned = [("qT", l, 0, b) for b in range(6)] + [("qT", l, 1, b) for b in range(6)]
                for c in range(9):
                    w = slab("in", l, c).rearrange("p (k n) -> p k n", k=KD)
                    for t in range(TILES):
                        run(tokens_by_features(("qkv", l, c, t), w, lambda k: hT[:, k, t * P:(t + 1) * P], range(KD), 512))
                        if c >= 6:
                            for _ in range(2):
                                key = turned.pop(0)
                                j, b = key[2], key[3]
                                pe.wait_ge(*qk_roped.at(l, j))
                                o = open_bank(*key)
                                for m in range(4):
                                    ch, tt = 2 * b + m // 2, m % 2
                                    ins = tr(o[:, m * P:(m + 1) * P], qkv[:, j, tt, ch * P:(ch + 1) * P], ident[:, :])
                                close_bank(ins, *key)
                    free_slab(("in", l, c), "qkv", l, c, TILES - 1)
                for c in range(6, 9):
                    for t in range(TILES):
                        pe.wait_ge(*emptied("qkv", l, c, t))
                for j in range(2):
                    for b in range(6):
                        pe.wait_ge(*emptied("qT", l, j, b))

                def gate_groups():
                    for c in range(9, 15):
                        w = slab("in", l, c).rearrange("p (k n) -> p k n", k=KD)
                        for t in range(TILES):
                            key = ("gate", l, c - 9, t)
                            yield from tokens_by_features(key, w, lambda k: hT[:, k, t * P:(t + 1) * P], range(KD), 512)
                        free_slab(("in", l, c), "gate", l, c - 9, TILES - 1)

                def head(j, h, cols):
                    half = DH * (h % 2)
                    return qkT[half:half + DH, j, h // 2, cols]

                def scores(u):
                    kind, h, t = U[u]
                    q = slice(t * P, (t + 1) * P)
                    if kind == "A":
                        span = (t + 1) * P
                        o = open_bank("s", l, u)
                        for g in range(G_A):
                            hd = g * N_A + h
                            if g == 2 and t == 1:
                                close_bank(ins, "s", l, u)
                                o = open_bank("s2", l, u)
                            c = g * span if not (g == 2 and t == 1) else 0
                            ins = mm(o[:, c:c + span], head(0, hd, q), head(1, hd, slice(0, span)), start=True, stop=True)
                        close_bank(ins, "s2" if t else "s", l, u)
                    elif kind == "B":
                        o = open_bank("s", l, u)
                        hd = 12 + h
                        ins = mm(o[:, 0:(t + 1) * P], head(0, hd, q), head(1, hd, slice(0, (t + 1) * P)), start=True, stop=True)
                        close_bank(ins, "s", l, u)
                    else:
                        hd = ROT + h
                        o = open_bank("s", l, u)
                        mm(o[:, 0:SEQ], head(1, hd, slice(0, P)), head(0, hd, slice(0, SEQ)), start=True, stop=True)
                        ins = mm(o[:, SEQ:SEQ + P], head(1, hd, slice(P, SEQ)), head(0, hd, slice(P, SEQ)), start=True, stop=True)
                        close_bank(ins, "s", l, u)

                def second(u):
                    kind, h, t = U[u]
                    if kind == "C":
                        pe.wait_ge(*stick_summed.at(l, u))
                        sp = PT[:, u % 2, 384:768]
                        o = open_bank("p", l, u, 0)
                        mm(o[:, 0:SEQ], tri, sp[:, 0:SEQ], start=True, stop=False)
                        mm(o[:, P:SEQ], ones[:, :], sp[:, SEQ:SEQ + P], start=False, stop=True)
                        ins = mm(o[:, SEQ:SEQ + P], tri, sp[:, SEQ:SEQ + P], start=True, stop=True)
                        close_bank(ins, "p", l, u, 0)
                        return
                    pe.wait_ge(*probs_scaled.at(l, u))
                    blocks = (G_A if kind == "A" else 1) * (t + 1)
                    for b0 in range(0, blocks, 4):
                        o = open_bank("p", l, u, b0 // 4)
                        for b in range(b0, min(blocks, b0 + 4)):
                            ins = tr(o[:, (b - b0) * P:(b - b0 + 1) * P], S[:, u % 2, b * P:(b + 1) * P], ident[:, :])
                        close_bank(ins, "p", l, u, b0 // 4)

                def values(u):
                    kind, h, t = U[u]
                    v = lambda hd, jt: qkv[:, 2, jt, hd * DH:(hd + 1) * DH]
                    o = None
                    if kind == "C":
                        pe.wait_ge(*stick_weights.at(l, u))
                        o = open_bank("o", l, u)
                        a = PT[:, u % 2, 0:384]
                        mm(o[0:DH, 0:SEQ], v(ROT + h, 0), a[:, 0:SEQ], start=True, stop=False)
                        ins = mm(o[0:DH, P:SEQ], v(ROT + h, 1), a[:, SEQ:SEQ + P], start=False, stop=True)
                        close_bank(ins, "o", l, u)
                        return
                    blocks = (G_A if kind == "A" else 1) * (t + 1)
                    for b0 in range(0, blocks, 4):
                        pe.wait_ge(*emptied("p", l, u, b0 // 4))
                    o = open_bank("o", l, u)
                    for b in range(blocks):
                        g, jt = b // (t + 1), b % (t + 1)
                        hd = g * N_A + h if kind == "A" else 12 + h
                        ins = mm(o[0:DH, 0:P], v(hd, jt), PT[:, u % 2, b * P:(b + 1) * P], start=b == 0, stop=b == blocks - 1)
                    close_bank(ins, "o", l, u)

                U = units_of_block1()
                filler = gate_groups()
                for u in range(len(U) + 1):
                    ended_in[(l, "at")] = []
                    if u < len(U):
                        scores(u)
                    if u >= 1:
                        second(u - 1)
                    advance(filler, 4 if u < len(U) else 1000)
                    if u >= 1:
                        values(u - 1)
                    ended_in[(l, u)] = ended_in[(l, "at")]

                for u in range(len(U)):
                    pe.wait_ge(*emptied("o", l, u))
                for c in range(2):
                    w = slab("out", l, c).rearrange("p (k n) -> p k n", k=KD)
                    for t in range(TILES):
                        for br, ks in enumerate((range(0, 2), range(2, 5), range(5, 8))):
                            run(tokens_by_features(("y", l, c, t, br), w, lambda k: oT[:, k, t * P:(t + 1) * P], ks, 512))
                    free_slab(("out", l, c), "y", l, c, TILES - 1, 2)
                pe.wait_ge(*merged_ready.at(l))
                for b in range(4):
                    o = open_bank("mT", l, b)
                    for m in range(4):
                        k, t = 2 * b + m // 2, m % 2
                        ins = tr(o[:, m * P:(m + 1) * P], merged[:, t, k * P:(k + 1) * P], ident[:, :])
                    close_bank(ins, "mT", l, b)
                for b in range(4):
                    pe.wait_ge(*emptied("mT", l, b))
                for c in range(2):
                    w = slab("o", l, c).rearrange("p (k n) -> p k n", k=KD)
                    for t in range(TILES):
                        run(tokens_by_features(("wo", l, c, t), w, lambda k: hT[:, k, t * P:(t + 1) * P], range(KD), 512))
                    free_slab(("o", l, c), "wo", l, c, TILES - 1)

                norm_transposes(2 * l + 1, xn1, TILES, 2)
                wait_hT(2 * l + 1, 2)
                for c in range(8):
                    w = slab("up", l, c).rearrange("p (k n) -> p k n", k=KD)
                    for m in range(2):
                        o = open_bank("up", l, 2 * c + m)
                        for j in range(2):
                            ch = (2 * m + j) * P
                            for k in range(KD):
                                ins = mm(o[:, j * SEQ:(j + 1) * SEQ], w[:, k, ch:ch + P], hT[:, k, :],
                                         start=k == 0, stop=k == KD - 1)
                        close_bank(ins, "up", l, 2 * c + m)
                    free_slab(("up", l, c), "up", l, 2 * c + 1)
                accs = {(t, c): open_bank("down", l, t, c) for t in range(TILES) for c in range(2)}
                for s in range(8):
                    w = slab("down", l, s).rearrange("p (k n) -> p k n", k=4)
                    for kk in range(4):
                        k = 4 * s + kk
                        if k % 2 == 0:
                            pe.wait_ge(*emptied("up", l, k // 2))
                        for t in range(TILES):
                            for c in range(2):
                                ins = mm(accs[t, c][:, :], uT[:, k, t * P:(t + 1) * P], w[:, kk, c * 512:(c + 1) * 512],
                                         start=k == 0, stop=k == FF // P - 1)
                                if k == FF // P - 1:
                                    close_bank(ins, "down", l, t, c)
                                elif kk == 3 and t == 1 and c == 1:
                                    if s < 7:
                                        ins.then_inc(down_used.by(l, s)[0], 1)
                    last_use[slab_at["down", l, s]] = down_used.at(l, s) if s < 7 else filled("down", l, 1, 1)

            def modulation(l, row):
                pe.wait_ge(*cond_ready_s.at("done"))
                for c in range(6):
                    w = slab("ada", l, c).rearrange("p (k n) -> p k n", k=KD)
                    o = open_bank("ada", l, c)
                    for k in range(KD):
                        ins = mm(o[0:2, :], cond[:, k, :], w[:, k, :], start=k == 0, stop=k == KD - 1)
                    close_bank(ins, "ada", l, c)
                    free_slab(("ada", l, c), "ada", l, c)
                for c in range(6):
                    pe.wait_ge(*emptied("ada", l, c))
                o = open_bank("adaT", l)
                for k in range(16):
                    ins = tr(o[:, 2 * k:2 * k + 2], row[0:2, k * P:(k + 1) * P], ident[0:2, 0:2])
                close_bank(ins, "adaT", l)
                for s in range(2):
                    for c in range(2):
                        o = open_bank("gateB", l, s, c)
                        ins = mm(o[:, :], select[:, s, :], row[0:2, 2 * D + c * 512:2 * D + (c + 1) * 512], start=True, stop=True)
                        close_bank(ins, "gateB", l, s, c)

            def project2(l, j, tiles):
                w = slab("in2", l, j).rearrange("p (k n) -> p k n", k=KD)
                width = IN2[j][1] - IN2[j][0]
                for t in tiles:
                    run(tokens_by_features(("in2", l, j, t), w, lambda k: hT2[:, k, t * P:(t + 1) * P], range(KD), width))
                free_slab(("in2", l, j), "in2", l, j, tiles[-1])

            def feature_groups(l, j, n):
                w = slab("in2", l, j).rearrange("p (k n) -> p k n", k=KD)
                for c in range(4):
                    key = ("in2f", l, 4 * (j - 2) + c)
                    o = open_bank(*key)
                    for k in range(KD):
                        ins = mm(o[:, 0:n], w[:, k, c * P:(c + 1) * P], hT2[:, k, 0:n], start=k == 0, stop=k == KD - 1)
                        if k < KD - 1:
                            yield
                    close_bank(ins, *key)
                    ended_in.setdefault((2 + l, "at"), []).append(key)
                    yield
                free_slab(("in2", l, j), "in2f", l, 4 * (j - 2) + 3)

            def turn_heads(l, j, src, chunks, tiles, per_bank):
                pe.wait_ge(*heads_ready.at(l, j))
                for b in range(chunks // per_bank):
                    o = open_bank("heads", l, j, b)
                    for m in range(per_bank):
                        for t in range(tiles):
                            ins = tr(o[:, (m * tiles + t) * P:(m * tiles + t + 1) * P], src(b * per_bank + m, t), ident[:, :])
                    close_bank(ins, "heads", l, j, b)

            def attention2(l, filler, per_unit):
                U = units_of_block2(l)

                def scores(u):
                    kind, h, t = U[u]
                    half = DH * (h % 2)
                    first = SEQ if kind == "G" and t >= TILES else 0
                    if kind == "G":
                        q, k = qT2, kT2[half:half + DH, h // 4, first:N4]
                    elif kind == "W":
                        q, k = wqT, wkT[half:half + DH, h // 4, :]
                    else:
                        q, k = nqT, nkT[half:half + DH, h // 2, :]
                    o = open_bank("s", 2 + l, u)
                    ins = mm(o[:, 0:N4 - first], q[half:half + DH, h // 2, t * P:(t + 1) * P], k, start=True, stop=True)
                    close_bank(ins, "s", 2 + l, u)

                def blocks_of(u):
                    kind, h, t = U[u]
                    return range(2, 4) if kind == "G" and t >= TILES else range(4)

                def second(u):
                    pe.wait_ge(*probs_scaled.at(2 + l, u))
                    o = open_bank("p", 2 + l, u, 0)
                    for n, _ in enumerate(blocks_of(u)):
                        ins = tr(o[:, n * P:(n + 1) * P], S[:, u % 2, n * P:(n + 1) * P], ident[:, :])
                    close_bank(ins, "p", 2 + l, u, 0)

                def values(u):
                    kind, h, t = U[u]
                    pe.wait_ge(*emptied("p", 2 + l, u, 0))
                    o = open_bank("o", 2 + l, u)
                    blocks = blocks_of(u)
                    for n, b in enumerate(blocks):
                        if kind == "G":
                            v = kv2[:, b, (KVH + h // 4) * DH:(KVH + h // 4 + 1) * DH]
                        elif kind == "W":
                            v = kv3[:, b, (KVH + h // 4) * DH:(KVH + h // 4 + 1) * DH]
                        else:
                            v = nv[:, b, h * DH:(h + 1) * DH]
                        ins = mm(o[0:DH, 0:P], v, PT[:, u % 2, n * P:(n + 1) * P], start=n == 0, stop=n == len(blocks) - 1)
                    close_bank(ins, "o", 2 + l, u)

                for u in range(len(U) + 1):
                    ended_in[(2 + l, "at")] = []
                    if u < len(U):
                        scores(u)
                    if u >= 1:
                        second(u - 1)
                    advance(filler, per_unit(u) if u < len(U) else 1000)
                    if u >= 1:
                        values(u - 1)
                    ended_in[(2 + l, u)] = ended_in[(2 + l, "at")]

            def out2(l, tiles, low, high):
                for c in range(2):
                    w = slab("out2", l, c).rearrange("p (k n) -> p k n", k=KD)
                    for t in tiles:
                        lhs = lambda k: (low[:, k, t * P:(t + 1) * P] if k < 4 else high[:, k - 4, t * P:(t + 1) * P])
                        run(tokens_by_features(("out2", l, c, t), w, lhs, range(KD), 512))
                    free_slab(("out2", l, c), "out2", l, c, tiles[-1])

            pe.wait_ge(late_loaded, LATE0 * 16)
            modulation(0, ada_row)
            norm_transposes(5, xn2, T4, 1)
            wait_hT(5, 1)
            project2(0, 0, range(T4))
            project2(0, 1, range(T4))

            def fill0():
                for j in range(2, 7):
                    yield from feature_groups(0, j, N4)

            filler = fill0()
            ended_in[(2, "at")] = []
            advance(filler, 8)
            ended_in[(2, "before")] = ended_in[(2, "at")]
            turn_heads(0, 0, lambda c, t: q2[:, t, c * P:(c + 1) * P], 4, T4, 1)
            turn_heads(0, 1, lambda c, t: k2d[:, t, c, :], KVH, T4, 1)
            for b in range(4):
                pe.wait_ge(*emptied("heads", 0, 0, b))
            for b in range(KVH):
                pe.wait_ge(*emptied("heads", 0, 1, b))
            for t in range(T4):
                pe.wait_ge(*emptied("in2", 0, 1, t))
            attention2(0, filler, lambda u: 5)

            pe.wait_ge(filter_loaded, FILTERS * 16)
            o = open_bank("f", 0)
            close_bank(mm(o[0:HID, 0:SEQ], hyena_w1, positions, start=True, stop=True), "f", 0)
            pe.wait_ge(*sin_ready.at(0))
            o = open_bank("f", 1)
            close_bank(mm(o[0:HID, 0:SEQ], hyena_w2, hidden[0:HID, 0, :], start=True, stop=True), "f", 1)
            pe.wait_ge(*sin_ready.at(1))
            for od in range(2):
                for d in range(2):
                    for t in range(TILES):
                        o = open_bank("tap", od, d, t)
                        ins = mm(o[:, :], hidden[0:HID, 1, t * P:(t + 1) * P], w3[0:HID, od, d, :], start=True, stop=True)
                        close_bank(ins, "tap", od, d, t)
                pe.wait_ge(*taps_squared.at(od))
                o = open_bank("energy", od)
                for n in range(4):
                    ins = mm(o[:, :], ones[:, :], work.rearrange("p (a n) -> p a n", a=4)[:, n, :], start=n == 0, stop=n == 3)
                close_bank(ins, "energy", od)
                pe.wait_ge(*taps_mixed.at(od))
                for m in range(2):
                    for which in range(2):
                        o = open_bank("spec", od, m, which)
                        for t in range(TILES):
                            ins = mm(o[:, :], fourier[:, which, t, m * P:(m + 1) * P], taps_sd[:, which, t, :], start=t == 0, stop=t == 1)
                        close_bank(ins, "spec", od, m, which)
                o = open_bank("nyq", od)
                for t in range(TILES):
                    ins = mm(o[0:1, :], fourier[:, 1, t, 0:1], taps_sd[:, 0, t, :], start=t == 0, stop=t == 1)
                close_bank(ins, "nyq", od)
            for c in range(HY_CH):
                pe.wait_ge(*emptied("in2f", 0, c))
            for c in range(8):
                o = open_bank("zg", c)
                for t in range(T4):
                    ins = tr(o[:, t * P:(t + 1) * P], uc[:, c, t * P:(t + 1) * P], ident[:, :])
                close_bank(ins, "zg", c)
            for c in range(8):
                pe.wait_ge(*emptied("zg", c))
            for od in range(2):
                for s in range(2):
                    if od == 1:
                        for t in range(TILES):
                            pe.wait_ge(*emptied("z1", s, t))
                    for m in range(2):
                        for which in range(2):
                            o = open_bank("zf", od, s, m, which)
                            for t in range(TILES):
                                ins = mm(o[:, :], fourier[:, which, t, m * P:(m + 1) * P], Z[:, 2 * s + t, :], start=t == 0, stop=t == 1)
                            close_bank(ins, "zf", od, s, m, which)
                    if s == 1:
                        inverse_now = (0, 1)
                    else:
                        inverse_now = ()
                    for ss in inverse_now:
                        pe.wait_ge(*spectrum_ready.at(od, ss))
                        if od == 0:
                            for t in range(TILES):
                                o = open_bank("z1", ss, t)
                                for kk in range(4):
                                    ins = mm(o[:, :], fourier[:, 2 + kk // 2, kk % 2, t * P:(t + 1) * P], spectrum(ss)[:, kk, :],
                                             start=kk == 0, stop=kk == 3)
                                close_bank(ins, "z1", ss, t)
                        else:
                            for c2 in range(2):
                                o = open_bank("y2", ss, c2)
                                for cc in range(2):
                                    c = 2 * c2 + cc
                                    for kk in range(4):
                                        ins = mm(o[:, cc * SEQ:(cc + 1) * SEQ], spectrum(ss)[:, kk, c * P:(c + 1) * P],
                                                 fourier[:, 2 + kk // 2, kk % 2, :], start=kk == 0, stop=kk == 3)
                                close_bank(ins, "y2", ss, c2)
            for s in range(2):
                for c2 in range(2):
                    pe.wait_ge(*emptied("y2", s, c2))
            pe.wait_ge(*gated_ready.at(0))
            out2(0, range(T4), oT2, yTh)

            modulation(1, ada_row3)
            norm_transposes(6, xn3, T4, 1)
            wait_hT(6, 1)
            project2(1, 0, range(TILES))
            project2(1, 1, range(T4))
            project2(1, 2, range(TILES))
            project2(1, 3, range(T4))
            turn_heads(1, 0, lambda c, t: wq[:, t, c * P:(c + 1) * P], 4, TILES, 2)
            turn_heads(1, 1, lambda c, t: k3d[:, t, c, :], KVH, T4, 1)
            project2(1, 4, range(T4))
            turn_heads(1, 2, lambda c, t: nq[:, t, c * P:(c + 1) * P], 4, TILES, 2)
            turn_heads(1, 3, lambda c, t: nk[:, t, c * P:(c + 1) * P], 4, T4, 1)
            for j, n in ((0, 2), (1, 2), (2, 2), (3, 4)):
                for b in range(n):
                    pe.wait_ge(*emptied("heads", 1, j, b))
            for j in (1, 4):
                for t in range(T4):
                    pe.wait_ge(*emptied("in2", 1, j, t))

            def fill1():
                for j in (5, 6):
                    yield from feature_groups(1, j, SEQ)

            attention2(1, fill1(), lambda u: 8 if u % 4 == 0 else 0)
            pe.wait_ge(*gated_ready.at(1))
            out2(1, range(TILES), oT3, yT3)

        @block.scalar
        def _(act):
            run = Steps(act, scalar_step)
            A_ = nc.scalar.activation

            def norm_guess(n, tiles, xn):
                for t in range(tiles):
                    run(A_(xn[:, t, :], X[:, t, :], ACT.Square, accum_out=nstat[:, 0, t:t + 1]))
                run.settle()
                run(A_(nstat[:, 1, 0:tiles], nstat[:, 0, 0:tiles], ACT.Ln, bias=eps_col[:, 0:1], scale=1.0 / D))
                run.settle()
                run(A_(nstat[:, 2, 0:tiles], nstat[:, 1, 0:tiles], ACT.Exp, scale=-0.5), rsqrt_guess.by(n))

            def norm_scale(n, tiles, xn):
                act.wait_ge(*rstd_ready.at(n))
                run.settle()
                for t in range(1, tiles, 2):
                    last = t + 2 > tiles
                    run(A_(xn[:, t, :], X[:, t, :], ACT.Copy, scale=nstat[:, 2, t:t + 1]),
                        xn_by_scalar.by(n) if last else None)

            def copy_out(dst, src, *key):
                act.wait_ge(*filled(*key))
                run(A_(dst, src, ACT.Copy), emptied(*key))

            def norm_evacuate(n, which, l):
                for b in (1, 3):
                    act.wait_ge(*filled("hT", n, b))
                    for kk in range(2):
                        k = 2 * b + kk
                        run(A_(hT[:, k, :], bank("hT", n, b)[:, kk * SEQ:(kk + 1) * SEQ], ACT.Copy,
                               scale=g_cols[:, which, l, k:k + 1]), emptied("hT", n, b) if kk else None)

            def softmax_exp(l, u, width, src, kind, scale):
                act.wait_ge(*bias_ready.at(l, u))
                if kind in "WN":
                    if kind == "W":
                        h = units_of_block2(l - 2)[u][1]
                        run(A_(stat[:, u % 2, 3, 1:2], sink[:, h:h + 1], ACT.Exp, bias=stat[:, u % 2, 1, 0:1]))
                run(A_(S[:, u % 2, 0:width], src, ACT.Exp, bias=stat[:, u % 2, 1, 0:1], scale=scale,
                       accum_out=stat[:, u % 2, 2, 0:1]), probs_ready.by(l, u))

            act.wait_ge(x_loaded, 16)
            act.wait_ge(consts_loaded, CONSTS * 16)
            act.wait_ge(ones_set, 1)
            run(A_(cond_e[:, :, :], cond[:, :, :], ACT.Exp, scale=-1.0), cond_exp.by(0))
            for l in range(LAYERS):
                if l:
                    act.wait_ge(*x_added.at(2 * l - 1))
                norm_guess(2 * l, TILES, xn1)
                norm_scale(2 * l, TILES, xn1)
                norm_evacuate(2 * l, 0, l)
                for c in range(9):
                    for t in range(TILES):
                        copy_out(qkv[:, c // 3, t, c % 3 * 512:(c % 3 + 1) * 512], bank("qkv", l, c, t)[:, :], "qkv", l, c, t)
                        if c >= 6:
                            for _ in range(2):
                                n = (c - 6) * 4 + t * 2 + _
                                j, b = n // 6, n % 6
                                if n % 2:
                                    copy_out(qkT[:, j, 2 * b:2 * b + 2, :], bank("qT", l, j, b)[:, :].rearrange("p (a n) -> p a n", a=2), "qT", l, j, b)
                U = units_of_block1()

                def take_second(u):
                    kind, h, t = U[u]
                    if u >= 2:
                        act.wait_ge(*filled("o", l, u - 2))
                    if kind == "C":
                        act.wait_ge(*stick_argument.at(l, u))
                        run(A_(PT[:, u % 2, 0:384], S[:, u % 2, 384:768], ACT.Exp, scale=SCALE), stick_weights.by(l, u))
                        return
                    blocks = (G_A if kind == "A" else 1) * (t + 1)
                    for b0 in range(0, blocks, 4):
                        n = min(4, blocks - b0) * P
                        copy_out(PT[:, u % 2, b0 * P:b0 * P + n], bank("p", l, u, b0 // 4)[:, 0:n], "p", l, u, b0 // 4)

                def take_values(u):
                    kind, h, t = U[u]
                    chunk, half = {"A": 0, "B": 2, "C": 5}[kind] + h // 2, DH * (h % 2)
                    cols = slice(0, SEQ) if kind == "C" else slice(t * P, (t + 1) * P)
                    n = SEQ if kind == "C" else P
                    copy_out(oT[half:half + DH, chunk, cols], bank("o", l, u)[0:DH, 0:n], "o", l, u)

                for u in range(len(U) + 1):
                    if u >= 1:
                        take_second(u - 1)
                    if u < len(U):
                        kind, h, t = U[u]
                        if kind == "C":
                            act.wait_ge(*stick_masked.at(l, u))
                            s = S[:, u % 2, 384:768]
                            run(A_(s, S[:, u % 2, 0:384], ACT.Abs))
                            run.settle()
                            run(A_(s, s, ACT.Exp, scale=-SCALE))
                            run.settle()
                            run(A_(s, s, ACT.Ln, bias=eps_col[:, 1:2]), softplus_part.by(l, u))
                        else:
                            w = (G_A if kind == "A" else 1) * (t + 1) * P
                            softmax_exp(l, u, w, S[:, u % 2, 0:w], kind, SCALE)
                    for key in ended_in[(l, u)]:
                        _, _, c, t = key
                        act.wait_ge(*filled(*key))
                        if l + c + t == 0:
                            act.wait_ge(rel_stored, 16)
                        run(A_(gates[:, t, c // 2, c % 2 * 512:(c % 2 + 1) * 512], bank(*key)[:, :], ACT.Exp, scale=-1.0),
                            emptied(*key))
                    if u >= 1:
                        take_values(u - 1)
                for b in range(4):
                    copy_out(hT[:, 2 * b:2 * b + 2, :], bank("mT", l, b)[:, :].rearrange("p (a n) -> p a n", a=2), "mT", l, b)
                act.wait_ge(*x_added.at(2 * l))
                norm_guess(2 * l + 1, TILES, xn1)
                norm_scale(2 * l + 1, TILES, xn1)
                norm_evacuate(2 * l + 1, 1, l)
            act.wait_ge(*x_added.at(3))
            norm_guess(4, TILES, xn1)

            def modulated_evacuate(n, l):
                for k in range(KD):
                    act.wait_ge(*filled("hT", n, k))
                    if k == 0:
                        act.wait_ge(*ada_ready.at(l))
                    run(A_(hT2[:, k, SEQ:N4], bank("hT", n, k)[:, SEQ:N4], ACT.Identity,
                           scale=gain[:, k, 1:2], bias=ada_t[:, k, 1:2]), hT_by_scalar.by(n, k))

            def gate_rows(l):
                for s in range(2):
                    for c in range(2):
                        copy_out(gate_b[:, s, c * 512:(c + 1) * 512], bank("gateB", l, s, c)[:, :], "gateB", l, s, c)

            def heads_rsqrt(l, j, n):
                act.wait_ge(*heads_squared.at(l, j))
                run(A_(nstat[:, 1, 0:n], nstat[:, 0, 0:n], ACT.Ln, bias=eps_col[:, 0:1], scale=1.0 / DH))
                run.settle()
                run(A_(nstat[:, 2, 0:n], nstat[:, 1, 0:n], ACT.Exp, scale=-0.5), heads_guess.by(l, j))

            def take_features(l, key):
                c = key[2]
                if l == 0 and c < HY_CH:
                    act.wait_ge(*filled(*key))
                    run(A_(uc[:, c, :], bank(*key)[:, :], ACT.Identity, scale=conv_w[:, 1, c:c + 1], bias=conv_w[:, 3, c:c + 1]),
                        conv_begun.by(c))
                else:
                    n, dst = (N4, (ag, hg)) if l == 0 else (SEQ, (wgT, ngT))
                    c -= HY_CH
                    act.wait_ge(*filled(*key))
                    run(A_(dst[c // 4][:, c % 4, :], bank(*key)[:, 0:n], ACT.Exp, scale=-1.0), silu_exp.by(l, c))

            def attention2(l):
                U = units_of_block2(l)
                for u in range(len(U) + 1):
                    if u >= 1:
                        n = (2 if U[u - 1][0] == "G" and U[u - 1][2] >= TILES else 4) * P
                        if u >= 3:
                            act.wait_ge(*filled("o", 2 + l, u - 3))
                        copy_out(PT[:, (u - 1) % 2, 0:n], bank("p", 2 + l, u - 1, 0)[:, 0:n], "p", 2 + l, u - 1, 0)
                    if u < len(U):
                        kind, h, t = U[u]
                        n = SEQ if kind == "G" and t >= TILES else N4
                        if kind == "G":
                            act.wait_ge(*bias_ready.at(2, u))
                            if u >= 2:
                                act.wait_ge(*filled("p", 2 + l, u - 2, 0))
                            run(A_(S[:, u % 2, 0:n], bank("s", 2, u)[:, 0:n], ACT.Exp, bias=stat[:, u % 2, 1, 0:1],
                                   scale=SCALE, accum_out=stat[:, u % 2, 2, 0:1]), probs_ready.by(2, u))
                        else:
                            softmax_exp(2 + l, u, n, S[:, u % 2, 0:n], kind, 1.0)
                    for key in ended_in[(2 + l, u)]:
                        take_features(l, key)
                    if u >= 1:
                        kind, h, t = U[u - 1]
                        half = DH * (h % 2)
                        dst = {"G": oT2, "W": oT3, "N": yT3}[kind]
                        copy_out(dst[half:half + DH, h // 2, t * P:(t + 1) * P], bank("o", 2 + l, u - 1)[0:DH, 0:P], "o", 2 + l, u - 1)

            act.wait_ge(*x_added.at(4))
            act.wait_ge(x_loaded, 32)
            norm_guess(5, T4, xn2)
            norm_scale(5, T4, xn2)
            gate_rows(0)
            modulated_evacuate(5, 0)
            for t in range(T4):
                copy_out(q2[:, t, :], bank("in2", 0, 0, t)[:, :], "in2", 0, 0, t)
            for t in range(T4):
                copy_out(kv2[:, t, :], bank("in2", 0, 1, t)[:, 0:256], "in2", 0, 1, t)
            heads_rsqrt(0, 0, T4 * QH)
            heads_rsqrt(0, 1, T4 * KVH)
            for key in ended_in[(2, "before")]:
                take_features(0, key)
            for b in range(4):
                copy_out(qT2[:, b, :], bank("heads", 0, 0, b)[:, :], "heads", 0, 0, b)
            for b in range(KVH):
                copy_out(kT2[:, b, :], bank("heads", 0, 1, b)[:, :], "heads", 0, 1, b)
            attention2(0)
            for n in range(2):
                act.wait_ge(*sin_in_range.at(n))
                run(A_(hidden[0:HID, n, :], hidden[0:HID, n, :], ACT.Sin), sin_ready.by(n))
            for od in range(2):
                act.wait_ge(*filled("energy", od))
                run(A_(rn[:, 0, :], bank("energy", od)[:, :], ACT.Ln, bias=eps_col[:, 0:1]))
                run.settle()
                run(A_(rn[:, 0, :], rn[:, 0, :], ACT.Exp, scale=-0.5), taps_guess.by(od))
            act.wait_ge(*spectra_ready.at(1))
            for c in range(8):
                if c % 2:
                    dst = (Z, G1)[c // 4][:, :, c % 4 * P:(c % 4 + 1) * P]
                    copy_out(dst, bank("zg", c)[:, :].rearrange("p (t n) -> p t n", t=T4), "zg", c)

            act.wait_ge(*x_added.at(5))
            norm_guess(6, T4, xn3)
            norm_scale(6, T4, xn3)
            gate_rows(1)
            modulated_evacuate(6, 1)
            for t in range(TILES):
                copy_out(wq[:, t, :], bank("in2", 1, 0, t)[:, :], "in2", 1, 0, t)
            for t in range(T4):
                copy_out(kv3[:, t, :], bank("in2", 1, 1, t)[:, 0:256], "in2", 1, 1, t)
            for t in range(TILES):
                copy_out(nq[:, t, :], bank("in2", 1, 2, t)[:, :], "in2", 1, 2, t)
            for t in range(T4):
                copy_out(nk[:, t, :], bank("in2", 1, 3, t)[:, :], "in2", 1, 3, t)
            heads_rsqrt(1, 0, TILES * QH)
            heads_rsqrt(1, 1, T4 * KVH)
            for b in range(2):
                copy_out(wqT[:, 2 * b:2 * b + 2, :], bank("heads", 1, 0, b)[:, :].rearrange("p (a n) -> p a n", a=2), "heads", 1, 0, b)
            for b in range(KVH):
                copy_out(wkT[:, b, :], bank("heads", 1, 1, b)[:, :], "heads", 1, 1, b)
            for t in range(T4):
                copy_out(nv[:, t, :], bank("in2", 1, 4, t)[:, :], "in2", 1, 4, t)
            heads_rsqrt(1, 2, TILES * QH)
            heads_rsqrt(1, 3, T4 * QH)
            for b in range(2):
                copy_out(nqT[:, 2 * b:2 * b + 2, :], bank("heads", 1, 2, b)[:, :].rearrange("p (a n) -> p a n", a=2), "heads", 1, 2, b)
            for b in range(4):
                copy_out(nkT[:, b, :], bank("heads", 1, 3, b)[:, :], "heads", 1, 3, b)
            attention2(1)

        @block.vector
        def _(dve):
            run = Steps(dve, vector_step)
            V = nc.vector

            def newton(v, y, t, width=None):
                run(V.tensor_tensor(t, y, y, ALU.mult))
                run.settle()
                run(V.tensor_tensor(t, t, v, ALU.mult))
                run.settle()
                run(V.tensor_scalar(t, t, -0.5, 1.5, ALU.mult, ALU.add))
                run.settle()

            def norm_finish(n, tiles, xn):
                dve.wait_ge(*rsqrt_guess.at(n))
                v, y, t = nstat[:, 0, 0:tiles], nstat[:, 2, 0:tiles], nstat[:, 3, 0:tiles]
                run(V.tensor_scalar(v, v, 1.0 / D, EPS, ALU.mult, ALU.add))
                run.settle()
                newton(v, y, t)
                run(V.tensor_tensor(y, y, t, ALU.mult), rstd_ready.by(n))
                run.settle()
                if xn is None:
                    return
                for tt in range(0, tiles, 2):
                    run(V.tensor_scalar(xn[:, tt, :], X[:, tt, :], nstat[:, 2, tt:tt + 1], None, ALU.mult),
                        xn_by_vector.by(n) if tt + 2 >= tiles else None)

            def norm_evacuate(n, which, l):
                for b in (0, 2):
                    dve.wait_ge(*filled("hT", n, b))
                    g = g_cols[:, which, l, 2 * b:2 * b + 2].unsqueeze(2).to_broadcast([P, 2, SEQ])
                    run(V.tensor_tensor(hT[:, 2 * b:2 * b + 2, :], bank("hT", n, b)[:, :].rearrange("p (a n) -> p a n", a=2),
                                        g, ALU.mult), emptied("hT", n, b))

            dve.wait_ge(consts_loaded, CONSTS * 16)
            run(V.memset(ones[:, :], 1.0))
            run(V.memset(eps_col[:, 0:1], EPS))
            V.memset(eps_col[:, 1:2], 1.0).then_inc(ones_set, 1)
            dve.wait_ge(ones_set, 1)
            dve.wait_ge(*cond_exp.at(0))
            run(V.tensor_scalar(cond_e[:, :, :], cond_e[:, :, :], 1.0, None, ALU.add), cond_ready_s.by("sum"))
            run.settle()
            run(V.reciprocal(cond_e[:, :, :], cond_e[:, :, :]))
            run.settle()
            run(V.tensor_tensor(cond[:, :, :], cond[:, :, :], cond_e[:, :, :], ALU.mult), cond_ready_s.by("done"))
            dve.wait_ge(x_loaded, 16)

            for l in range(LAYERS):
                norm_finish(2 * l, TILES, xn1)
                norm_evacuate(2 * l, 0, l)
                for j in range(2):
                    for c in range(3 * j, 3 * j + 3):
                        for t in range(TILES):
                            dve.wait_ge(*emptied("qkv", l, c, t))
                    h3 = ROPE // 2
                    for t in range(TILES):
                        hd = qkv[:, j, t, 0:ROT * DH].rearrange("p (h d) -> p h d", h=ROT)
                        x1, x2 = hd[:, :, 0:h3], hd[:, :, h3:ROPE]
                        cos = rope_a[:, t, 0:h3].unsqueeze(1).to_broadcast([P, ROT, h3])
                        sin = rope_a[:, t, h3:ROPE].unsqueeze(1).to_broadcast([P, ROT, h3])
                        r = [rope_tmp[:, n, t, :, :] for n in range(4)]
                        run(V.tensor_tensor(r[0], x1, cos, ALU.mult))
                        run(V.tensor_tensor(r[1], x2, sin, ALU.mult))
                        run(V.tensor_tensor(r[2], x2, cos, ALU.mult))
                        run(V.tensor_tensor(r[3], x1, sin, ALU.mult))
                        run.settle()
                        run(V.tensor_tensor(x1, r[0], r[1], ALU.subtract))
                        run(V.tensor_tensor(x2, r[2], r[3], ALU.add), qk_roped.by(l, j) if t else None)
                    run.settle()
                for n in range(0, 12, 2):
                    j, b = n // 6, n % 6
                    dve.wait_ge(*filled("qT", l, j, b))
                    run(V.tensor_copy(qkT[:, j, 2 * b:2 * b + 2, :], bank("qT", l, j, b)[:, :].rearrange("p (a n) -> p a n", a=2)),
                        emptied("qT", l, j, b))

                U = units_of_block1()
                last_p = lambda u: filled("p", l, u, 1 if U[u][0] == "A" and U[u][2] else 0)

                def finish_gates(u):
                    for key in ended_in[(l, u)]:
                        _, _, c, t = key
                        g = gates[:, t, c // 2, c % 2 * 512:(c % 2 + 1) * 512]
                        dve.wait_ge(*emptied(*key))
                        run(V.tensor_scalar(g, g, 1.0, None, ALU.add))
                        run.settle()
                        run(V.reciprocal(g, g))

                for u in range(len(U) + 1):
                    if u < len(U):
                        kind, h, t = U[u]
                        st = stat[:, u % 2, :, :]
                        if u >= 2:
                            dve.wait_ge(*last_p(u - 2))
                        dve.wait_ge(*filled("s", l, u))
                        if kind == "C":
                            run(V.tensor_tensor(S[:, u % 2, 0:384], bank("s", l, u)[:, 0:384], mask_c.rearrange("p a n -> p (a n)"), ALU.add),
                                emptied("s", l, u))
                            run.settle()
                            run(V.tensor_copy(small[:, 0:1], S[:, u % 2, 0:1]), stick_masked.by(l, u))
                        elif kind == "A":
                            n = G_A if t == 0 else 2
                            w = (t + 1) * P
                            run(V.tensor_tensor_reduce(
                                S[:, u % 2, 0:n * w].rearrange("p (g n) -> p g n", g=n),
                                bank("s", l, u)[:, 0:n * w].rearrange("p (g n) -> p g n", g=n),
                                mask_a[:, 0:n, SEQ - w:SEQ], 1.0, -3e38, ALU.add, ALU.max, st[:, 0, 0:1]), emptied("s", l, u))
                            if t:
                                dve.wait_ge(*filled("s2", l, u))
                                run(V.tensor_tensor_reduce(S[:, u % 2, 512:768], bank("s2", l, u)[:, 0:w], mask_a[:, 2, :],
                                                           1.0, -3e38, ALU.add, ALU.max, st[:, 0, 1:2]), emptied("s2", l, u))
                                run.settle()
                                run(V.tensor_tensor(st[:, 0, 0:1], st[:, 0, 0:1], st[:, 0, 1:2], ALU.max))
                        else:
                            w = (t + 1) * P
                            run(V.tensor_tensor_reduce(S[:, u % 2, 0:w], bank("s", l, u)[:, 0:w], mask_b[:, SEQ - w:SEQ],
                                                       1.0, -3e38, ALU.add, ALU.max, st[:, 0, 0:1]), emptied("s", l, u))
                        if kind != "C":
                            run.settle()
                            run(V.tensor_scalar(st[:, 1, 0:1], st[:, 0, 0:1], -SCALE, None, ALU.mult), bias_ready.by(l, u))
                    if u >= 1 and U[u - 1][0] == "C":
                        dve.wait_ge(*filled("p", l, u - 1, 0))
                        s = S[:, (u - 1) % 2, :]
                        run(V.tensor_tensor(s[:, 384:768], s[:, 0:384], bank("p", l, u - 1, 0)[:, 0:384], ALU.subtract),
                            emptied("p", l, u - 1, 0))
                        run.settle()
                        run(V.tensor_copy(small[:, 1:2], s[:, 384:385]), stick_argument.by(l, u - 1))
                    if u >= 1:
                        finish_gates(u - 1)
                    if u < len(U):
                        if kind == "C":
                            sp = PT[:, u % 2, 384:768]
                            if u >= 2:
                                dve.wait_ge(*filled("o", l, u - 2))
                            run(V.tensor_scalar(sp, S[:, u % 2, 0:384], 0.0, None, ALU.max))
                            run.settle()
                            dve.wait_ge(*softplus_part.at(l, u))
                            run(V.scalar_tensor_tensor(out=sp, in0=S[:, u % 2, 384:768], scalar=1.0 / SCALE, in1=sp,
                                                       op0=ALU.mult, op1=ALU.add), stick_summed.by(l, u))
                        else:
                            w = (G_A if kind == "A" else 1) * (t + 1) * P
                            dve.wait_ge(*probs_ready.at(l, u))
                            run(V.reciprocal(st[:, 2, 1:2], st[:, 2, 0:1]))
                            run.settle()
                            run(V.tensor_scalar(S[:, u % 2, 0:w], S[:, u % 2, 0:w], st[:, 2, 1:2], None, ALU.mult),
                                probs_scaled.by(l, u))
                finish_gates(len(U))

                run.settle()
                for c in range(2):
                    for t in range(TILES):
                        cols = slice(c * 512, (c + 1) * 512)
                        for br in range(3):
                            dve.wait_ge(*filled("y", l, c, t, br))
                            dst = merged[:, t, cols] if br == 0 else gated[:, br - 1, :]
                            run(V.tensor_tensor(dst, bank("y", l, c, t, br)[:, :], gates[:, t, br, cols], ALU.mult),
                                emptied("y", l, c, t, br))
                        run.settle()
                        run(V.tensor_tensor(merged[:, t, cols], merged[:, t, cols], gated[:, 0, :], ALU.add))
                        run.settle()
                        last = c + t == 2
                        run(V.tensor_tensor(merged[:, t, cols], merged[:, t, cols], gated[:, 1, :], ALU.add),
                            merged_ready.by(l) if last else None)
                        run.settle()

                def add_to_x(name, n):
                    for c in range(2):
                        for t in range(TILES):
                            key = (name, l, c, t) if name == "wo" else (name, l, t, c)
                            dve.wait_ge(*filled(*key))
                            x = X[:, t, c * 512:(c + 1) * 512]
                            run(V.tensor_tensor(x, x, bank(*key)[:, :], ALU.add), emptied(*key))
                    run.settle()
                    run(V.tensor_copy(small[:, 2:3], X[:, 1, D - 1:D]), x_added.by(n))
                    run.settle()

                add_to_x("wo", 2 * l)
                norm_finish(2 * l + 1, TILES, xn1)
                norm_evacuate(2 * l + 1, 1, l)
                for m in range(16):
                    dve.wait_ge(*filled("up", l, m))
                    b = bank("up", l, m)[:, :].rearrange("p (a n) -> p a n", a=2)
                    run(V.tensor_scalar(uT[:, 2 * m:2 * m + 2, :], b, 0.0, None, ALU.max))
                    run.settle()
                    run(V.tensor_tensor(uT[:, 2 * m:2 * m + 2, :], uT[:, 2 * m:2 * m + 2, :], b, ALU.mult), emptied("up", l, m))
                add_to_x("down", 2 * l + 1)

            norm_finish(4, TILES, None)
            dve.wait_ge(final_g_loaded, 16)
            for t in range(TILES):
                run(V.scalar_tensor_tensor(out=X[:, t, :], in0=X[:, t, :], scalar=nstat[:, 2, t:t + 1], in1=final_g,
                                           op0=ALU.mult, op1=ALU.mult), x_added.by(4) if t else None)

            def modulation(l, row, bias):
                dve.wait_ge(late_loaded, LATE0 * 16)
                if l:
                    dve.wait_ge(ada_bias_loaded, 16)
                for c in range(6):
                    cols = slice(c * 512, (c + 1) * 512)
                    dve.wait_ge(*filled("ada", l, c))
                    run(V.tensor_tensor(row[0:2, cols], bank("ada", l, c)[0:2, :], bias[0:2, cols], ALU.add), emptied("ada", l, c))
                dve.wait_ge(*filled("adaT", l))
                run(V.tensor_copy(ada_t[:, :, :], bank("adaT", l)[:, 0:32].rearrange("p (k s) -> p k s", k=16)), emptied("adaT", l))
                run.settle()
                run(V.tensor_scalar(gain[:, :, :], ada_t[:, KD:2 * KD, :], 1.0, None, ALU.add))
                run.settle()
                g = g_cols[:, 2, l, :].unsqueeze(2).to_broadcast([P, KD, 2])
                run(V.tensor_tensor(gain[:, :, :], gain[:, :, :], g, ALU.mult), ada_ready.by(l))

            def modulated_evacuate(n):
                run.settle()
                for k in range(KD):
                    dve.wait_ge(*filled("hT", n, k))
                    dve.wait_ge(*hT_by_scalar.at(n, k))
                    run(V.tensor_scalar(hT2[:, k, 0:SEQ], bank("hT", n, k)[:, 0:SEQ], gain[:, k, 0:1], ada_t[:, k, 0:1],
                                        ALU.mult, ALU.add), emptied("hT", n, k))

            def heads_norm(l, j, x, tiles, heads, g, rope, dup, ready):
                n = tiles * heads
                for key in ready:
                    dve.wait_ge(*emptied(*key))
                x3 = x.rearrange("p t (h d) -> p t h d", h=heads)
                sq = work[:, 0:n * DH].rearrange("p (t h d) -> p t h d", t=tiles, h=heads)
                for t in range(tiles):
                    run(V.tensor_tensor(sq[:, t], x3[:, t], x3[:, t], ALU.mult))
                run.settle()
                run(V.tensor_reduce(nstat[:, 0, 0:n], work[:, 0:n * DH].rearrange("p (a d) -> p a d", d=DH), AX_X, ALU.add),
                    heads_squared.by(l, j))
                v, y, t_ = nstat[:, 0, 0:n], nstat[:, 2, 0:n], nstat[:, 3, 0:n]
                dve.wait_ge(*heads_guess.at(l, j))
                run(V.tensor_scalar(v, v, 1.0 / DH, EPS, ALU.mult, ALU.add))
                run.settle()
                newton(v, y, t_)
                run(V.tensor_tensor(y, y, t_, ALU.mult))
                run.settle()
                for t in range(tiles):
                    r = y[:, t * heads:(t + 1) * heads].unsqueeze(2).to_broadcast([P, heads, DH])
                    run(V.tensor_tensor(x3[:, t], x3[:, t], r, ALU.mult))
                run.settle()
                gb = head_gain[:, g, :].unsqueeze(1).to_broadcast([P, heads, DH])
                for t in range(tiles):
                    run(V.tensor_tensor(x3[:, t], x3[:, t], gb, ALU.mult))
                run.settle()
                if rope:
                    hd = DH // 2
                    for t in range(TILES):
                        x0, x1 = x3[:, t, :, 0:DH:2], x3[:, t, :, 1:DH:2]
                        cos = rope_b[:, t, 0:hd].unsqueeze(1).to_broadcast([P, heads, hd])
                        sin = rope_b[:, t, hd:DH].unsqueeze(1).to_broadcast([P, heads, hd])
                        r = [work[:, (4 * t + m) * 256:(4 * t + m) * 256 + heads * hd].rearrange("p (h d) -> p h d", h=heads)
                             for m in range(4)]
                        run(V.tensor_tensor(r[0], x0, cos, ALU.mult))
                        run(V.tensor_tensor(r[1], x1, sin, ALU.mult))
                        run(V.tensor_tensor(r[2], x0, sin, ALU.mult))
                        run(V.tensor_tensor(r[3], x1, cos, ALU.mult))
                        run.settle()
                        run(V.tensor_tensor(x0, r[0], r[1], ALU.subtract))
                        run(V.tensor_tensor(x1, r[2], r[3], ALU.add))
                    run.settle()
                if dup is not None:
                    for half in range(2):
                        ins = V.tensor_copy(dup.rearrange("p t h (a d) -> p t h a d", a=2)[:, :, :, half, :], x3)
                        run(ins, heads_ready.by(l, j) if half else None)
                else:
                    run(V.tensor_copy(small[:, 3:4], small[:, 3:4]), heads_ready.by(l, j))
                run.settle()

            def silu_finish(l, key):
                c = key[2] - HY_CH
                n, dst = (N4, (ag, hg)) if l == 0 else (SEQ, (wgT, ngT))
                g = dst[c // 4][:, c % 4, :]
                dve.wait_ge(*silu_exp.at(l, c))
                run(V.tensor_scalar(g, g, 1.0, None, ALU.add))
                run.settle()
                run(V.reciprocal(g, g))
                run.settle()
                run(V.tensor_tensor(g, g, bank(*key)[:, 0:n], ALU.mult), emptied(*key))

            def take_features(l, key):
                c = key[2]
                if l or c >= HY_CH:
                    return silu_finish(l, key)
                dve.wait_ge(*conv_begun.at(c))
                b = bank(*key)[:, :].rearrange("p (s n) -> p s n", s=2)
                u = uc[:, c, :].rearrange("p (s n) -> p s n", s=2)
                for s in range(2):
                    run(V.scalar_tensor_tensor(out=u[:, s, 1:SEQ], in0=b[:, s, 0:SEQ - 1], scalar=conv_w[:, 0, c:c + 1],
                                               in1=u[:, s, 1:SEQ], op0=ALU.mult, op1=ALU.add))
                run.settle()
                for s in range(2):
                    run(V.scalar_tensor_tensor(out=u[:, s, 0:SEQ - 1], in0=b[:, s, 1:SEQ], scalar=conv_w[:, 2, c:c + 1],
                                               in1=u[:, s, 0:SEQ - 1], op0=ALU.mult, op1=ALU.add), emptied(*key) if s else None)

            def attention2(l):
                U = units_of_block2(l)
                for u in range(len(U) + 1):
                    if u >= 1:
                        for key in ended_in[(2 + l, u - 1)]:
                            take_features(l, key)
                    if u < len(U):
                        kind, h, t = U[u]
                        st = stat[:, u % 2, :, :]
                        n = SEQ if kind == "G" and t >= TILES else N4
                        b = bank("s", 2 + l, u)
                        dve.wait_ge(*filled("s", 2 + l, u))
                        if kind == "G":
                            run(V.tensor_reduce(st[:, 0, 0:1], b[:, 0:n], AX_X, ALU.max))
                            run.settle()
                            run(V.tensor_scalar(st[:, 1, 0:1], st[:, 0, 0:1], -SCALE, None, ALU.mult), bias_ready.by(2 + l, u))
                        else:
                            if u >= 2:
                                dve.wait_ge(*filled("p", 2 + l, u - 2, 0))
                            m = mask_w[:, t, :] if kind == "W" else rel_bias[:, t, h, :]
                            run(V.scalar_tensor_tensor(out=S[:, u % 2, 0:SEQ], in0=b[:, 0:SEQ], scalar=SCALE, in1=m,
                                                       op0=ALU.mult, op1=ALU.add))
                            run(V.tensor_scalar(S[:, u % 2, SEQ:N4], b[:, SEQ:N4], SCALE, None, ALU.mult), emptied("s", 2 + l, u))
                            run.settle()
                            run(V.tensor_reduce(st[:, 0, 0:1], S[:, u % 2, 0:N4], AX_X, ALU.max))
                            run.settle()
                            if kind == "W":
                                run(V.tensor_tensor(st[:, 0, 0:1], st[:, 0, 0:1], sink[:, h:h + 1], ALU.max))
                                run.settle()
                            run(V.tensor_scalar(st[:, 1, 0:1], st[:, 0, 0:1], -1.0, None, ALU.mult), bias_ready.by(2 + l, u))
                    if u < len(U):
                        dve.wait_ge(*probs_ready.at(2 + l, u))
                        total = st[:, 2, 0:1]
                        if kind == "W":
                            run(V.tensor_tensor(total, total, st[:, 3, 1:2], ALU.add))
                            run.settle()
                        run(V.reciprocal(st[:, 2, 1:2], total))
                        run.settle()
                        if kind == "G":
                            signal = emptied("s", 2 + l, u)
                            run(V.tensor_scalar(S[:, u % 2, 0:n], S[:, u % 2, 0:n], st[:, 2, 1:2], None, ALU.mult), signal)
                            run.settle()
                            run(V.tensor_copy(small[:, 4:5], small[:, 4:5]), probs_scaled.by(2 + l, u))
                        else:
                            run(V.tensor_scalar(S[:, u % 2, 0:n], S[:, u % 2, 0:n], st[:, 2, 1:2], None, ALU.mult),
                                probs_scaled.by(2 + l, u))
                for key in ended_in[(2 + l, len(U))]:
                    take_features(l, key)
                run.settle()
                for b in range(len(U)):
                    dve.wait_ge(*emptied("o", 2 + l, b))

            def add_gated(l, n, tiles):
                for c in range(2):
                    for t in tiles:
                        key = ("out2", l, c, t)
                        cols = slice(c * 512, (c + 1) * 512)
                        dve.wait_ge(*filled(*key))
                        w = work[:, t * 512:(t + 1) * 512]
                        run(V.tensor_tensor(w, bank(*key)[:, :], gate_b[:, t // 2, cols], ALU.mult), emptied(*key))
                        run.settle()
                        run(V.tensor_tensor(X[:, t, cols], X[:, t, cols], w, ALU.add),
                            x_added.by(n) if c and t == tiles[-1] else None)

            run(V.memset(small[:, 3:5], 0.0))
            modulation(0, ada_row, ada_bias)
            norm_finish(5, T4, xn2)
            modulated_evacuate(5)
            heads_norm(0, 0, q2, T4, QH, 0, True, None, [("in2", 0, 0, t) for t in range(T4)])
            heads_norm(0, 1, kv2[:, :, 0:KVH * DH], T4, KVH, 1, True, k2d, [("in2", 0, 1, t) for t in range(T4)])
            for key in ended_in[(2, "before")]:
                take_features(0, key)
            attention2(0)
            run(V.tensor_tensor(oT2, oT2, ag, ALU.mult))
            run(V.tensor_tensor(uc[:, 8:12, :], uc[:, 8:12, :], hg, ALU.mult), silu_used.by(0))
            run.settle()

            dve.wait_ge(filter_loaded, FILTERS * 16)
            for n in range(2):
                a, k = hidden[0:HID, n, :], work[0:HID, 0:SEQ]
                dve.wait_ge(*filled("f", n))
                run(V.tensor_scalar(a, bank("f", n)[0:HID, 0:SEQ], hid[:, n:n + 1], hid[:, 2:3], ALU.add, ALU.mult), emptied("f", n))
                run.settle()
                run(V.tensor_scalar(k, a, 1.0 / TWO_PI, ROUND, ALU.mult, ALU.add))
                run.settle()
                run(V.tensor_scalar(k, k, ROUND, None, ALU.subtract))
                run.settle()
                run(V.scalar_tensor_tensor(out=a, in0=k, scalar=-TWO_PI_HI, in1=a, op0=ALU.mult, op1=ALU.add))
                run.settle()
                run(V.scalar_tensor_tensor(out=a, in0=k, scalar=-TWO_PI_LO, in1=a, op0=ALU.mult, op1=ALU.add))
                run.settle()
                run(V.tensor_scalar(a, a, PI_IN, -PI_IN, ALU.min, ALU.max), sin_in_range.by(n))
                run.settle()
            sq = work.rearrange("p (a n) -> p a n", a=4)
            for od in range(2):
                for d in range(2):
                    for t in range(TILES):
                        dve.wait_ge(*filled("tap", od, d, t))
                        run(V.tensor_tensor(taps[:, d, t, :], bank("tap", od, d, t)[:, :], decay[:, t, :], ALU.mult), emptied("tap", od, d, t))
                run.settle()
                run(V.memset(taps[0:1, 1, 0, :], 0.0))
                run.settle()
                if od:
                    dve.wait_ge(*filled("energy", 0))
                    dve.wait_ge(*filled("nyq", 0))
                for d in range(2):
                    for t in range(TILES):
                        run(V.tensor_tensor(sq[:, 2 * d + t, :], taps[:, d, t, :], taps[:, d, t, :], ALU.mult),
                            taps_squared.by(od) if d and t else None)
                run(V.tensor_tensor(taps_sd[:, 0], taps[:, 0], taps[:, 1], ALU.add))
                run(V.tensor_tensor(taps_sd[:, 1], taps[:, 0], taps[:, 1], ALU.subtract), taps_mixed.by(od))
                dve.wait_ge(*taps_guess.at(od))
                v, y, t_ = rn[:, 1, :], rn[:, 0, :], taps[:, 0, 0, :]
                run.settle()
                run(V.tensor_scalar(v, bank("energy", od)[:, :], EPS, None, ALU.add), emptied("energy", od))
                run.settle()
                newton(v, y, t_)
                run(V.tensor_tensor(y, y, t_, ALU.mult))
                run.settle()
                for m in range(2):
                    dve.wait_ge(*filled("spec", od, m, 0))
                    run(V.tensor_tensor(spec_a[:, od, m, :], bank("spec", od, m, 0)[:, :], y, ALU.mult), emptied("spec", od, m, 0))
                    dve.wait_ge(*filled("spec", od, m, 1))
                    run(V.tensor_tensor(spec_b[:, od, m, :], bank("spec", od, m, 1)[:, :], y, ALU.mult), emptied("spec", od, m, 1))
                    run.settle()
                    run(V.tensor_tensor(spec_a[:, od, m, :], spec_a[:, od, m, :], skip_b[:, od, :], ALU.add))
                run(V.memset(spec_b[0:1, od, 0, :], 0.0))
                dve.wait_ge(*filled("nyq", od))
                run(V.tensor_tensor(spec_c[0:1, od, :], bank("nyq", od)[0:1, :], y[0:1, :], ALU.mult), emptied("nyq", od))
                run.settle()
                run(V.tensor_tensor(spec_c[0:1, od, :], spec_c[0:1, od, :], skip_b[0:1, od, :], ALU.add), spectra_ready.by(od))
                run.settle()
            for c in range(0, 8, 2):
                dst = (Z, G1)[c // 4][:, :, c % 4 * P:(c % 4 + 1) * P]
                dve.wait_ge(*filled("zg", c))
                run(V.tensor_copy(dst, bank("zg", c)[:, :].rearrange("p (t n) -> p t n", t=T4)), emptied("zg", c))

            for od in range(2):
                for s in range(2):
                    y = spectrum(s)
                    if od:
                        for n in range(2):
                            dve.wait_ge(*filled("z1", s, n))
                    for m in range(2):
                        zr, zi = bank("zf", od, s, m, 0), bank("zf", od, s, m, 1)
                        a, b = spec_a[:, od, m, :], spec_b[:, od, m, :]
                        re, im = y[:, m, :], y[:, 2 + m, :]
                        t0, t1 = spec_tmp[:, 0, :], spec_tmp[:, 1, :]
                        dve.wait_ge(*filled("zf", od, s, m, 0))
                        dve.wait_ge(*filled("zf", od, s, m, 1))
                        run(V.tensor_tensor(re, zr[:, :], a, ALU.mult))
                        run(V.tensor_tensor(im, zr[:, :], b, ALU.mult), emptied("zf", od, s, m, 0))
                        run(V.tensor_tensor(t0, zi[:, :], b, ALU.mult))
                        run(V.tensor_tensor(t1, zi[:, :], a, ALU.mult))
                        run.settle()
                        run(V.tensor_tensor(re, re, t0, ALU.subtract))
                        run(V.tensor_tensor(im, im, t1, ALU.add))
                        run.settle()
                        if m == 0:
                            run(V.tensor_tensor(im[0:1, :], zi[0:1, :], spec_c[0:1, od, :], ALU.mult), emptied("zf", od, s, m, 1))
                            run.settle()
                        else:
                            run(V.tensor_copy(small[:, 5:6], zi[:, 0:1]), emptied("zf", od, s, m, 1))
                            run.settle()
                    run(V.tensor_copy(small[:, 5:6], small[:, 4:5]), spectrum_ready.by(od, s))
                for s in range(2):
                    if od == 0:
                        for t in range(TILES):
                            dve.wait_ge(*filled("z1", s, t))
                            run(V.tensor_tensor(Z[:, 2 * s + t, :], bank("z1", s, t)[:, :], G1[:, 2 * s + t, :], ALU.mult), emptied("z1", s, t))
                    else:
                        for c2 in range(2):
                            cols = slice(s * SEQ, (s + 1) * SEQ)
                            dve.wait_ge(*filled("y2", s, c2))
                            run(V.tensor_tensor(yTh[:, 2 * c2:2 * c2 + 2, cols], bank("y2", s, c2)[:, :].rearrange("p (a n) -> p a n", a=2),
                                                uc[:, 8 + 2 * c2:10 + 2 * c2, cols], ALU.mult), emptied("y2", s, c2))
            run(V.tensor_copy(small[:, 5:6], small[:, 4:5]), gated_ready.by(0))
            add_gated(0, 5, list(range(T4)))
            run.settle()

            modulation(1, ada_row3, ada_bias3)
            norm_finish(6, T4, xn3)
            modulated_evacuate(6)
            heads_norm(1, 0, wq, TILES, QH, 2, True, None, [("in2", 1, 0, t) for t in range(TILES)])
            heads_norm(1, 1, kv3[:, :, 0:KVH * DH], T4, KVH, 3, True, k3d, [("in2", 1, 1, t) for t in range(T4)])
            heads_norm(1, 2, nq, TILES, QH, 4, False, None, [("in2", 1, 2, t) for t in range(TILES)])
            heads_norm(1, 3, nk, T4, QH, 5, False, None, [("in2", 1, 3, t) for t in range(T4)])
            dve.wait_ge(bias_loaded, BIASES * 16)
            dve.wait_ge(bias_masked, 1)
            attention2(1)
            run(V.tensor_tensor(oT3, oT3, wgT, ALU.mult))
            run(V.tensor_tensor(yT3, yT3, ngT, ALU.mult), gated_ready.by(1))
            add_gated(1, 6, [0, 1])

        @block.gpsimd
        def _(pool):
            run = Steps(pool, pool_step)
            G = nc.gpsimd
            n = QH * REL_R
            run(G.memset(rel_pad[0:n, :], 0.0))
            run.settle()
            pool.dma_start(rel_pad[0:n, GRID_W - NA_COLS:GRID_W - NA_COLS + REL_C],
                           A["nat_rpb_2"][0].rearrange("h r c -> (h r) c")).then_inc(rel_loaded, 16)
            pool.wait_ge(rel_loaded, 16)
            for c in range(GRID_W):
                run(G.tensor_copy(rel_toep[0:n, c, :], rel_pad[0:n, GRID_W - 1 - c:2 * GRID_W - 1 - c]))
            run.settle()
            pool.dma_start(rel_rows.rearrange("c n k -> n c k"), rel_toep[0:n, :, :]).then_inc(rel_stored, 16)
            pool.wait_ge(rel_stored, 16)
            pool.wait_ge(*merged_ready.at(1))
            pool.dma_start(final_g, A["norm_final"].partition_broadcast(P)).then_inc(final_g_loaded, 16)
            pool.dma_start(fourier.rearrange("p a b n -> p (a b n)"), C["fourier"]).then_inc(late_loaded, 16)
            pool.dma_start(ada_bias[0:2, :], A["b_ada_2"][0].partition_broadcast(2)).then_inc(late_loaded, 16)
            pool.wait_ge(*silu_used.at(0))
            for u in range(len(units_of_block2(0))):
                pool.wait_ge(*filled("o", 2, u))
            w3v = A["hy_w3_2"][0].rearrange("k (o d n) -> k o d n", o=2, d=2)
            for dst, src in ((w3[0:HID, :, :, :].rearrange("k o d n -> k (o d n)"), A["hy_w3_2"][0]),
                             (skip_b.rearrange("p o n -> p (o n)"), A["hy_skip_2"][0].rearrange("o n -> (o n)").partition_broadcast(P)),
                             (decay.rearrange("p t n -> p (t n)"), C["decay"]),
                             (positions, C["positions"]), (hyena_w1, A["hy_w1_2"][0]), (hyena_w2, A["hy_w2_2"][0])):
                pool.dma_start(dst, src).then_inc(filter_loaded, 16)
            pool.wait_ge(*filled("zg", 7))
            pool.dma_start(ada_bias3[0:2, :], A["b_ada_2"][1].partition_broadcast(2)).then_inc(ada_bias_loaded, 16)
            pool.wait_ge(*filled("hT", 6, 7))
            for r in range(ROWS):
                part = slice(r % 2 * GRID_W, (r % 2 + 1) * GRID_W)
                src = rel_rows.rearrange("c (h r) k -> c h r k", h=QH)[:, :, NA_ROWS - 1 - r:NA_ROWS - 1 - r + ROWS, :]
                pool.dma_start(rel_bias[part, r // 2, :, :], src.rearrange("c h r k -> c h (r k)")).then_inc(bias_loaded, 16)
            pool.dma_start(mask_w.rearrange("p t n -> p (t n)"), C["mask_w"]).then_inc(bias_loaded, 16)
            pool.dma_start(mask_n, C["mask_n"]).then_inc(bias_loaded, 16)
            pool.wait_ge(bias_loaded, BIASES * 16)
            for t in range(TILES):
                for h in range(QH):
                    b = rel_bias[:, t, h, :].rearrange("p (r c) -> p r c", r=ROWS)
                    ins = G.tensor_tensor(b, b, mask_n.unsqueeze(1).to_broadcast([P, ROWS, GRID_W]), ALU.add)
            ins.then_inc(bias_masked, 1)

        @block.sync
        def _(sp):
            x_rows = A["x"][0].rearrange("(t p) n -> p t n", p=P)
            sp.dma_start(X[:, 0:TILES, :], x_rows).then_inc(x_loaded, 16)
            loads = [(ident[:, :], C["ident"]), (tri, C["tri"]), (rope_a[:, :, :].rearrange("p t n -> p (t n)"), C["rope_a"]),
                     (mask_a.rearrange("p g n -> p (g n)"), C["mask_a"]), (mask_b, C["mask_b"]),
                     (mask_c.rearrange("p a n -> p (a n)"), C["mask_c"]),
                     (rope_b[:, :, :].rearrange("p t n -> p (t n)"), C["rope_b"]),
                     (select[:, :, :].rearrange("p t n -> p (t n)"), C["select"]),
                     (sink[:, :], A["win_sink_2"][0].partition_broadcast(P))]
            for n, name in enumerate(("norm_mix", "norm_mlp", "norm_g_2")):
                for l in range(LAYERS):
                    loads.append((g_cols[:, n, l, :], A[name][l].rearrange("(k p) -> p k", p=P)))
            loads.append((cond[:, :, 0], A["c_2"][0].rearrange("(k p) -> p k", p=P)))
            loads.append((cond[:, :, 1], A["c_ctx_2"].rearrange("(k p) -> p k", p=P)))
            for n, name in enumerate(("glob_q", "glob_k", "win_q", "win_k", "nat_q", "nat_k")):
                loads.append((head_gain[:, n, :], A[name + "_norm_2"][0].partition_broadcast(P)))
            for n in range(3):
                loads.append((conv_w[:, n, :], A["hy_conv_w_2"][0, n].rearrange("(c p) -> p c", p=P)))
            loads.append((conv_w[:, 3, :], A["hy_conv_b_2"][0].rearrange("(c p) -> p c", p=P)))
            for n, name in enumerate(("hy_b1_2", "hy_b2_2", "hy_freq_2")):
                loads.append((hid[:, n:n + 1], A[name].rearrange("a n -> n a")))
            assert len(loads) == CONSTS, len(loads)
            with nc.allow_non_contiguous_dma("small vectors, once"):
                for dst, src in loads:
                    sp.dma_start(dst, src).then_inc(consts_loaded, 16)
            sp.dma_start(X[:, TILES:T4, :], A["ctx_2"][0].rearrange("(t p) n -> p t n", p=P)).then_inc(x_loaded, 16)
            rows = lambda w: w.rearrange("(k p) n -> p k n", p=P)
            for n, key in enumerate(SLABS):
                name, l, c = key
                s = n % SLOTS
                if n >= SLOTS:
                    sp.wait_ge(*last_use[n - SLOTS])
                dst = slabs[:, s, :].rearrange("p (k n) -> p k n", k=KD)
                cols = slice(c * 512, (c + 1) * 512)
                if name == "out":
                    for w, k0, k1 in (("w_out_a", 0, 2), ("w_out_b", 2, 5), ("w_out_c", 5, 8)):
                        sp.dma_start(dst[:, k0:k1, :], rows(A[w][l, :, cols])).then_inc(slab_loaded[s], 16)
                    continue
                if name == "down":
                    dst, src = slabs[:, s, :].rearrange("p (k n) -> p k n", k=4), rows(A["w_down"][l, cols, :])
                elif name == "in2":
                    a, b = IN2[c]
                    dst, src = dst[:, :, 0:b - a], rows(A["w_in_2"][l, :, a:b])
                else:
                    w = {"in": "w_in", "o": "w_o", "up": "w_up", "ada": "w_ada_2", "out2": "w_out_2"}[name]
                    src = rows(A[w][l, :, cols])
                sp.dma_start(dst, src).then_inc(slab_loaded[s], 16)
            sp.wait_ge(*x_added.at(6))
            sp.dma_start(out.rearrange("(t p) n -> p t n", p=P), X[:, 0:TILES, :]).then_inc(out_stored, 16)
            sp.wait_ge(out_stored, 16)


INPUTS = ["x", "norm_mix", "w_in", "w_out_a", "w_out_b", "w_out_c", "w_o", "norm_mlp", "w_up", "w_down", "norm_final",
          "c_2", "ctx_2", "c_ctx_2", "norm_g_2", "w_ada_2", "b_ada_2", "w_in_2", "w_out_2", "glob_q_norm_2",
          "glob_k_norm_2", "hy_conv_w_2", "hy_conv_b_2", "hy_w1_2", "hy_b1_2", "hy_w2_2", "hy_b2_2", "hy_freq_2",
          "hy_w3_2", "hy_skip_2", "win_q_norm_2", "win_k_norm_2", "win_sink_2", "nat_q_norm_2", "nat_k_norm_2",
          "nat_rpb_2"]


def kernel(**inputs):
    import concourse.bacc as bacc
    from concourse.bass_utils import run_bass_kernel_spmd

    nc = bacc.Bacc("TRN2", target_bir_lowering=False, num_devices=1)
    arrays, A, C = {}, {}, {}
    for name in INPUTS:
        arrays["in_" + name] = np.ascontiguousarray(inputs[name])
        A[name] = nc.dram_tensor("in_" + name, arrays["in_" + name].shape, F32, kind="ExternalInput").ap()
    for name, a in constants().items():
        arrays["const_" + name] = a
        C[name] = nc.dram_tensor("const_" + name, a.shape, F32, kind="ExternalInput").ap()
    out = nc.dram_tensor("out_dram", (SEQ, D), F32, kind="ExternalOutput").ap()
    two_blocks(nc, A, C, out)
    r = run_bass_kernel_spmd(nc, [arrays], core_ids=[0])
    return np.asarray(r.results[0]["out_dram"]).reshape(1, SEQ, D)
```

```python
import math
from contextlib import ExitStack

import numpy as np

import concourse.bass as bass
from concourse import mybir

F32 = mybir.dt.float32
F32R = mybir.dt.float32r
ACT = mybir.ActivationFunctionType
ALU = mybir.AluOpType
AX_X = mybir.AxisListType.X

P = 128
SEQ = 256
D = 1024
KD = D // P
TILES = SEQ // P
DH = 64
SCALE = DH ** -0.5
EPS = 1e-6
NEG = -1e30
LAYERS = 2
HEADS = 24
MIX = HEADS * DH
ROT = 18
ROPE = 16
N_A, N_B, N_C = 4, 6, 6
GROUPS_A = ((128, 1), (512, 4), (2048, 16))
G_A = len(GROUPS_A)
FF = 4096
CTX = 256
T4 = (SEQ + CTX) // P
N4 = T4 * P
QH = 8
KVH = 2
GW = QH * DH
IN2 = [(0, 512), (512, 768), (768, 1280), (1280, 1792), (1792, 2304), (2304, 2816), (2816, 3328)]
HY = 512
HY_CH = 3 * HY // P
HID, EMB = 64, 33
NA_ROWS, NA_COLS, GRID_W = 8, 16, 64
ROWS = SEQ // GRID_W
REL_R, REL_C = 2 * NA_ROWS - 1, 2 * NA_COLS - 1
TWO_PI = 2.0 * math.pi
TWO_PI_HI = float(np.float32(6.28125))
TWO_PI_LO = float(np.float32(TWO_PI - 6.28125))
ROUND = 1.5 * 2.0 ** 23
PI_IN = float(np.nextafter(np.float32(math.pi), np.float32(0)))

HALF, QUARTER = 2048, 1024
SLOTS = 4
SPLITS = 4
BANKS = 8
ANY_BANK = tuple(range(BANKS))
ATTENTION_BANKS = (0, 1, 2, 3, 4)
GATE_BANKS = (5, 6, 7)
CONSTS = 9 + 6 + 2 + 6 + 4 + 3
LATE0, FILTERS, BIASES = 2, 7, ROWS + 2


def constants():
    f = np.float32
    i = np.arange(P)
    c = {"ident": np.eye(P, dtype=f)}
    c["tri"] = (i[:, None] >= i[None, :]).astype(f)
    off = i[:, None] + P - i[None, :]
    on = i[:, None] - i[None, :]
    mask_a = np.zeros((P, G_A, 2, P), f)
    for g, (w, d) in enumerate(GROUPS_A):
        for b, dist in enumerate((off, on)):
            ok = (dist >= 0) & (dist <= w) & (dist % d == 0)
            mask_a[:, g, b] = np.where(ok, 0, NEG)
    c["mask_a"] = mask_a.reshape(P, -1)
    causal = np.where(on >= 0, 0, NEG)
    c["mask_b"] = np.concatenate([np.zeros((P, P)), causal], 1).astype(f)
    strict = np.where(i[None, :] > i[:, None], 0, NEG)
    c["mask_c"] = np.concatenate([strict, np.zeros((P, P)), strict], 1).astype(f)
    pos = np.arange(SEQ, dtype=f)
    inv = np.exp(f(-math.log(500000.0)) * np.arange(0, ROPE, 2, dtype=f) / f(ROPE)).astype(f)
    ang = (pos[:, None] * inv).astype(f).astype(np.float64)
    table = np.concatenate([np.cos(ang), np.sin(ang)], 1).astype(f)
    c["rope_a"] = np.concatenate([table[:P], table[P:]], 1)
    row, col = (np.arange(SEQ) // GRID_W).astype(f), (np.arange(SEQ) % GRID_W).astype(f)
    inv = (f(10000.0) ** (-np.arange(16, dtype=f) / f(16))).astype(f)
    ang = np.concatenate([row[:, None] * inv, col[:, None] * inv], 1).astype(f).astype(np.float64)
    table = np.concatenate([np.cos(ang), np.sin(ang)], 1).astype(f)
    c["rope_b"] = np.concatenate([table[:P], table[P:]], 1)
    sel = np.zeros((2, 2, P), f)
    sel[0, 0] = sel[1, 1] = 1
    c["select"] = sel.reshape(2, -1)
    near0 = np.where(i[None, :] <= i[:, None], 0, NEG)
    near1 = np.where(i[:, None] <= i[None, :], 0, NEG)
    z = np.zeros((P, P))
    c["mask_w"] = np.concatenate([z, near0, near1, z], 1).astype(f)
    gc = i % GRID_W
    c0 = np.clip(gc - NA_COLS // 2, 0, GRID_W - NA_COLS)
    k = np.arange(GRID_W)
    c["mask_n"] = np.where((k >= c0[:, None]) & (k < c0[:, None] + NA_COLS), 0, NEG).astype(f)
    t = np.arange(SEQ)
    theta = TWO_PI * ((t[:, None] * t[None, :]) % (2 * SEQ)) / (2 * SEQ)
    alt = np.where(t % 2, -1.0, 1.0)
    fc, fs = np.cos(theta), -np.sin(theta)
    fs[:, 0] = alt
    gcos, gsin = 2 * np.cos(theta) / (2 * SEQ), -2 * np.sin(theta) / (2 * SEQ)
    gcos[0] /= 2
    gsin[0] = alt / (2 * SEQ)
    c["fourier"] = np.concatenate([m[h * P:(h + 1) * P] for m in (fc, fs, gcos, gsin) for h in (0, 1)], 1).astype(f)
    tt = np.linspace(0.0, 1.0, SEQ, dtype=f)[:, None]
    bands = (EMB - 1) // 2
    w = (f(TWO_PI) * np.arange(SEQ, dtype=f)[:, None] / f(SEQ)).astype(f)
    fr = np.linspace(1e-4, bands - 1, bands, dtype=f)[None]
    a = (fr * w).astype(f).astype(np.float64)
    c["positions"] = np.ascontiguousarray(np.concatenate([tt, np.cos(a), -np.sin(a)], 1).astype(f).T)
    deltas = np.linspace(math.log(1e-2) / 1.5, math.log(1e-2) / 0.3, HY, dtype=f)
    decay = np.exp((-tt * np.abs(deltas)).astype(f)).astype(f)
    c["decay"] = np.concatenate([decay[:P], decay[P:]], 1)
    return {n: np.ascontiguousarray(a.astype(f)) for n, a in c.items()}


def units_of_block1():
    soft = [("A", s, t) for s in range(N_A) for t in range(TILES)]
    soft += [("B", b, t) for b in range(N_B) for t in range(TILES)]
    return soft + [("C", c, 0) for c in range(N_C)]


def units_of_block2(layer):
    if layer == 0:
        return [("G", h, t) for h in range(QH) for t in range(T4)]
    return [(k, h, t) for k in ("W", "N") for h in range(QH) for t in range(TILES)]


def half_list():
    slabs = []
    for l in range(LAYERS):
        slabs += [("in", l, c) for c in range(15)]
        slabs += [("out", l, c) for c in range(2)] + [("o", l, c) for c in range(2)]
        slabs += [("up", l, c) for c in range(8)] + [("down", l, c) for c in range(8)]
    for l in range(LAYERS):
        slabs += [("ada", l, c) for c in range(6)] + [("in2", l, c) for c in range(7)]
        slabs += [("out2", l, c) for c in range(2)]
    return [s + (h,) for s in slabs for h in range(2)]


def by_features(key):
    return key[0] == "up" or (key[0] == "in2" and key[2] >= (2 if key[1] == 0 else 5))


class Signal:

    def __init__(self, sem, keys):
        self.sem = sem
        self.value = {k: n + 1 for n, k in enumerate(keys)}
        self.count = 0

    def at(self, *key):
        return self.sem, self.value[key]

    def by(self, *key):
        self.count += 1
        assert self.value[key] == self.count, (self.sem, key)
        return self.sem, self.count


class Steps:

    def __init__(self, eng, sem):
        self.eng, self.sem, self.n, self.last = eng, sem, 0, None

    def __call__(self, instruction, signal=None):
        if signal is None:
            self.n += 1
            signal = (self.sem, self.n)
        instruction.then_inc(signal[0], 1)
        self.last = signal

    def settle(self):
        self.eng.wait_ge(*self.last)


def two_blocks(nc, A, C, out):
    ctx = ExitStack()
    with ctx:
        def sb(name, shape):
            return ctx.enter_context(nc.sbuf_tensor(name, shape, F32))

        def sem(name):
            return ctx.enter_context(nc.semaphore(name))

        raw = sb("raw", [P, SLOTS, HALF])
        w_high = ctx.enter_context(nc.sbuf_tensor("w_high", [P, SPLITS, QUARTER], F32R))
        w_low = ctx.enter_context(nc.sbuf_tensor("w_low", [P, SPLITS, QUARTER], F32R))
        X = sb("X", [P, T4, D])
        ident = sb("ident", [P, P])
        ones = sb("ones", [P, P])
        rope_a = sb("rope_a", [P, TILES, ROPE])
        g_cols = sb("g_cols", [P, 3, LAYERS, KD])
        stat = sb("stat", [P, 2, 4, 8])
        nstat = sb("nstat", [P, 4, 64])
        small = sb("small", [P, 64])
        rope_b = sb("rope_b", [P, TILES, DH])
        select = sb("select", [2, 2, P])
        eps_col = sb("eps_col", [P, 2])
        ada_t = sb("ada_t", [P, 16, 2])
        gain = sb("gain", [P, KD, 2])
        cond = sb("cond", [P, KD, 2])
        cond_e = sb("cond_e", [P, KD, 2])
        sink = sb("sink", [P, QH])
        head_gain = sb("head_gain", [P, 6, DH])
        conv_w = sb("conv_w", [P, 4, HY_CH])
        hid = sb("hid", [HID, 8])
        arena_cols = 31000
        arena_at = (nc.sbuf_base + 31) // 32 * 32
        arena = sb("arena", [P, arena_cols])
        scores_cols, acts_cols = 4 * 768, 4 * KD * SEQ
        acts_r = nc.alloc_sbuf_tensor_at("acts_r", [P, acts_cols], F32R, offset=arena_at + 4 * scores_cols)
        hidden_r = nc.alloc_sbuf_tensor_at("hidden_r", [P, 2 * FF // P * SEQ], F32R,
                                           offset=arena_at + 4 * (scores_cols + acts_cols))
        rel_rows = nc.dram_tensor("rel_rows", (GRID_W, QH * REL_R, GRID_W), F32, kind="Internal").ap()

        def carve(at, *shape, of=arena, start=0):
            n = int(np.prod(shape))
            assert at[0] + n <= arena_cols, (at[0] + n)
            v = of[:, at[0] - start:at[0] - start + n]
            at[0] += n
            if len(shape) == 2:
                v = v.rearrange("p (a b) -> p a b", a=shape[0])
            elif len(shape) == 3:
                v = v.rearrange("p (a b c) -> p a b c", a=shape[0], b=shape[1])
            elif len(shape) == 4:
                v = v.rearrange("p (a b c d) -> p a b c d", a=shape[0], b=shape[1], c=shape[2])
            return v

        at = [0]
        S = carve(at, 2, 768)
        PT = carve(at, 2, 768)
        work = arena[:, 0:2048]
        base = at[0]
        hT = carve(at, 2, KD, SEQ, of=acts_r, start=base)
        oT = carve(at, 2, KD, SEQ, of=acts_r, start=base)
        qkv_at = at[0]
        qkv = carve(at, 3, TILES, MIX)
        qT_at = at[0]
        qkT = carve(at, 2, MIX // P, SEQ)
        at = [qkv_at + 2 * FF // P * SEQ]
        mask_a = carve(at, G_A, SEQ)
        mask_b = carve(at, SEQ)
        mask_c = carve(at, 3, P)
        tri = carve(at, P)
        up_tmp = carve([0], 2, 2, 512)
        gates = carve([qkv_at], TILES, 3, D)
        uT = carve([qkv_at], 2, FF // P, SEQ, of=hidden_r, start=qkv_at)
        xn1 = carve([qT_at], TILES, D)
        rope_tmp = carve([qT_at + 4 * D], 4, TILES, ROT, ROPE // 2)
        merged = carve([qT_at + 2 * D], TILES, D)
        gated = carve([qT_at + 4 * D], 2, 512)
        final_g = carve([base + 4 * D], D)
        assert qT_at + 2 * MIX // P * SEQ <= qkv_at + 2 * FF // P * SEQ
        rel_pad = carve([at[0]], 2 * GRID_W)
        rel_toep = carve([qT_at + 2 * D], GRID_W, GRID_W)
        at = [base]
        hT2 = carve(at, 2, KD, N4, of=acts_r, start=base)
        q_at = at[0]
        q2 = carve(at, T4, GW)
        kv2 = carve(at, T4, 2 * KVH * DH)
        k2d = carve(at, T4, KVH, 2 * DH)
        qT2 = carve(at, QH // 2, N4)
        kT2 = carve(at, KVH, N4)
        uc_at = at[0]
        uc = carve(at, HY_CH, N4)
        ag_at = at[0]
        ag = carve(at, 4, N4)
        hg = carve(at, 4, N4)
        gate_row_at = at[0]
        gate_row = carve(at, D)
        fourier_at = at[0]
        fourier_fwd = carve(at, 2, 2, SEQ)
        oT2 = carve([q_at], QH // 2, N4)
        xn2 = carve([uc_at], T4, D)
        mod_tmp = carve([uc_at + 4 * D], 2, N4)
        ada_bias = carve([uc_at + 5 * D], 3 * D)
        ada_row = carve([uc_at + 8 * D], 2 * D)
        at = [base]
        Z = carve(at, T4, HY)
        G1 = carve(at, T4, HY)
        taps = carve([base], 2, 2, HY)
        taps_sd = carve([base + 2048], 2, 2, HY)
        yThr = carve([base], 2, 4, N4, of=acts_r, start=base)
        oT2r = carve([base + 4096], 2, 4, N4, of=acts_r, start=base)
        at = [q_at]
        spec_a = carve(at, 2, 2, HY)
        spec_b = carve(at, 2, 2, HY)
        positions = carve(at, SEQ)[0:EMB, :]
        hyena_w1 = carve(at, HID)[0:EMB, :]
        hyena_w2 = carve(at, HID)[0:HID, :]
        hidden = carve(at, 2, SEQ)
        decay = carve(at, 2, HY)
        fourier_inv = carve(at, 2, 2, SEQ)
        assert at[0] <= q_at + 7 * D
        y_tmp = carve([q_at + 2 * D], 2, N4)
        w3 = carve([ag_at], 2, 2, HY)
        Y1 = carve([ag_at], 4, HY)
        skip_b = carve([ag_at + 2048], 2, HY)
        spec_c = carve([ag_at + 3072], 2, HY)
        Y = carve([0], 4, HY)
        rn = carve([2048], 2, HY)
        spec_tmp = carve([2048], 2, HY)
        gate_b0 = carve([uc_at], 2, D)

        def spectrum(s):
            return (Y, Y1)[s]

        at = [base + 8 * D]
        wq_at = at[0]
        wq = carve(at, TILES, GW)
        nq = carve(at, TILES, GW)
        kv3 = carve(at, T4, 2 * KVH * DH)
        k3d = carve(at, T4, KVH, 2 * DH)
        nk_at = at[0]
        nk = carve(at, T4, GW)
        nv = carve(at, T4, GW)
        wqT = carve(at, QH // 2, SEQ)
        nqT = carve(at, QH // 2, SEQ)
        wkT = carve(at, KVH, N4)
        nkT = carve(at, QH // 2, N4)
        wgT = carve([nk_at], 4, SEQ)
        ngT = carve([nk_at + 1024], 4, SEQ)
        gate_b1 = carve(at, 1, D)
        bias_at = at[0]
        rel_bias = carve(at, TILES, QH, SEQ)
        mask_w = carve(at, TILES, SEQ)
        mask_n = carve(at, GRID_W)
        oT3 = carve([wq_at], 4, SEQ)
        yT3 = carve([wq_at + 1024], 4, SEQ)
        oT3r = carve([base], 2, 4, SEQ, of=acts_r, start=base)
        yT3r = carve([base + 2048], 2, 4, SEQ, of=acts_r, start=base)
        xn3 = carve([bias_at], T4, D)
        mod_tmp3 = carve([wq_at], 2, N4)
        ada_row3 = carve([nk_at], 3 * D)
        ada_bias3 = carve([uc_at + 2 * D], 3 * D)

        banks = [ctx.enter_context(nc.psum_tensor(f"bank{b}", [P, 512], F32)) for b in range(BANKS)]

        bank_filled = [sem(f"bank_filled{b}") for b in range(BANKS)]
        bank_emptied = [sem(f"bank_emptied{b}") for b in range(BANKS)]
        half_loaded = [sem(f"half_loaded{s}") for s in range(SLOTS)]
        high_ready = sem("high_ready")
        split_ready = sem("split_ready")
        quarter_used = sem("quarter_used")
        high_taken = sem("high_taken")
        gates_ready = sem("gates_ready")
        x_loaded = sem("x_loaded")
        consts_loaded = sem("consts_loaded")
        late_loaded = sem("late_loaded")
        final_g_loaded = sem("final_g_loaded")
        filter_loaded = sem("filter_loaded")
        bias_loaded = sem("bias_loaded")
        ada_bias_loaded = sem("ada_bias_loaded")
        rel_loaded = sem("rel_loaded")
        rel_stored = sem("rel_stored")
        out_stored = sem("out_stored")
        vector_step = sem("vector_step")
        scalar_step = sem("scalar_step")
        NORMS = range(7)
        b1u = [(l, u) for l in range(LAYERS) for u in range(len(units_of_block1()))]
        b2u = [(2 + l, u) for l in range(LAYERS) for u in range(len(units_of_block2(l)))]
        kinds = {(l, u): units_of_block1()[u][0] for l, u in b1u}
        kinds |= {(l, u): units_of_block2(l - 2)[u][0] for l, u in b2u}
        softs = [k for k in b1u + b2u if kinds[k] != "C"]
        sticks = [k for k in b1u if kinds[k] == "C"]
        ones_set = sem("ones_set")
        x_added = Signal(sem("x_added"), [(n,) for n in range(8)])
        rstd_ready = Signal(sem("rstd_ready"), [(n,) for n in NORMS])
        xn_by_vector = Signal(sem("xn_by_vector"), [(n,) for n in NORMS if n != 4])
        qk_roped = Signal(sem("qk_roped"), [(l, j) for l in range(LAYERS) for j in range(2)])
        bias_ready = Signal(sem("bias_ready"), softs)
        probs_scaled = Signal(sem("probs_scaled"), softs)
        stick_masked = Signal(sem("stick_masked"), sticks)
        stick_summed = Signal(sem("stick_summed"), sticks)
        merged_ready = Signal(sem("merged_ready"), [(l,) for l in range(LAYERS)])
        heads_squared = Signal(sem("heads_squared"), [(l, j) for l, n in ((0, 2), (1, 4)) for j in range(n)])
        heads_ready = Signal(sem("heads_ready"), [(l, j) for l, n in ((0, 2), (1, 4)) for j in range(n)])
        cond_ready = sem("cond_ready")
        cond_ready_s = Signal(cond_ready, [("sum",), ("done",)])
        ada_ready = Signal(sem("ada_ready"), [(l,) for l in range(LAYERS)])
        gated_ready = Signal(sem("gated_ready"), [(0,), (1,)])
        sin_in_range = Signal(sem("sin_in_range"), [(0,), (1,)])
        taps_squared = Signal(sem("taps_squared"), [(0,), (1,)])
        taps_mixed = Signal(sem("taps_mixed"), [(0,), (1,)])
        stick_argument = Signal(sem("stick_argument"), sticks)
        spectra_ready = Signal(sem("spectra_ready"), [(0,), (1,)])
        silu_used = Signal(sem("silu_used"), [(0,)])
        pool_step = sem("pool_step")
        bias_masked = sem("bias_masked")
        spectrum_ready = Signal(sem("spectrum_ready"), [(o, s) for o in range(2) for s in range(2)])
        rsqrt_guess = Signal(sem("rsqrt_guess"), [(n,) for n in NORMS])
        xn_by_scalar = Signal(sem("xn_by_scalar"), [(n,) for n in NORMS if n != 4])
        probs_ready = Signal(sem("probs_ready"), softs)
        softplus_part = Signal(sem("softplus_part"), sticks)
        stick_weights = Signal(sem("stick_weights"), sticks)
        heads_guess = Signal(sem("heads_guess"), [(l, j) for l, n in ((0, 2), (1, 4)) for j in range(n)])
        cond_exp = Signal(sem("cond_exp"), [(0,)])
        sin_ready = Signal(sem("sin_ready"), [(0,), (1,)])
        taps_guess = Signal(sem("taps_guess"), [(0,), (1,)])
        conv_begun = Signal(sem("conv_begun"), [(c,) for c in range(HY_CH)])
        silu_exp = Signal(sem("silu_exp"), [(l, c) for l in range(LAYERS) for c in range(8)])
        up_ready = Signal(sem("up_ready"), [(l, m) for l in range(LAYERS) for m in range(16)])
        low_ready = Signal(sem("low_ready"), [("o2",), ("y",), ("3",)])
        out_gated = Signal(sem("out_gated"), [("o2",), ("y", 0, 0), ("y", 0, 1), ("y", 1, 0), ("y", 1, 1), ("3",)])
        relu_ready = Signal(sem("relu_ready"), [(l, m) for l in range(LAYERS) for m in range(16)])

        number = {}
        uses = [0] * BANKS
        opened = [-1] * BANKS
        HALVES = half_list()
        half_at = {k: n for n, k in enumerate(HALVES)}
        loads_of = [2 if k[0] == "out" or by_features(k) else 1 for k in HALVES]
        quarters = [k + (q,) for k in HALVES if k[0] != "ada" for q in range(2)]
        quarter_at = {k: n for n, k in enumerate(quarters)}
        last_use = {}
        half_used = {}
        ended_in = {}
        high_done = {}
        position = {}

        def bank(*key):
            return banks[number[key][0]]

        def filled(*key):
            b, n = number[key]
            return bank_filled[b], n + 1

        def emptied(*key):
            b, n = number[key]
            return bank_emptied[b], n + 1

        def half_is_loaded(n):
            return half_loaded[n % SLOTS], 16 * sum(loads_of[m] for m in range(n % SLOTS, n + 1, SLOTS))

        def raw_quarter(n):
            key = quarters[n]
            h, q = half_at[key[:4]], key[4]
            width = 512 if key[0] == "in2" and key[2] == 1 else QUARTER
            return raw[:, h % SLOTS, q * width:(q + 1) * width], w_high[:, n % SPLITS, 0:width], w_low[:, n % SPLITS, 0:width]

        class Splits:

            def __init__(self, one):
                self.one, self.n = one, 0

            def due(self, *key, ahead=0):
                p = position[key] + ahead
                while self.n < len(quarters) and (self.n < SPLITS or position[self.n - SPLITS] <= p):
                    name, l = quarters[self.n][:2]
                    if name == "in2" and position["ada", l, 5] >= p:
                        return
                    self.one(self.n)
                    self.n += 1

        block = ctx.enter_context(nc.Block())

        @block.tensor
        def _(pe):
            mm, tr = nc.tensor.matmul, nc.tensor.transpose

            counts = {"used": 0, "order": 0}

            def open_bank(*key, among=ANY_BANK):
                b = min(among, key=lambda x: opened[x])
                number[key] = (b, uses[b])
                if uses[b]:
                    pe.wait_ge(bank_emptied[b], uses[b])
                uses[b] += 1
                opened[b] = max(opened) + 1
                return banks[b]

            def close_bank(ins, *key):
                ins.then_inc(filled(*key)[0], 1)
                counts["order"] += 1
                position[key] = counts["order"]

            def split(*key):
                n = quarter_at[key]
                pe.wait_ge(split_ready, n + 1)
                return w_high[:, n % SPLITS, :], w_low[:, n % SPLITS, :]

            def end_quarter(key, ins, *group):
                n = quarter_at[key]
                if group:
                    last_use[n] = filled(*group)
                else:
                    ins.then_inc(quarter_used, 1)
                    counts["used"] += 1
                    last_use[n] = (quarter_used, counts["used"])
                counts["order"] += 1
                position[n] = counts["order"]

            def product(o, left, right, start, stop):
                (lh, ll), (rh, rl) = left, right
                mm(o, lh, rh, start=start, stop=False)
                mm(o, lh, rl, start=False, stop=False)
                return mm(o, ll, rh, start=False, stop=stop)

            def tiles_of(x, width=P):
                return lambda k, t: (x[:, 0, k, t * P:(t + 1) * P], x[:, 1, k, t * P:(t + 1) * P])

            def norm_transposes(n, xn, tiles, per_bank):
                pe.wait_ge(*xn_by_vector.at(n))
                pe.wait_ge(*xn_by_scalar.at(n))
                for b in range(KD // per_bank):
                    o = open_bank("hT", n, b)
                    for kk in range(per_bank):
                        k = b * per_bank + kk
                        for t in range(tiles):
                            c = (kk * tiles + t) * P
                            ins = tr(o[:, c:c + P], xn[:, t, k * P:(k + 1) * P], ident[:, :])
                    close_bank(ins, "hT", n, b)

            def tokens_by_features(slab, name, acts, tiles, width=512, among=ANY_BANK, ready=None):
                group = (name,) + slab[1:]
                o = {}
                for k in range(KD):
                    key = slab + (k // 4, k // 2 % 2)
                    if k % 2 == 0:
                        wh, wl = (w.rearrange("p (k n) -> p k n", k=2) for w in (x[:, 0:2 * width] for x in split(*key)))
                    if ready:
                        pe.wait_ge(*ready(k))
                    for t in tiles:
                        if k == 0:
                            o[t] = open_bank(*group, t, among=among)
                        ins = product(o[t][:, 0:width], acts(k, t), (wh[:, k % 2, :], wl[:, k % 2, :]), k == 0, k == KD - 1)
                        if k == KD - 1:
                            close_bank(ins, *group, t)
                            if name == "gate":
                                ended_in[(slab[1], "at")].append(group + (t,))
                        if k % 2 and t == tiles[-1]:
                            end_quarter(key, ins, *(group + (t,) if k == KD - 1 else ()))
                        yield

            def run(steps):
                for _ in steps:
                    pass

            def advance(steps, n):
                for _ in range(n):
                    if next(steps, "end") == "end":
                        return

            pe.wait_ge(consts_loaded, CONSTS * 16)
            pe.wait_ge(ones_set, 1)
            for l in range(LAYERS):
                norm_transposes(2 * l, xn1, TILES, 2)
                turned = [("qT", l, 0, b) for b in range(6)] + [("qT", l, 1, b) for b in range(6)]
                for c in range(9):
                    turned_token = (lambda k: emptied("hT", 2 * l, k // 2)) if c == 0 else None
                    steps = tokens_by_features(("in", l, c), "qkv", tiles_of(hT), range(TILES), ready=turned_token)
                    if c < 6:
                        run(steps)
                        continue
                    for _ in range(4):
                        advance(steps, 4)
                        key = turned.pop(0)
                        j, b = key[2], key[3]
                        pe.wait_ge(*qk_roped.at(l, j))
                        o = open_bank(*key)
                        for m in range(4):
                            ch, tt = 2 * b + m // 2, m % 2
                            ins = tr(o[:, m * P:(m + 1) * P], qkv[:, j, tt, ch * P:(ch + 1) * P], ident[:, :])
                        close_bank(ins, *key)
                for c in range(6, 9):
                    for t in range(TILES):
                        pe.wait_ge(*emptied("qkv", l, c, t))
                for j in range(2):
                    for b in range(6):
                        pe.wait_ge(*emptied("qT", l, j, b))

                def gate_groups():
                    for c in range(9, 15):
                        yield from tokens_by_features(("in", l, c), "gate", tiles_of(hT), range(TILES), among=GATE_BANKS)

                def head(j, h, cols):
                    half = DH * (h % 2)
                    return qkT[half:half + DH, j, h // 2, cols]

                def scores(u):
                    kind, h, t = U[u]
                    q = slice(t * P, (t + 1) * P)
                    if kind == "A":
                        span = (t + 1) * P
                        o = open_bank("s", l, u, among=ATTENTION_BANKS)
                        for g in range(G_A):
                            hd = g * N_A + h
                            if g == 2 and t == 1:
                                close_bank(ins, "s", l, u)
                                o = open_bank("s2", l, u, among=ATTENTION_BANKS)
                            c = g * span if not (g == 2 and t == 1) else 0
                            ins = mm(o[:, c:c + span], head(0, hd, q), head(1, hd, slice(0, span)), start=True, stop=True)
                        close_bank(ins, "s2" if t else "s", l, u)
                    elif kind == "B":
                        o = open_bank("s", l, u, among=ATTENTION_BANKS)
                        hd = 12 + h
                        ins = mm(o[:, 0:(t + 1) * P], head(0, hd, q), head(1, hd, slice(0, (t + 1) * P)), start=True, stop=True)
                        close_bank(ins, "s", l, u)
                    else:
                        hd = ROT + h
                        o = open_bank("s", l, u, among=ATTENTION_BANKS)
                        mm(o[:, 0:SEQ], head(1, hd, slice(0, P)), head(0, hd, slice(0, SEQ)), start=True, stop=True)
                        ins = mm(o[:, SEQ:SEQ + P], head(1, hd, slice(P, SEQ)), head(0, hd, slice(P, SEQ)), start=True, stop=True)
                        close_bank(ins, "s", l, u)

                def second(u):
                    kind, h, t = U[u]
                    if kind == "C":
                        pe.wait_ge(*stick_summed.at(l, u))
                        sp = PT[:, u % 2, 384:768]
                        o = open_bank("p", l, u, 0, among=ATTENTION_BANKS)
                        mm(o[:, 0:SEQ], tri, sp[:, 0:SEQ], start=True, stop=False)
                        mm(o[:, P:SEQ], ones[:, :], sp[:, SEQ:SEQ + P], start=False, stop=True)
                        ins = mm(o[:, SEQ:SEQ + P], tri, sp[:, SEQ:SEQ + P], start=True, stop=True)
                        close_bank(ins, "p", l, u, 0)
                        return
                    pe.wait_ge(*probs_scaled.at(l, u))
                    blocks = (G_A if kind == "A" else 1) * (t + 1)
                    for b0 in range(0, blocks, 4):
                        o = open_bank("p", l, u, b0 // 4, among=ATTENTION_BANKS)
                        for b in range(b0, min(blocks, b0 + 4)):
                            ins = tr(o[:, (b - b0) * P:(b - b0 + 1) * P], S[:, u % 2, b * P:(b + 1) * P], ident[:, :])
                        close_bank(ins, "p", l, u, b0 // 4)

                def values(u):
                    kind, h, t = U[u]
                    v = lambda hd, jt: qkv[:, 2, jt, hd * DH:(hd + 1) * DH]
                    o = None
                    if kind == "C":
                        pe.wait_ge(*stick_weights.at(l, u))
                        o = open_bank("o", l, u, among=ATTENTION_BANKS)
                        a = PT[:, u % 2, 0:384]
                        mm(o[0:DH, 0:SEQ], v(ROT + h, 0), a[:, 0:SEQ], start=True, stop=False)
                        ins = mm(o[0:DH, P:SEQ], v(ROT + h, 1), a[:, SEQ:SEQ + P], start=False, stop=True)
                        close_bank(ins, "o", l, u)
                        return
                    blocks = (G_A if kind == "A" else 1) * (t + 1)
                    for b0 in range(0, blocks, 4):
                        pe.wait_ge(*emptied("p", l, u, b0 // 4))
                    o = open_bank("o", l, u, among=ATTENTION_BANKS)
                    for b in range(blocks):
                        g, jt = b // (t + 1), b % (t + 1)
                        hd = g * N_A + h if kind == "A" else 12 + h
                        ins = mm(o[0:DH, 0:P], v(hd, jt), PT[:, u % 2, b * P:(b + 1) * P], start=b == 0, stop=b == blocks - 1)
                    close_bank(ins, "o", l, u)

                U = units_of_block1()
                filler = gate_groups()
                for u in range(len(U) + 1):
                    ended_in[(l, "at")] = []
                    if u < len(U):
                        scores(u)
                    if u >= 1:
                        second(u - 1)
                    advance(filler, 4 if u < len(U) else 1000)
                    if u >= 1:
                        values(u - 1)
                    ended_in[(l, u)] = ended_in[(l, "at")]

                for u in range(len(U)):
                    pe.wait_ge(*emptied("o", l, u))
                kinds_k = (range(0, 2), range(2, 5), range(5, 8))
                for c in range(2):
                    for k in range(KD):
                        br = [k in ks for ks in kinds_k].index(True)
                        key = ("out", l, c, k // 4, k // 2 % 2)
                        if k % 2 == 0:
                            wh, wl = (w.rearrange("p (k n) -> p k n", k=2) for w in split(*key))
                        for t in range(TILES):
                            group = ("y", l, c, t, br)
                            first, end = k == kinds_k[br][0], k == kinds_k[br][-1]
                            if first:
                                open_bank(*group)
                            ins = product(bank(*group)[:, :], tiles_of(oT)(k, t), (wh[:, k % 2, :], wl[:, k % 2, :]), first, end)
                            if end:
                                close_bank(ins, *group)
                        if k % 2:
                            end_quarter(key, ins, *(group if end else ()))
                pe.wait_ge(*merged_ready.at(l))
                for b in range(4):
                    o = open_bank("mT", l, b)
                    for m in range(4):
                        k, t = 2 * b + m // 2, m % 2
                        ins = tr(o[:, m * P:(m + 1) * P], merged[:, t, k * P:(k + 1) * P], ident[:, :])
                    close_bank(ins, "mT", l, b)
                for c in range(2):
                    turned_token = (lambda k: emptied("mT", l, k // 2)) if c == 0 else None
                    run(tokens_by_features(("o", l, c), "wo", tiles_of(hT), range(TILES), ready=turned_token))

                norm_transposes(2 * l + 1, xn1, TILES, 2)
                for m in range(16):
                    o = open_bank("up", l, m)
                    for j in range(2):
                        key = ("up", l, m // 2, m % 2, j)
                        wh, wl = (w.rearrange("p (k n) -> p k n", k=KD) for w in split(*key))
                        for k in range(KD):
                            if m + j == 0:
                                pe.wait_ge(*emptied("hT", 2 * l + 1, k // 2))
                            ins = product(o[:, j * SEQ:(j + 1) * SEQ], (wh[:, k, :], wl[:, k, :]),
                                          (hT[:, 0, k, :], hT[:, 1, k, :]), k == 0, k == KD - 1)
                        if j:
                            close_bank(ins, "up", l, m)
                        end_quarter(key, ins, *(("up", l, m) if j else ()))
                accs = {(t, c): open_bank("down", l, t, c) for t in range(TILES) for c in range(2)}
                for k in range(FF // P):
                    key = ("down", l, k // 4, k // 2 % 2, k % 2)
                    wh, wl = split(*key)
                    if k % 2 == 0:
                        pe.wait_ge(*up_ready.at(l, k // 2))
                    for t in range(TILES):
                        for c in range(2):
                            cols = slice(c * 512, (c + 1) * 512)
                            ins = product(accs[t, c][:, :], tiles_of(uT)(k, t), (wh[:, cols], wl[:, cols]), k == 0, k == FF // P - 1)
                            if k == FF // P - 1:
                                close_bank(ins, "down", l, t, c)
                    end_quarter(key, ins, *(("down", l, 1, 1) if k == FF // P - 1 else ()))

            def modulation(l, row):
                pe.wait_ge(*cond_ready_s.at("done"))
                for c in range(6):
                    o = open_bank("ada", l, c)
                    for k in range(KD):
                        n = half_at["ada", l, c, k // 4]
                        if k % 4 == 0:
                            pe.wait_ge(*half_is_loaded(n))
                        w = raw[:, n % SLOTS, k % 4 * 512:(k % 4 + 1) * 512]
                        ins = mm(o[0:2, :], cond[:, k, :], w, start=k == 0, stop=k == KD - 1)
                    close_bank(ins, "ada", l, c)
                    half_used[half_at["ada", l, c, 0]] = half_used[half_at["ada", l, c, 1]] = filled("ada", l, c)
                for c in range(6):
                    pe.wait_ge(*emptied("ada", l, c))
                o = open_bank("adaT", l)
                for k in range(16):
                    ins = tr(o[:, 2 * k:2 * k + 2], row[0:2, k * P:(k + 1) * P], ident[0:2, 0:2])
                close_bank(ins, "adaT", l)

            def gate_rows(l, row, sequences):
                for s in range(sequences):
                    for c in range(2):
                        o = open_bank("gateB", l, s, c)
                        ins = mm(o[:, :], select[:, s, :], row[0:2, c * 512:(c + 1) * 512], start=True, stop=True)
                        close_bank(ins, "gateB", l, s, c)

            def project2(l, j, tiles):
                turned_token = (lambda k: emptied("hT", 5 + l, k)) if j == 0 else None
                run(tokens_by_features(("in2", l, j), "in2", tiles_of(hT2), tiles, width=IN2[j][1] - IN2[j][0], ready=turned_token))

            def feature_groups(l, j, n):
                for c in range(4):
                    group, key = ("in2f", l, 4 * (j - 2) + c), ("in2", l, j, c // 2, c % 2)
                    o = open_bank(*group)
                    wh, wl = (w.rearrange("p (k n) -> p k n", k=KD) for w in split(*key))
                    for k in range(KD):
                        ins = product(o[:, 0:n], (wh[:, k, :], wl[:, k, :]), (hT2[:, 0, k, 0:n], hT2[:, 1, k, 0:n]),
                                      k == 0, k == KD - 1)
                        if k == KD - 1:
                            close_bank(ins, *group)
                            end_quarter(key, ins, *group)
                            ended_in.setdefault((2 + l, "at"), []).append(group)
                        yield

            def turn_heads(l, j, src, chunks, tiles, per_bank):
                pe.wait_ge(*heads_ready.at(l, j))
                for b in range(chunks // per_bank):
                    o = open_bank("heads", l, j, b)
                    for m in range(per_bank):
                        for t in range(tiles):
                            ins = tr(o[:, (m * tiles + t) * P:(m * tiles + t + 1) * P], src(b * per_bank + m, t), ident[:, :])
                    close_bank(ins, "heads", l, j, b)

            def attention2(l, filler, per_unit):
                U = units_of_block2(l)

                def scores(u):
                    kind, h, t = U[u]
                    half = DH * (h % 2)
                    first = SEQ if kind == "G" and t >= TILES else 0
                    if kind == "G":
                        q, k = qT2, kT2[half:half + DH, h // 4, first:N4]
                    elif kind == "W":
                        q, k = wqT, wkT[half:half + DH, h // 4, :]
                    else:
                        q, k = nqT, nkT[half:half + DH, h // 2, :]
                    o = open_bank("s", 2 + l, u)
                    ins = mm(o[:, 0:N4 - first], q[half:half + DH, h // 2, t * P:(t + 1) * P], k, start=True, stop=True)
                    close_bank(ins, "s", 2 + l, u)

                def blocks_of(u):
                    kind, h, t = U[u]
                    return range(2, 4) if kind == "G" and t >= TILES else range(4)

                def second(u):
                    pe.wait_ge(*probs_scaled.at(2 + l, u))
                    o = open_bank("p", 2 + l, u, 0)
                    for n, _ in enumerate(blocks_of(u)):
                        ins = tr(o[:, n * P:(n + 1) * P], S[:, u % 2, n * P:(n + 1) * P], ident[:, :])
                    close_bank(ins, "p", 2 + l, u, 0)

                def values(u):
                    kind, h, t = U[u]
                    pe.wait_ge(*emptied("p", 2 + l, u, 0))
                    o = open_bank("o", 2 + l, u)
                    blocks = blocks_of(u)
                    for n, b in enumerate(blocks):
                        if kind == "G":
                            v = kv2[:, b, (KVH + h // 4) * DH:(KVH + h // 4 + 1) * DH]
                        elif kind == "W":
                            v = kv3[:, b, (KVH + h // 4) * DH:(KVH + h // 4 + 1) * DH]
                        else:
                            v = nv[:, b, h * DH:(h + 1) * DH]
                        ins = mm(o[0:DH, 0:P], v, PT[:, u % 2, n * P:(n + 1) * P], start=n == 0, stop=n == len(blocks) - 1)
                    close_bank(ins, "o", 2 + l, u)

                for u in range(len(U) + 1):
                    ended_in[(2 + l, "at")] = []
                    if u < len(U):
                        scores(u)
                    if u >= 1:
                        second(u - 1)
                    advance(filler, per_unit(u) if u < len(U) else 1000)
                    if u >= 1:
                        values(u - 1)
                    ended_in[(2 + l, u)] = ended_in[(2 + l, "at")]

            def out2(l, tiles, first, second):
                acts = lambda k, t: tiles_of(first)(k, t) if k < 4 else tiles_of(second)(k - 4, t)
                for c in range(2):
                    run(tokens_by_features(("out2", l, c), "out2", acts, tiles))

            pe.wait_ge(late_loaded, LATE0 * 16)
            modulation(0, ada_row)
            norm_transposes(5, xn2, T4, 1)
            project2(0, 0, range(T4))
            project2(0, 1, range(T4))

            def fill0():
                for j in range(2, 7):
                    yield from feature_groups(0, j, N4)

            filler = fill0()
            ended_in[(2, "at")] = []
            advance(filler, 24)
            ended_in[(2, "before")] = ended_in[(2, "at")]
            turn_heads(0, 0, lambda c, t: q2[:, t, c * P:(c + 1) * P], 4, T4, 1)
            turn_heads(0, 1, lambda c, t: k2d[:, t, c, :], KVH, T4, 1)
            for b in range(4):
                pe.wait_ge(*emptied("heads", 0, 0, b))
            for b in range(KVH):
                pe.wait_ge(*emptied("heads", 0, 1, b))
            for t in range(T4):
                pe.wait_ge(*emptied("in2", 0, 1, t))
            attention2(0, filler, lambda u: 5)

            pe.wait_ge(filter_loaded, FILTERS * 16)
            o = open_bank("f", 0)
            close_bank(mm(o[0:HID, 0:SEQ], hyena_w1, positions, start=True, stop=True), "f", 0)
            pe.wait_ge(*sin_ready.at(0))
            o = open_bank("f", 1)
            close_bank(mm(o[0:HID, 0:SEQ], hyena_w2, hidden[0:HID, 0, :], start=True, stop=True), "f", 1)
            pe.wait_ge(*sin_ready.at(1))
            for od in range(2):
                for d in range(2):
                    for t in range(TILES):
                        o = open_bank("tap", od, d, t)
                        ins = mm(o[:, :], hidden[0:HID, 1, t * P:(t + 1) * P], w3[0:HID, od, d, :], start=True, stop=True)
                        close_bank(ins, "tap", od, d, t)
                pe.wait_ge(*taps_squared.at(od))
                o = open_bank("energy", od)
                for n in range(4):
                    ins = mm(o[:, :], ones[:, :], work.rearrange("p (a n) -> p a n", a=4)[:, n, :], start=n == 0, stop=n == 3)
                close_bank(ins, "energy", od)
                pe.wait_ge(*taps_mixed.at(od))
                for m in range(2):
                    for which in range(2):
                        o = open_bank("spec", od, m, which)
                        for t in range(TILES):
                            ins = mm(o[:, :], fourier_fwd[:, which, t, m * P:(m + 1) * P], taps_sd[:, which, t, :], start=t == 0, stop=t == 1)
                        close_bank(ins, "spec", od, m, which)
                o = open_bank("nyq", od)
                for t in range(TILES):
                    ins = mm(o[0:1, :], fourier_fwd[:, 1, t, 0:1], taps_sd[:, 0, t, :], start=t == 0, stop=t == 1)
                close_bank(ins, "nyq", od)
            for c in range(HY_CH):
                pe.wait_ge(*emptied("in2f", 0, c))
            for c in range(8):
                o = open_bank("zg", c)
                for t in range(T4):
                    ins = tr(o[:, t * P:(t + 1) * P], uc[:, c, t * P:(t + 1) * P], ident[:, :])
                close_bank(ins, "zg", c)
            for c in range(8):
                pe.wait_ge(*emptied("zg", c))
            for od in range(2):
                for s in range(2):
                    if od == 1:
                        for t in range(TILES):
                            pe.wait_ge(*emptied("z1", s, t))
                    for m in range(2):
                        for which in range(2):
                            o = open_bank("zf", od, s, m, which)
                            for t in range(TILES):
                                ins = mm(o[:, :], fourier_fwd[:, which, t, m * P:(m + 1) * P], Z[:, 2 * s + t, :], start=t == 0, stop=t == 1)
                            close_bank(ins, "zf", od, s, m, which)
                    if s == 1:
                        inverse_now = (0, 1)
                    else:
                        inverse_now = ()
                    for ss in inverse_now:
                        pe.wait_ge(*spectrum_ready.at(od, ss))
                        if od == 0:
                            for t in range(TILES):
                                o = open_bank("z1", ss, t)
                                for kk in range(4):
                                    ins = mm(o[:, :], fourier_inv[:, kk // 2, kk % 2, t * P:(t + 1) * P], spectrum(ss)[:, kk, :],
                                             start=kk == 0, stop=kk == 3)
                                close_bank(ins, "z1", ss, t)
                        else:
                            for c2 in range(2):
                                o = open_bank("y2", ss, c2)
                                for cc in range(2):
                                    c = 2 * c2 + cc
                                    for kk in range(4):
                                        ins = mm(o[:, cc * SEQ:(cc + 1) * SEQ], spectrum(ss)[:, kk, c * P:(c + 1) * P],
                                                 fourier_inv[:, kk // 2, kk % 2, :], start=kk == 0, stop=kk == 3)
                                close_bank(ins, "y2", ss, c2)
            gate_rows(0, gate_row, 2)
            pe.wait_ge(*low_ready.at("o2"))
            pe.wait_ge(*low_ready.at("y"))
            out2(0, range(T4), oT2r, yThr)

            modulation(1, ada_row3)
            gate_rows(1, ada_row3[:, 2 * D:3 * D], 1)
            norm_transposes(6, xn3, T4, 1)
            project2(1, 0, range(TILES))
            project2(1, 1, range(T4))
            project2(1, 2, range(TILES))
            project2(1, 3, range(T4))
            turn_heads(1, 0, lambda c, t: wq[:, t, c * P:(c + 1) * P], 4, TILES, 2)
            turn_heads(1, 1, lambda c, t: k3d[:, t, c, :], KVH, T4, 1)
            project2(1, 4, range(T4))
            turn_heads(1, 2, lambda c, t: nq[:, t, c * P:(c + 1) * P], 4, TILES, 2)
            turn_heads(1, 3, lambda c, t: nk[:, t, c * P:(c + 1) * P], 4, T4, 1)
            for j, n in ((0, 2), (1, 2), (2, 2), (3, 4)):
                for b in range(n):
                    pe.wait_ge(*emptied("heads", 1, j, b))
            for j in (1, 4):
                for t in range(T4):
                    pe.wait_ge(*emptied("in2", 1, j, t))

            def fill1():
                for j in (5, 6):
                    yield from feature_groups(1, j, SEQ)

            attention2(1, fill1(), lambda u: 8 if u % 4 == 0 else 0)
            pe.wait_ge(*low_ready.at("3"))
            out2(1, range(TILES), oT3r, yT3r)

        @block.scalar
        def _(act):
            run = Steps(act, scalar_step)
            A_ = nc.scalar.activation

            def norm_guess(n, tiles, xn):
                for t in range(tiles):
                    run(A_(xn[:, t, :], X[:, t, :], ACT.Square, accum_out=nstat[:, 0, t:t + 1]))
                run.settle()
                run(A_(nstat[:, 1, 0:tiles], nstat[:, 0, 0:tiles], ACT.Ln, bias=eps_col[:, 0:1], scale=1.0 / D))
                run.settle()
                run(A_(nstat[:, 2, 0:tiles], nstat[:, 1, 0:tiles], ACT.Exp, scale=-0.5), rsqrt_guess.by(n))

            def norm_scale(n, tiles, xn):
                act.wait_ge(*rstd_ready.at(n))
                run.settle()
                for t in range(1, tiles, 2):
                    last = t + 2 > tiles
                    run(A_(xn[:, t, :], X[:, t, :], ACT.Copy, scale=nstat[:, 2, t:t + 1]),
                        xn_by_scalar.by(n) if last else None)

            def round_weights(n):
                src, high, _ = raw_quarter(n)
                act.wait_ge(*half_is_loaded(half_at[quarters[n][:4]]))
                if n >= SPLITS:
                    act.wait_ge(*last_use[n - SPLITS])
                run(A_(high, src, ACT.Copy), (high_ready, n + 1))

            splits = Splits(round_weights)

            def copy_out(dst, src, *key):
                splits.due(*key)
                act.wait_ge(*filled(*key))
                run(A_(dst, src, ACT.Copy), emptied(*key))

            taken = [0]

            def take_high(ins, *key):
                taken[0] += 1
                run(ins, (high_taken, taken[0]))
                high_done[key] = (high_taken, taken[0])

            def norm_evacuate(n, which, l):
                for b in range(4):
                    splits.due("hT", n, b)
                    act.wait_ge(*filled("hT", n, b))
                    for kk in range(2):
                        k = 2 * b + kk
                        ins = A_(hT[:, 0, k, :], bank("hT", n, b)[:, kk * SEQ:(kk + 1) * SEQ], ACT.Copy,
                                 scale=g_cols[:, which, l, k:k + 1])
                        take_high(ins, "hT", n, b) if kk else run(ins)

            def softmax_exp(l, u, width, src, kind, scale):
                act.wait_ge(*bias_ready.at(l, u))
                if kind in "WN":
                    if kind == "W":
                        h = units_of_block2(l - 2)[u][1]
                        run(A_(stat[:, u % 2, 3, 1:2], sink[:, h:h + 1], ACT.Exp, bias=stat[:, u % 2, 1, 0:1]))
                run(A_(S[:, u % 2, 0:width], src, ACT.Exp, bias=stat[:, u % 2, 1, 0:1], scale=scale,
                       accum_out=stat[:, u % 2, 2, 0:1]), probs_ready.by(l, u))

            act.wait_ge(x_loaded, 16)
            act.wait_ge(consts_loaded, CONSTS * 16)
            act.wait_ge(ones_set, 1)
            run(A_(cond_e[:, :, :], cond[:, :, :], ACT.Exp, scale=-1.0), cond_exp.by(0))
            for l in range(LAYERS):
                if l:
                    act.wait_ge(*x_added.at(2 * l - 1))
                else:
                    for n in range(SPLITS):
                        splits.one(n)
                    splits.n = SPLITS
                norm_guess(2 * l, TILES, xn1)
                norm_scale(2 * l, TILES, xn1)
                norm_evacuate(2 * l, 0, l)
                for c in range(9):
                    if c >= 6:
                        for n in range((c - 6) * 4 + 1, (c - 6) * 4 + 4, 2):
                            j, b = n // 6, n % 6
                            copy_out(qkT[:, j, 2 * b:2 * b + 2, :], bank("qT", l, j, b)[:, :].rearrange("p (a n) -> p a n", a=2), "qT", l, j, b)
                    for t in range(TILES):
                        copy_out(qkv[:, c // 3, t, c % 3 * 512:(c % 3 + 1) * 512], bank("qkv", l, c, t)[:, :], "qkv", l, c, t)
                U = units_of_block1()

                def take_second(u):
                    kind, h, t = U[u]
                    if u >= 2:
                        act.wait_ge(*filled("o", l, u - 2))
                    if kind == "C":
                        act.wait_ge(*stick_argument.at(l, u))
                        run(A_(PT[:, u % 2, 0:384], S[:, u % 2, 384:768], ACT.Exp, scale=SCALE), stick_weights.by(l, u))
                        return
                    blocks = (G_A if kind == "A" else 1) * (t + 1)
                    for b0 in range(0, blocks, 4):
                        n = min(4, blocks - b0) * P
                        copy_out(PT[:, u % 2, b0 * P:b0 * P + n], bank("p", l, u, b0 // 4)[:, 0:n], "p", l, u, b0 // 4)

                def take_values(u):
                    kind, h, t = U[u]
                    chunk, half = {"A": 0, "B": 2, "C": 5}[kind] + h // 2, DH * (h % 2)
                    cols = slice(0, SEQ) if kind == "C" else slice(t * P, (t + 1) * P)
                    n = SEQ if kind == "C" else P
                    act.wait_ge(*filled("o", l, u))
                    take_high(A_(oT[half:half + DH, 0, chunk, cols], bank("o", l, u)[0:DH, 0:n], ACT.Copy), "o", l, u)

                for u in range(len(U) + 1):
                    if u >= 1:
                        take_second(u - 1)
                    if u < len(U):
                        splits.due("s", l, u)
                        kind, h, t = U[u]
                        if kind == "C":
                            act.wait_ge(*stick_masked.at(l, u))
                            s = S[:, u % 2, 384:768]
                            run(A_(s, S[:, u % 2, 0:384], ACT.Abs))
                            run.settle()
                            run(A_(s, s, ACT.Exp, scale=-SCALE))
                            run.settle()
                            run(A_(s, s, ACT.Ln, bias=eps_col[:, 1:2]), softplus_part.by(l, u))
                        else:
                            w = (G_A if kind == "A" else 1) * (t + 1) * P
                            softmax_exp(l, u, w, S[:, u % 2, 0:w], kind, SCALE)
                    for key in ended_in[(l, u)]:
                        _, _, c, t = key
                        c -= 9
                        splits.due(*key)
                        act.wait_ge(*filled(*key))
                        run(A_(gates[:, t, c // 2, c % 2 * 512:(c % 2 + 1) * 512], bank(*key)[:, :], ACT.Exp, scale=-1.0),
                            emptied(*key))
                    if u >= 1:
                        take_values(u - 1)
                for b in range(4):
                    splits.due("mT", l, b)
                    act.wait_ge(*filled("mT", l, b))
                    take_high(A_(hT[:, 0, 2 * b:2 * b + 2, :], bank("mT", l, b)[:, :].rearrange("p (a n) -> p a n", a=2), ACT.Copy),
                              "mT", l, b)
                splits.due("wo", l, 1, 1)
                act.wait_ge(*x_added.at(2 * l))
                norm_guess(2 * l + 1, TILES, xn1)
                norm_scale(2 * l + 1, TILES, xn1)
                norm_evacuate(2 * l + 1, 1, l)
                for m in range(16):
                    splits.due("up", l, m)
                    if m >= 2:
                        act.wait_ge(*up_ready.at(l, m - 2))
                    act.wait_ge(*filled("up", l, m))
                    run(A_(up_tmp[:, m % 2, 0, :], bank("up", l, m)[:, :], ACT.Relu), emptied("up", l, m))
                    run.settle()
                    take_high(A_(uT[:, 0, 2 * m:2 * m + 2, :], up_tmp[:, m % 2, 0, :].rearrange("p (a n) -> p a n", a=2), ACT.Square),
                              "up", l, m)
                splits.due("down", l, 1, 1)
            act.wait_ge(*x_added.at(3))
            norm_guess(4, TILES, xn1)

            def modulated_evacuate(n, l):
                for k in range(KD):
                    splits.due("hT", n, k)
                    act.wait_ge(*filled("hT", n, k))
                    if k == 0:
                        act.wait_ge(*ada_ready.at(l))
                    for s in range(2):
                        cols = slice(s * SEQ, (s + 1) * SEQ)
                        ins = A_(hT2[:, 0, k, cols], bank("hT", n, k)[:, cols], ACT.Identity,
                                 scale=gain[:, k, s:s + 1], bias=ada_t[:, k, s:s + 1])
                        take_high(ins, "hT", n, k) if s else run(ins)

            def gate_rows(l, dst, sequences):
                for s in range(sequences):
                    for c in range(2):
                        copy_out(dst[:, s, c * 512:(c + 1) * 512], bank("gateB", l, s, c)[:, :], "gateB", l, s, c)

            def heads_rsqrt(l, j, n):
                act.wait_ge(*heads_squared.at(l, j))
                run(A_(nstat[:, 1, 0:n], nstat[:, 0, 0:n], ACT.Ln, bias=eps_col[:, 0:1], scale=1.0 / DH))
                run.settle()
                run(A_(nstat[:, 2, 0:n], nstat[:, 1, 0:n], ACT.Exp, scale=-0.5), heads_guess.by(l, j))

            def take_features(l, key):
                c = key[2]
                splits.due(*key)
                if l == 0 and c < HY_CH:
                    act.wait_ge(*filled(*key))
                    run(A_(uc[:, c, :], bank(*key)[:, :], ACT.Identity, scale=conv_w[:, 1, c:c + 1], bias=conv_w[:, 3, c:c + 1]),
                        conv_begun.by(c))
                else:
                    n, dst = (N4, (ag, hg)) if l == 0 else (SEQ, (wgT, ngT))
                    c -= HY_CH
                    act.wait_ge(*filled(*key))
                    run(A_(dst[c // 4][:, c % 4, :], bank(*key)[:, 0:n], ACT.Exp, scale=-1.0), silu_exp.by(l, c))

            def attention2(l):
                U = units_of_block2(l)
                for u in range(len(U) + 1):
                    if u >= 1:
                        n = (2 if U[u - 1][0] == "G" and U[u - 1][2] >= TILES else 4) * P
                        if u >= 3:
                            act.wait_ge(*filled("o", 2 + l, u - 3))
                        copy_out(PT[:, (u - 1) % 2, 0:n], bank("p", 2 + l, u - 1, 0)[:, 0:n], "p", 2 + l, u - 1, 0)
                    if u < len(U):
                        splits.due("s", 2 + l, u)
                        kind, h, t = U[u]
                        n = SEQ if kind == "G" and t >= TILES else N4
                        if kind == "G":
                            act.wait_ge(*bias_ready.at(2, u))
                            if u >= 2:
                                act.wait_ge(*filled("p", 2 + l, u - 2, 0))
                            run(A_(S[:, u % 2, 0:n], bank("s", 2, u)[:, 0:n], ACT.Exp, bias=stat[:, u % 2, 1, 0:1],
                                   scale=SCALE, accum_out=stat[:, u % 2, 2, 0:1]), probs_ready.by(2, u))
                        else:
                            softmax_exp(2 + l, u, n, S[:, u % 2, 0:n], kind, 1.0)
                    for key in ended_in[(2 + l, u)]:
                        take_features(l, key)
                    if u >= 1:
                        kind, h, t = U[u - 1]
                        half = DH * (h % 2)
                        dst = {"G": oT2, "W": oT3, "N": yT3}[kind]
                        copy_out(dst[half:half + DH, h // 2, t * P:(t + 1) * P], bank("o", 2 + l, u - 1)[0:DH, 0:P], "o", 2 + l, u - 1)

            act.wait_ge(*x_added.at(4))
            act.wait_ge(x_loaded, 32)
            norm_guess(5, T4, xn2)
            norm_scale(5, T4, xn2)
            modulated_evacuate(5, 0)
            for t in range(T4):
                copy_out(q2[:, t, :], bank("in2", 0, 0, t)[:, :], "in2", 0, 0, t)
            for t in range(T4):
                copy_out(kv2[:, t, :], bank("in2", 0, 1, t)[:, 0:256], "in2", 0, 1, t)
            heads_rsqrt(0, 0, T4 * QH)
            heads_rsqrt(0, 1, T4 * KVH)
            for key in ended_in[(2, "before")]:
                take_features(0, key)
            for b in range(4):
                copy_out(qT2[:, b, :], bank("heads", 0, 0, b)[:, :], "heads", 0, 0, b)
            for b in range(KVH):
                copy_out(kT2[:, b, :], bank("heads", 0, 1, b)[:, :], "heads", 0, 1, b)
            attention2(0)
            act.wait_ge(*out_gated.at("o2"))
            take_high(A_(oT2r[:, 0], oT2, ACT.Copy), "o2")
            for n in range(2):
                act.wait_ge(*sin_in_range.at(n))
                run(A_(hidden[0:HID, n, :], hidden[0:HID, n, :], ACT.Sin), sin_ready.by(n))
            for od in range(2):
                act.wait_ge(*filled("energy", od))
                run(A_(rn[:, 0, :], bank("energy", od)[:, :], ACT.Ln, bias=eps_col[:, 0:1]))
                run.settle()
                run(A_(rn[:, 0, :], rn[:, 0, :], ACT.Exp, scale=-0.5), taps_guess.by(od))
            act.wait_ge(*spectra_ready.at(1))
            for c in range(8):
                if c % 2:
                    dst = (Z, G1)[c // 4][:, :, c % 4 * P:(c % 4 + 1) * P]
                    copy_out(dst, bank("zg", c)[:, :].rearrange("p (t n) -> p t n", t=T4), "zg", c)
            for s in range(2):
                for c2 in range(2):
                    cols = slice(s * SEQ, (s + 1) * SEQ)
                    act.wait_ge(*out_gated.at("y", s, c2))
                    take_high(A_(yThr[:, 0, 2 * c2:2 * c2 + 2, cols], y_tmp[:, c2, :].rearrange("p (a n) -> p a n", a=2), ACT.Copy), "y", s, c2)
            gate_rows(0, gate_b0, 2)
            splits.due("out2", 0, 1, T4 - 1)
            act.wait_ge(*x_added.at(5))
            norm_guess(6, T4, xn3)
            norm_scale(6, T4, xn3)
            gate_rows(1, gate_b1, 1)
            modulated_evacuate(6, 1)
            for t in range(TILES):
                copy_out(wq[:, t, :], bank("in2", 1, 0, t)[:, :], "in2", 1, 0, t)
            for t in range(T4):
                copy_out(kv3[:, t, :], bank("in2", 1, 1, t)[:, 0:256], "in2", 1, 1, t)
            for t in range(TILES):
                copy_out(nq[:, t, :], bank("in2", 1, 2, t)[:, :], "in2", 1, 2, t)
            for t in range(T4):
                copy_out(nk[:, t, :], bank("in2", 1, 3, t)[:, :], "in2", 1, 3, t)
            heads_rsqrt(1, 0, TILES * QH)
            heads_rsqrt(1, 1, T4 * KVH)
            for b in range(2):
                copy_out(wqT[:, 2 * b:2 * b + 2, :], bank("heads", 1, 0, b)[:, :].rearrange("p (a n) -> p a n", a=2), "heads", 1, 0, b)
            for b in range(KVH):
                copy_out(wkT[:, b, :], bank("heads", 1, 1, b)[:, :], "heads", 1, 1, b)
            for t in range(T4):
                copy_out(nv[:, t, :], bank("in2", 1, 4, t)[:, :], "in2", 1, 4, t)
            heads_rsqrt(1, 2, TILES * QH)
            heads_rsqrt(1, 3, T4 * QH)
            for b in range(2):
                copy_out(nqT[:, 2 * b:2 * b + 2, :], bank("heads", 1, 2, b)[:, :].rearrange("p (a n) -> p a n", a=2), "heads", 1, 2, b)
            for b in range(4):
                copy_out(nkT[:, b, :], bank("heads", 1, 3, b)[:, :], "heads", 1, 3, b)
            attention2(1)
            act.wait_ge(*out_gated.at("3"))
            run(A_(oT3r[:, 0], oT3, ACT.Copy))
            take_high(A_(yT3r[:, 0], yT3, ACT.Copy), "3")
            splits.due("out2", 1, 1, 1)

        @block.vector
        def _(dve):
            run = Steps(dve, vector_step)
            V = nc.vector

            def newton(v, y, t, width=None):
                run(V.tensor_tensor(t, y, y, ALU.mult))
                run.settle()
                run(V.tensor_tensor(t, t, v, ALU.mult))
                run.settle()
                run(V.tensor_scalar(t, t, -0.5, 1.5, ALU.mult, ALU.add))
                run.settle()

            def norm_finish(n, tiles, xn):
                dve.wait_ge(*rsqrt_guess.at(n))
                v, y, t = nstat[:, 0, 0:tiles], nstat[:, 2, 0:tiles], nstat[:, 3, 0:tiles]
                run(V.tensor_scalar(v, v, 1.0 / D, EPS, ALU.mult, ALU.add))
                run.settle()
                newton(v, y, t)
                run(V.tensor_tensor(y, y, t, ALU.mult), rstd_ready.by(n))
                run.settle()
                if xn is None:
                    return
                for tt in range(0, tiles, 2):
                    run(V.tensor_scalar(xn[:, tt, :], X[:, tt, :], nstat[:, 2, tt:tt + 1], None, ALU.mult),
                        xn_by_vector.by(n) if tt + 2 >= tiles else None)

            def subtract_high(n):
                src, high, low = raw_quarter(n)
                dve.wait_ge(high_ready, n + 1)
                run(V.tensor_tensor(low, src, high.bitcast(F32), ALU.subtract), (split_ready, n + 1))

            splits = Splits(subtract_high)

            def take_low(x, k, value, signal, *key):
                dve.wait_ge(*high_done[key])
                run(V.tensor_tensor(x[:, 1][k], value, x[:, 0][k].bitcast(F32), ALU.subtract), signal)

            def norm_evacuate(n, which, l):
                for b in range(4):
                    splits.due("hT", n, b)
                    dve.wait_ge(*high_done["hT", n, b])
                    for kk in range(2):
                        k = 2 * b + kk
                        run(V.scalar_tensor_tensor(out=hT[:, 1, k, :], in0=bank("hT", n, b)[:, kk * SEQ:(kk + 1) * SEQ],
                                                   scalar=g_cols[:, which, l, k:k + 1], in1=hT[:, 0, k, :].bitcast(F32),
                                                   op0=ALU.mult, op1=ALU.subtract), emptied("hT", n, b) if kk else None)

            dve.wait_ge(consts_loaded, CONSTS * 16)
            run(V.memset(ones[:, :], 1.0))
            run(V.memset(eps_col[:, 0:1], EPS))
            V.memset(eps_col[:, 1:2], 1.0).then_inc(ones_set, 1)
            dve.wait_ge(ones_set, 1)
            dve.wait_ge(*cond_exp.at(0))
            run(V.tensor_scalar(cond_e[:, :, :], cond_e[:, :, :], 1.0, None, ALU.add), cond_ready_s.by("sum"))
            run.settle()
            run(V.reciprocal(cond_e[:, :, :], cond_e[:, :, :]))
            run.settle()
            run(V.tensor_tensor(cond[:, :, :], cond[:, :, :], cond_e[:, :, :], ALU.mult), cond_ready_s.by("done"))
            dve.wait_ge(x_loaded, 16)

            for n in range(SPLITS):
                splits.one(n)
            splits.n = SPLITS
            for l in range(LAYERS):
                norm_finish(2 * l, TILES, xn1)
                norm_evacuate(2 * l, 0, l)
                for j in range(2):
                    for c in range(3 * j, 3 * j + 3):
                        for t in range(TILES):
                            splits.due("qkv", l, c, t)
                            dve.wait_ge(*emptied("qkv", l, c, t))
                    if l + j == 0:
                        dve.wait_ge(rel_stored, 16)
                    h3 = ROPE // 2
                    for t in range(TILES):
                        hd = qkv[:, j, t, 0:ROT * DH].rearrange("p (h d) -> p h d", h=ROT)
                        x1, x2 = hd[:, :, 0:h3], hd[:, :, h3:ROPE]
                        cos = rope_a[:, t, 0:h3].unsqueeze(1).to_broadcast([P, ROT, h3])
                        sin = rope_a[:, t, h3:ROPE].unsqueeze(1).to_broadcast([P, ROT, h3])
                        r = [rope_tmp[:, n, t, :, :] for n in range(4)]
                        run(V.tensor_tensor(r[0], x1, cos, ALU.mult))
                        run(V.tensor_tensor(r[1], x2, sin, ALU.mult))
                        run(V.tensor_tensor(r[2], x2, cos, ALU.mult))
                        run(V.tensor_tensor(r[3], x1, sin, ALU.mult))
                        run.settle()
                        run(V.tensor_tensor(x1, r[0], r[1], ALU.subtract))
                        run(V.tensor_tensor(x2, r[2], r[3], ALU.add), qk_roped.by(l, j) if t else None)
                    run.settle()
                for n in range(0, 12, 2):
                    j, b = n // 6, n % 6
                    splits.due("qT", l, j, b)
                    dve.wait_ge(*filled("qT", l, j, b))
                    run(V.tensor_copy(qkT[:, j, 2 * b:2 * b + 2, :], bank("qT", l, j, b)[:, :].rearrange("p (a n) -> p a n", a=2)),
                        emptied("qT", l, j, b))

                U = units_of_block1()
                last_p = lambda u: filled("p", l, u, 1 if U[u][0] == "A" and U[u][2] else 0)

                def finish_gates(u):
                    for key in ended_in[(l, u)]:
                        _, _, c, t = key
                        c -= 9
                        g = gates[:, t, c // 2, c % 2 * 512:(c % 2 + 1) * 512]
                        dve.wait_ge(*emptied(*key))
                        run(V.tensor_scalar(g, g, 1.0, None, ALU.add))
                        run.settle()
                        run(V.reciprocal(g, g))

                def take_outputs(u):
                    kind, h, t = U[u]
                    chunk, half = {"A": 0, "B": 2, "C": 5}[kind] + h // 2, DH * (h % 2)
                    cols = slice(0, SEQ) if kind == "C" else slice(t * P, (t + 1) * P)
                    n = SEQ if kind == "C" else P
                    x = oT[half:half + DH]
                    dve.wait_ge(*high_done["o", l, u])
                    run(V.tensor_tensor(x[:, 1, chunk, cols], bank("o", l, u)[0:DH, 0:n], x[:, 0, chunk, cols].bitcast(F32),
                                        ALU.subtract), emptied("o", l, u))

                for u in range(len(U) + 1):
                    if u >= 2:
                        take_outputs(u - 2)
                    if u < len(U):
                        kind, h, t = U[u]
                        st = stat[:, u % 2, :, :]
                        if u >= 2:
                            dve.wait_ge(*last_p(u - 2))
                        dve.wait_ge(*filled("s", l, u))
                        if kind == "C":
                            run(V.tensor_tensor(S[:, u % 2, 0:384], bank("s", l, u)[:, 0:384], mask_c.rearrange("p a n -> p (a n)"), ALU.add),
                                emptied("s", l, u))
                            run.settle()
                            run(V.tensor_copy(small[:, 0:1], S[:, u % 2, 0:1]), stick_masked.by(l, u))
                        elif kind == "A":
                            n = G_A if t == 0 else 2
                            w = (t + 1) * P
                            run(V.tensor_tensor_reduce(
                                S[:, u % 2, 0:n * w].rearrange("p (g n) -> p g n", g=n),
                                bank("s", l, u)[:, 0:n * w].rearrange("p (g n) -> p g n", g=n),
                                mask_a[:, 0:n, SEQ - w:SEQ], 1.0, -3e38, ALU.add, ALU.max, st[:, 0, 0:1]), emptied("s", l, u))
                            if t:
                                dve.wait_ge(*filled("s2", l, u))
                                run(V.tensor_tensor_reduce(S[:, u % 2, 512:768], bank("s2", l, u)[:, 0:w], mask_a[:, 2, :],
                                                           1.0, -3e38, ALU.add, ALU.max, st[:, 0, 1:2]), emptied("s2", l, u))
                                run.settle()
                                run(V.tensor_tensor(st[:, 0, 0:1], st[:, 0, 0:1], st[:, 0, 1:2], ALU.max))
                        else:
                            w = (t + 1) * P
                            run(V.tensor_tensor_reduce(S[:, u % 2, 0:w], bank("s", l, u)[:, 0:w], mask_b[:, SEQ - w:SEQ],
                                                       1.0, -3e38, ALU.add, ALU.max, st[:, 0, 0:1]), emptied("s", l, u))
                        if kind != "C":
                            run.settle()
                            run(V.tensor_scalar(st[:, 1, 0:1], st[:, 0, 0:1], -SCALE, None, ALU.mult), bias_ready.by(l, u))
                    if u >= 1 and U[u - 1][0] == "C":
                        dve.wait_ge(*filled("p", l, u - 1, 0))
                        s = S[:, (u - 1) % 2, :]
                        run(V.tensor_tensor(s[:, 384:768], s[:, 0:384], bank("p", l, u - 1, 0)[:, 0:384], ALU.subtract),
                            emptied("p", l, u - 1, 0))
                        run.settle()
                        run(V.tensor_copy(small[:, 1:2], s[:, 384:385]), stick_argument.by(l, u - 1))
                    splits.due("s", l, min(u, len(U) - 1))
                    if u >= 1:
                        finish_gates(u - 1)
                    if u < len(U):
                        if kind == "C":
                            sp = PT[:, u % 2, 384:768]
                            if u >= 2:
                                dve.wait_ge(*filled("o", l, u - 2))
                            run(V.tensor_scalar(sp, S[:, u % 2, 0:384], 0.0, None, ALU.max))
                            run.settle()
                            dve.wait_ge(*softplus_part.at(l, u))
                            run(V.scalar_tensor_tensor(out=sp, in0=S[:, u % 2, 384:768], scalar=1.0 / SCALE, in1=sp,
                                                       op0=ALU.mult, op1=ALU.add), stick_summed.by(l, u))
                        else:
                            w = (G_A if kind == "A" else 1) * (t + 1) * P
                            dve.wait_ge(*probs_ready.at(l, u))
                            run(V.reciprocal(st[:, 2, 1:2], st[:, 2, 0:1]))
                            run.settle()
                            run(V.tensor_scalar(S[:, u % 2, 0:w], S[:, u % 2, 0:w], st[:, 2, 1:2], None, ALU.mult),
                                probs_scaled.by(l, u))
                take_outputs(len(U) - 1)
                finish_gates(len(U))

                run.settle()
                for c in range(2):
                    for t in range(TILES):
                        cols = slice(c * 512, (c + 1) * 512)
                        for br in range(3):
                            splits.due("y", l, c, t, br)
                            dve.wait_ge(*filled("y", l, c, t, br))
                            dst = merged[:, t, cols] if br == 0 else gated[:, br - 1, :]
                            run(V.tensor_tensor(dst, bank("y", l, c, t, br)[:, :], gates[:, t, br, cols], ALU.mult),
                                emptied("y", l, c, t, br))
                        run.settle()
                        run(V.tensor_tensor(merged[:, t, cols], merged[:, t, cols], gated[:, 0, :], ALU.add))
                        run.settle()
                        last = c + t == 2
                        run(V.tensor_tensor(merged[:, t, cols], merged[:, t, cols], gated[:, 1, :], ALU.add),
                            merged_ready.by(l) if last else None)
                        run.settle()

                def add_to_x(name, n):
                    for c in range(2):
                        for t in range(TILES):
                            key = (name, l, c, t) if name == "wo" else (name, l, t, c)
                            splits.due(*key)
                            dve.wait_ge(*filled(*key))
                            x = X[:, t, c * 512:(c + 1) * 512]
                            run(V.tensor_tensor(x, x, bank(*key)[:, :], ALU.add), emptied(*key))
                    run.settle()
                    run(V.tensor_copy(small[:, 2:3], X[:, 1, D - 1:D]), x_added.by(n))
                    run.settle()

                for b in range(4):
                    splits.due("mT", l, b)
                    dve.wait_ge(*high_done["mT", l, b])
                    k = slice(2 * b, 2 * b + 2)
                    run(V.tensor_tensor(hT[:, 1, k, :], bank("mT", l, b)[:, :].rearrange("p (a n) -> p a n", a=2),
                                        hT[:, 0, k, :].bitcast(F32), ALU.subtract), emptied("mT", l, b))
                add_to_x("wo", 2 * l)
                norm_finish(2 * l + 1, TILES, xn1)
                norm_evacuate(2 * l + 1, 1, l)
                for m in range(16):
                    splits.due("up", l, m)
                    t, v = up_tmp[:, m % 2, 0, :], up_tmp[:, m % 2, 1, :]
                    dve.wait_ge(*high_done["up", l, m])
                    run(V.tensor_tensor(v, t, t, ALU.mult))
                    run.settle()
                    k = slice(2 * m, 2 * m + 2)
                    run(V.tensor_tensor(uT[:, 1, k, :], v.rearrange("p (a n) -> p a n", a=2), uT[:, 0, k, :].bitcast(F32),
                                        ALU.subtract), up_ready.by(l, m))
                add_to_x("down", 2 * l + 1)

            norm_finish(4, TILES, None)
            dve.wait_ge(final_g_loaded, 16)
            for t in range(TILES):
                run(V.scalar_tensor_tensor(out=X[:, t, :], in0=X[:, t, :], scalar=nstat[:, 2, t:t + 1], in1=final_g,
                                           op0=ALU.mult, op1=ALU.mult), x_added.by(4) if t else None)

            def modulation(l, row, gate, bias):
                dve.wait_ge(late_loaded, LATE0 * 16)
                if l:
                    dve.wait_ge(ada_bias_loaded, 16)
                for c in range(6):
                    cols = slice(c * 512, (c + 1) * 512)
                    dst = row[0:2, cols] if c < 4 else gate[0:2, (c - 4) * 512:(c - 3) * 512]
                    splits.due("ada", l, c)
                    dve.wait_ge(*filled("ada", l, c))
                    run(V.tensor_tensor(dst, bank("ada", l, c)[0:2, :], bias[0:2, cols], ALU.add), emptied("ada", l, c))
                dve.wait_ge(*filled("adaT", l))
                run(V.tensor_copy(ada_t[:, :, :], bank("adaT", l)[:, 0:32].rearrange("p (k s) -> p k s", k=16)), emptied("adaT", l))
                run.settle()
                run(V.tensor_scalar(gain[:, :, :], ada_t[:, KD:2 * KD, :], 1.0, None, ALU.add))
                run.settle()
                g = g_cols[:, 2, l, :].unsqueeze(2).to_broadcast([P, KD, 2])
                run(V.tensor_tensor(gain[:, :, :], gain[:, :, :], g, ALU.mult), ada_ready.by(l))

            def modulated_evacuate(n, tmp):
                run.settle()
                for k in range(KD):
                    splits.due("hT", n, k)
                    dve.wait_ge(*high_done["hT", n, k])
                    b = bank("hT", n, k)
                    for s in range(2):
                        cols = slice(s * SEQ, (s + 1) * SEQ)
                        run(V.tensor_scalar(tmp[:, k % 2, cols], b[:, cols], gain[:, k, s:s + 1], ada_t[:, k, s:s + 1], ALU.mult, ALU.add))
                    run.settle()
                    run(V.tensor_tensor(hT2[:, 1, k, :], tmp[:, k % 2, :], hT2[:, 0, k, :].bitcast(F32), ALU.subtract), emptied("hT", n, k))

            def heads_norm(l, j, x, tiles, heads, g, rope, dup, ready, ahead=()):
                n = tiles * heads
                for key in ready:
                    splits.due(*key)
                    dve.wait_ge(*emptied(*key))
                x3 = x.rearrange("p t (h d) -> p t h d", h=heads)
                sq = work[:, 0:n * DH].rearrange("p (t h d) -> p t h d", t=tiles, h=heads)
                for t in range(tiles):
                    run(V.tensor_tensor(sq[:, t], x3[:, t], x3[:, t], ALU.mult))
                run.settle()
                run(V.tensor_reduce(nstat[:, 0, 0:n], work[:, 0:n * DH].rearrange("p (a d) -> p a d", d=DH), AX_X, ALU.add),
                    heads_squared.by(l, j))
                v, y, t_ = nstat[:, 0, 0:n], nstat[:, 2, 0:n], nstat[:, 3, 0:n]
                for key in ahead:
                    splits.due(*key)
                dve.wait_ge(*heads_guess.at(l, j))
                run(V.tensor_scalar(v, v, 1.0 / DH, EPS, ALU.mult, ALU.add))
                run.settle()
                newton(v, y, t_)
                run(V.tensor_tensor(y, y, t_, ALU.mult))
                run.settle()
                for t in range(tiles):
                    r = y[:, t * heads:(t + 1) * heads].unsqueeze(2).to_broadcast([P, heads, DH])
                    run(V.tensor_tensor(x3[:, t], x3[:, t], r, ALU.mult))
                run.settle()
                gb = head_gain[:, g, :].unsqueeze(1).to_broadcast([P, heads, DH])
                for t in range(tiles):
                    run(V.tensor_tensor(x3[:, t], x3[:, t], gb, ALU.mult))
                run.settle()
                if rope:
                    hd = DH // 2
                    for t in range(TILES):
                        x0, x1 = x3[:, t, :, 0:DH:2], x3[:, t, :, 1:DH:2]
                        cos = rope_b[:, t, 0:hd].unsqueeze(1).to_broadcast([P, heads, hd])
                        sin = rope_b[:, t, hd:DH].unsqueeze(1).to_broadcast([P, heads, hd])
                        r = [work[:, (4 * t + m) * 256:(4 * t + m) * 256 + heads * hd].rearrange("p (h d) -> p h d", h=heads)
                             for m in range(4)]
                        run(V.tensor_tensor(r[0], x0, cos, ALU.mult))
                        run(V.tensor_tensor(r[1], x1, sin, ALU.mult))
                        run(V.tensor_tensor(r[2], x0, sin, ALU.mult))
                        run(V.tensor_tensor(r[3], x1, cos, ALU.mult))
                        run.settle()
                        run(V.tensor_tensor(x0, r[0], r[1], ALU.subtract))
                        run(V.tensor_tensor(x1, r[2], r[3], ALU.add))
                    run.settle()
                if dup is not None:
                    for half in range(2):
                        ins = V.tensor_copy(dup.rearrange("p t h (a d) -> p t h a d", a=2)[:, :, :, half, :], x3)
                        run(ins, heads_ready.by(l, j) if half else None)
                else:
                    run(V.tensor_copy(small[:, 3:4], small[:, 3:4]), heads_ready.by(l, j))
                run.settle()

            def silu_finish(l, key):
                c = key[2] - HY_CH
                n, dst = (N4, (ag, hg)) if l == 0 else (SEQ, (wgT, ngT))
                g = dst[c // 4][:, c % 4, :]
                dve.wait_ge(*silu_exp.at(l, c))
                run(V.tensor_scalar(g, g, 1.0, None, ALU.add))
                run.settle()
                run(V.reciprocal(g, g))
                run.settle()
                run(V.tensor_tensor(g, g, bank(*key)[:, 0:n], ALU.mult), emptied(*key))

            def take_features(l, key):
                splits.due(*key)
                c = key[2]
                if l or c >= HY_CH:
                    return silu_finish(l, key)
                dve.wait_ge(*conv_begun.at(c))
                b = bank(*key)[:, :].rearrange("p (s n) -> p s n", s=2)
                u = uc[:, c, :].rearrange("p (s n) -> p s n", s=2)
                for s in range(2):
                    run(V.scalar_tensor_tensor(out=u[:, s, 1:SEQ], in0=b[:, s, 0:SEQ - 1], scalar=conv_w[:, 0, c:c + 1],
                                               in1=u[:, s, 1:SEQ], op0=ALU.mult, op1=ALU.add))
                run.settle()
                for s in range(2):
                    run(V.scalar_tensor_tensor(out=u[:, s, 0:SEQ - 1], in0=b[:, s, 1:SEQ], scalar=conv_w[:, 2, c:c + 1],
                                               in1=u[:, s, 0:SEQ - 1], op0=ALU.mult, op1=ALU.add), emptied(*key) if s else None)

            def attention2(l):
                U = units_of_block2(l)
                for u in range(len(U) + 1):
                    if u >= 1:
                        for key in ended_in[(2 + l, u - 1)]:
                            take_features(l, key)
                    splits.due("s", 2 + l, min(u, len(U) - 1))
                    if u < len(U):
                        kind, h, t = U[u]
                        st = stat[:, u % 2, :, :]
                        n = SEQ if kind == "G" and t >= TILES else N4
                        b = bank("s", 2 + l, u)
                        dve.wait_ge(*filled("s", 2 + l, u))
                        if kind == "G":
                            run(V.tensor_reduce(st[:, 0, 0:1], b[:, 0:n], AX_X, ALU.max))
                            run.settle()
                            run(V.tensor_scalar(st[:, 1, 0:1], st[:, 0, 0:1], -SCALE, None, ALU.mult), bias_ready.by(2 + l, u))
                        else:
                            if u >= 2:
                                dve.wait_ge(*filled("p", 2 + l, u - 2, 0))
                            m = mask_w[:, t, :] if kind == "W" else rel_bias[:, t, h, :]
                            run(V.scalar_tensor_tensor(out=S[:, u % 2, 0:SEQ], in0=b[:, 0:SEQ], scalar=SCALE, in1=m,
                                                       op0=ALU.mult, op1=ALU.add))
                            run(V.tensor_scalar(S[:, u % 2, SEQ:N4], b[:, SEQ:N4], SCALE, None, ALU.mult), emptied("s", 2 + l, u))
                            run.settle()
                            run(V.tensor_reduce(st[:, 0, 0:1], S[:, u % 2, 0:N4], AX_X, ALU.max))
                            run.settle()
                            if kind == "W":
                                run(V.tensor_tensor(st[:, 0, 0:1], st[:, 0, 0:1], sink[:, h:h + 1], ALU.max))
                                run.settle()
                            run(V.tensor_scalar(st[:, 1, 0:1], st[:, 0, 0:1], -1.0, None, ALU.mult), bias_ready.by(2 + l, u))
                    if u < len(U):
                        dve.wait_ge(*probs_ready.at(2 + l, u))
                        total = st[:, 2, 0:1]
                        if kind == "W":
                            run(V.tensor_tensor(total, total, st[:, 3, 1:2], ALU.add))
                            run.settle()
                        run(V.reciprocal(st[:, 2, 1:2], total))
                        run.settle()
                        if kind == "G":
                            signal = emptied("s", 2 + l, u)
                            run(V.tensor_scalar(S[:, u % 2, 0:n], S[:, u % 2, 0:n], st[:, 2, 1:2], None, ALU.mult), signal)
                            run.settle()
                            run(V.tensor_copy(small[:, 4:5], small[:, 4:5]), probs_scaled.by(2 + l, u))
                        else:
                            run(V.tensor_scalar(S[:, u % 2, 0:n], S[:, u % 2, 0:n], st[:, 2, 1:2], None, ALU.mult),
                                probs_scaled.by(2 + l, u))
                for key in ended_in[(2 + l, len(U))]:
                    take_features(l, key)
                run.settle()
                for b in range(len(U)):
                    dve.wait_ge(*emptied("o", 2 + l, b))

            def add_gated(l, n, tiles, gate_b):
                for c in range(2):
                    for t in tiles:
                        key = ("out2", l, c, t)
                        splits.due(*key)
                        cols = slice(c * 512, (c + 1) * 512)
                        dve.wait_ge(*filled(*key))
                        w = work[:, t * 512:(t + 1) * 512]
                        run(V.tensor_tensor(w, bank(*key)[:, :], gate_b[:, t // 2, cols], ALU.mult), emptied(*key))
                        run.settle()
                        run(V.tensor_tensor(X[:, t, cols], X[:, t, cols], w, ALU.add),
                            x_added.by(n) if c and t == tiles[-1] else None)

            run(V.memset(small[:, 3:5], 0.0))
            modulation(0, ada_row, gate_row, ada_bias)
            norm_finish(5, T4, xn2)
            modulated_evacuate(5, mod_tmp)
            heads_norm(0, 0, q2, T4, QH, 0, True, None, [("in2", 0, 0, t) for t in range(T4)],
                       [("in2", 0, 1, T4 - 1)])
            heads_norm(0, 1, kv2[:, :, 0:KVH * DH], T4, KVH, 1, True, k2d, [("in2", 0, 1, t) for t in range(T4)])
            for key in ended_in[(2, "before")]:
                take_features(0, key)
            attention2(0)
            run(V.tensor_tensor(oT2, oT2, ag, ALU.mult), out_gated.by("o2"))
            run(V.tensor_tensor(uc[:, 8:12, :], uc[:, 8:12, :], hg, ALU.mult), silu_used.by(0))
            run.settle()
            take_low(oT2r, slice(None), oT2, low_ready.by("o2"), "o2")
            run.settle()

            dve.wait_ge(filter_loaded, FILTERS * 16)
            for n in range(2):
                a, k = hidden[0:HID, n, :], work[0:HID, 0:SEQ]
                dve.wait_ge(*filled("f", n))
                run(V.tensor_scalar(a, bank("f", n)[0:HID, 0:SEQ], hid[:, n:n + 1], hid[:, 2:3], ALU.add, ALU.mult), emptied("f", n))
                run.settle()
                run(V.tensor_scalar(k, a, 1.0 / TWO_PI, ROUND, ALU.mult, ALU.add))
                run.settle()
                run(V.tensor_scalar(k, k, ROUND, None, ALU.subtract))
                run.settle()
                run(V.scalar_tensor_tensor(out=a, in0=k, scalar=-TWO_PI_HI, in1=a, op0=ALU.mult, op1=ALU.add))
                run.settle()
                run(V.scalar_tensor_tensor(out=a, in0=k, scalar=-TWO_PI_LO, in1=a, op0=ALU.mult, op1=ALU.add))
                run.settle()
                run(V.tensor_scalar(a, a, PI_IN, -PI_IN, ALU.min, ALU.max), sin_in_range.by(n))
                run.settle()
            sq = work.rearrange("p (a n) -> p a n", a=4)
            for od in range(2):
                for d in range(2):
                    for t in range(TILES):
                        dve.wait_ge(*filled("tap", od, d, t))
                        run(V.tensor_tensor(taps[:, d, t, :], bank("tap", od, d, t)[:, :], decay[:, t, :], ALU.mult), emptied("tap", od, d, t))
                run.settle()
                run(V.memset(taps[0:1, 1, 0, :], 0.0))
                run.settle()
                if od:
                    dve.wait_ge(*filled("energy", 0))
                    dve.wait_ge(*filled("nyq", 0))
                for d in range(2):
                    for t in range(TILES):
                        run(V.tensor_tensor(sq[:, 2 * d + t, :], taps[:, d, t, :], taps[:, d, t, :], ALU.mult),
                            taps_squared.by(od) if d and t else None)
                run(V.tensor_tensor(taps_sd[:, 0], taps[:, 0], taps[:, 1], ALU.add))
                run(V.tensor_tensor(taps_sd[:, 1], taps[:, 0], taps[:, 1], ALU.subtract), taps_mixed.by(od))
                dve.wait_ge(*taps_guess.at(od))
                v, y, t_ = rn[:, 1, :], rn[:, 0, :], taps[:, 0, 0, :]
                run.settle()
                run(V.tensor_scalar(v, bank("energy", od)[:, :], EPS, None, ALU.add), emptied("energy", od))
                run.settle()
                newton(v, y, t_)
                run(V.tensor_tensor(y, y, t_, ALU.mult))
                run.settle()
                for m in range(2):
                    dve.wait_ge(*filled("spec", od, m, 0))
                    run(V.tensor_tensor(spec_a[:, od, m, :], bank("spec", od, m, 0)[:, :], y, ALU.mult), emptied("spec", od, m, 0))
                    dve.wait_ge(*filled("spec", od, m, 1))
                    run(V.tensor_tensor(spec_b[:, od, m, :], bank("spec", od, m, 1)[:, :], y, ALU.mult), emptied("spec", od, m, 1))
                    run.settle()
                    run(V.tensor_tensor(spec_a[:, od, m, :], spec_a[:, od, m, :], skip_b[:, od, :], ALU.add))
                run(V.memset(spec_b[0:1, od, 0, :], 0.0))
                dve.wait_ge(*filled("nyq", od))
                run(V.tensor_tensor(spec_c[0:1, od, :], bank("nyq", od)[0:1, :], y[0:1, :], ALU.mult), emptied("nyq", od))
                run.settle()
                run(V.tensor_tensor(spec_c[0:1, od, :], spec_c[0:1, od, :], skip_b[0:1, od, :], ALU.add), spectra_ready.by(od))
                run.settle()
            for c in range(0, 8, 2):
                dst = (Z, G1)[c // 4][:, :, c % 4 * P:(c % 4 + 1) * P]
                dve.wait_ge(*filled("zg", c))
                run(V.tensor_copy(dst, bank("zg", c)[:, :].rearrange("p (t n) -> p t n", t=T4)), emptied("zg", c))

            for od in range(2):
                for s in range(2):
                    y = spectrum(s)
                    if od:
                        for n in range(2):
                            dve.wait_ge(*filled("z1", s, n))
                    for m in range(2):
                        zr, zi = bank("zf", od, s, m, 0), bank("zf", od, s, m, 1)
                        a, b = spec_a[:, od, m, :], spec_b[:, od, m, :]
                        re, im = y[:, m, :], y[:, 2 + m, :]
                        t0, t1 = spec_tmp[:, 0, :], spec_tmp[:, 1, :]
                        dve.wait_ge(*filled("zf", od, s, m, 0))
                        dve.wait_ge(*filled("zf", od, s, m, 1))
                        run(V.tensor_tensor(re, zr[:, :], a, ALU.mult))
                        run(V.tensor_tensor(im, zr[:, :], b, ALU.mult), emptied("zf", od, s, m, 0))
                        run(V.tensor_tensor(t0, zi[:, :], b, ALU.mult))
                        run(V.tensor_tensor(t1, zi[:, :], a, ALU.mult))
                        run.settle()
                        run(V.tensor_tensor(re, re, t0, ALU.subtract))
                        run(V.tensor_tensor(im, im, t1, ALU.add))
                        run.settle()
                        if m == 0:
                            run(V.tensor_tensor(im[0:1, :], zi[0:1, :], spec_c[0:1, od, :], ALU.mult), emptied("zf", od, s, m, 1))
                            run.settle()
                        else:
                            run(V.tensor_copy(small[:, 5:6], zi[:, 0:1]), emptied("zf", od, s, m, 1))
                            run.settle()
                    run(V.tensor_copy(small[:, 5:6], small[:, 4:5]), spectrum_ready.by(od, s))
                for s in range(2):
                    if od == 0:
                        for t in range(TILES):
                            dve.wait_ge(*filled("z1", s, t))
                            run(V.tensor_tensor(Z[:, 2 * s + t, :], bank("z1", s, t)[:, :], G1[:, 2 * s + t, :], ALU.mult), emptied("z1", s, t))
                    else:
                        for c2 in range(2):
                            cols = slice(s * SEQ, (s + 1) * SEQ)
                            dve.wait_ge(*filled("y2", s, c2))
                            y3 = y_tmp[:, c2, :].rearrange("p (a n) -> p a n", a=2)
                            run(V.tensor_tensor(y3, bank("y2", s, c2)[:, :].rearrange("p (a n) -> p a n", a=2),
                                                uc[:, 8 + 2 * c2:10 + 2 * c2, cols], ALU.mult), emptied("y2", s, c2))
                            run.settle()
                            run(V.tensor_copy(small[:, 5:6], small[:, 4:5]), out_gated.by("y", s, c2))
                        for c2 in range(2):
                            y3 = y_tmp[:, c2, :].rearrange("p (a n) -> p a n", a=2)
                            k = slice(2 * c2, 2 * c2 + 2)
                            dve.wait_ge(*high_done["y", s, c2])
                            run(V.tensor_tensor(yThr[:, 1, k, cols], y3, yThr[:, 0, k, cols].bitcast(F32), ALU.subtract),
                                low_ready.by("y") if s and c2 else None)
                        run.settle()
            add_gated(0, 5, list(range(T4)), gate_b0)
            run.settle()

            modulation(1, ada_row3, ada_row3[:, 2 * D:3 * D], ada_bias3)
            norm_finish(6, T4, xn3)
            modulated_evacuate(6, mod_tmp3)
            heads_norm(1, 0, wq, TILES, QH, 2, True, None, [("in2", 1, 0, t) for t in range(TILES)],
                       [("in2", 1, 3, T4 - 1)])
            heads_norm(1, 1, kv3[:, :, 0:KVH * DH], T4, KVH, 3, True, k3d, [("in2", 1, 1, t) for t in range(T4)])
            heads_norm(1, 2, nq, TILES, QH, 4, False, None, [("in2", 1, 2, t) for t in range(TILES)],
                       [("in2", 1, 4, T4 - 1)])
            heads_norm(1, 3, nk, T4, QH, 5, False, None, [("in2", 1, 3, t) for t in range(T4)])
            dve.wait_ge(bias_loaded, BIASES * 16)
            dve.wait_ge(bias_masked, 1)
            attention2(1)
            run(V.tensor_tensor(oT3, oT3, wgT, ALU.mult))
            run(V.tensor_tensor(yT3, yT3, ngT, ALU.mult), out_gated.by("3"))
            run.settle()
            dve.wait_ge(*high_done["3",])
            run(V.tensor_tensor(oT3r[:, 1], oT3, oT3r[:, 0].bitcast(F32), ALU.subtract))
            run(V.tensor_tensor(yT3r[:, 1], yT3, yT3r[:, 0].bitcast(F32), ALU.subtract), low_ready.by("3"))
            add_gated(1, 6, [0, 1], gate_b1)

        @block.gpsimd
        def _(pool):
            run = Steps(pool, pool_step)
            G = nc.gpsimd
            n = QH * REL_R
            run(G.memset(rel_pad[0:n, :], 0.0))
            run.settle()
            pool.dma_start(rel_pad[0:n, GRID_W - NA_COLS:GRID_W - NA_COLS + REL_C],
                           A["nat_rpb_2"][0].rearrange("h r c -> (h r) c")).then_inc(rel_loaded, 16)
            pool.wait_ge(rel_loaded, 16)
            for c in range(GRID_W):
                run(G.tensor_copy(rel_toep[0:n, c, :], rel_pad[0:n, GRID_W - 1 - c:2 * GRID_W - 1 - c]))
            run.settle()
            pool.dma_start(rel_rows.rearrange("c n k -> n c k"), rel_toep[0:n, :, :]).then_inc(rel_stored, 16)
            pool.wait_ge(rel_stored, 16)
            pool.wait_ge(*merged_ready.at(1))
            pool.dma_start(final_g, A["norm_final"].partition_broadcast(P)).then_inc(final_g_loaded, 16)
            pool.dma_start(fourier_fwd.rearrange("p a b n -> p (a b n)"), C["fourier"][:, 0:4 * SEQ]).then_inc(late_loaded, 16)
            pool.wait_ge(*x_added.at(3))
            pool.dma_start(ada_bias[0:2, :], A["b_ada_2"][0].partition_broadcast(2)).then_inc(late_loaded, 16)
            pool.wait_ge(*silu_used.at(0))
            pool.wait_ge(*low_ready.at("o2"))
            for u in range(len(units_of_block2(0))):
                pool.wait_ge(*filled("o", 2, u))
            w3v = A["hy_w3_2"][0].rearrange("k (o d n) -> k o d n", o=2, d=2)
            for dst, src in ((w3[0:HID, :, :, :].rearrange("k o d n -> k (o d n)"), A["hy_w3_2"][0]),
                             (skip_b.rearrange("p o n -> p (o n)"), A["hy_skip_2"][0].rearrange("o n -> (o n)").partition_broadcast(P)),
                             (fourier_inv.rearrange("p a b n -> p (a b n)"), C["fourier"][:, 4 * SEQ:8 * SEQ]),
                             (decay.rearrange("p t n -> p (t n)"), C["decay"]),
                             (positions, C["positions"]), (hyena_w1, A["hy_w1_2"][0]), (hyena_w2, A["hy_w2_2"][0])):
                pool.dma_start(dst, src).then_inc(filter_loaded, 16)
            for s in range(2):
                for c2 in range(2):
                    pool.wait_ge(*emptied("y2", s, c2))
            pool.dma_start(ada_bias3[0:2, :], A["b_ada_2"][1].partition_broadcast(2)).then_inc(ada_bias_loaded, 16)
            pool.wait_ge(*filled("hT", 6, 7))
            for r in range(ROWS):
                part = slice(r % 2 * GRID_W, (r % 2 + 1) * GRID_W)
                src = rel_rows.rearrange("c (h r) k -> c h r k", h=QH)[:, :, NA_ROWS - 1 - r:NA_ROWS - 1 - r + ROWS, :]
                pool.dma_start(rel_bias[part, r // 2, :, :], src.rearrange("c h r k -> c h (r k)")).then_inc(bias_loaded, 16)
            pool.dma_start(mask_w.rearrange("p t n -> p (t n)"), C["mask_w"]).then_inc(bias_loaded, 16)
            pool.dma_start(mask_n, C["mask_n"]).then_inc(bias_loaded, 16)
            pool.wait_ge(bias_loaded, BIASES * 16)
            for t in range(TILES):
                for h in range(QH):
                    b = rel_bias[:, t, h, :].rearrange("p (r c) -> p r c", r=ROWS)
                    ins = G.tensor_tensor(b, b, mask_n.unsqueeze(1).to_broadcast([P, ROWS, GRID_W]), ALU.add)
            ins.then_inc(bias_masked, 1)

        @block.sync
        def _(sp):
            x_rows = A["x"][0].rearrange("(t p) n -> p t n", p=P)
            sp.dma_start(X[:, 0:TILES, :], x_rows).then_inc(x_loaded, 16)
            loads = [(ident[:, :], C["ident"]), (tri, C["tri"]), (rope_a[:, :, :].rearrange("p t n -> p (t n)"), C["rope_a"]),
                     (mask_a.rearrange("p g n -> p (g n)"), C["mask_a"]), (mask_b, C["mask_b"]),
                     (mask_c.rearrange("p a n -> p (a n)"), C["mask_c"]),
                     (rope_b[:, :, :].rearrange("p t n -> p (t n)"), C["rope_b"]),
                     (select[:, :, :].rearrange("p t n -> p (t n)"), C["select"]),
                     (sink[:, :], A["win_sink_2"][0].partition_broadcast(P))]
            for n, name in enumerate(("norm_mix", "norm_mlp", "norm_g_2")):
                for l in range(LAYERS):
                    loads.append((g_cols[:, n, l, :], A[name][l].rearrange("(k p) -> p k", p=P)))
            loads.append((cond[:, :, 0], A["c_2"][0].rearrange("(k p) -> p k", p=P)))
            loads.append((cond[:, :, 1], A["c_ctx_2"].rearrange("(k p) -> p k", p=P)))
            for n, name in enumerate(("glob_q", "glob_k", "win_q", "win_k", "nat_q", "nat_k")):
                loads.append((head_gain[:, n, :], A[name + "_norm_2"][0].partition_broadcast(P)))
            for n in range(3):
                loads.append((conv_w[:, n, :], A["hy_conv_w_2"][0, n].rearrange("(c p) -> p c", p=P)))
            loads.append((conv_w[:, 3, :], A["hy_conv_b_2"][0].rearrange("(c p) -> p c", p=P)))
            for n, name in enumerate(("hy_b1_2", "hy_b2_2", "hy_freq_2")):
                loads.append((hid[:, n:n + 1], A[name].rearrange("a n -> n a")))
            assert len(loads) == CONSTS, len(loads)
            with nc.allow_non_contiguous_dma("small vectors, once"):
                for dst, src in loads:
                    sp.dma_start(dst, src).then_inc(consts_loaded, 16)
            sp.dma_start(X[:, TILES:T4, :], A["ctx_2"][0].rearrange("(t p) n -> p t n", p=P)).then_inc(x_loaded, 16)
            rows = lambda w: w.rearrange("(k p) n -> p k n", p=P)
            for n, key in enumerate(HALVES):
                name, l, c, h = key
                s = n % SLOTS
                if n >= SLOTS:
                    m = n - SLOTS
                    if m in half_used:
                        sp.wait_ge(*half_used[m])
                    else:
                        sp.wait_ge(split_ready, quarter_at[HALVES[m] + (1,)] + 1)
                cols = slice(c * 512, (c + 1) * 512)
                dst = raw[:, s, :].rearrange("p (k n) -> p k n", k=4)
                if name == "out":
                    parts = ((("w_out_a", 0, 2, 0), ("w_out_b", 0, 2, 2)), (("w_out_b", 2, 3, 0), ("w_out_c", 0, 3, 1)))[h]
                    for w, k0, k1, at_k in parts:
                        sp.dma_start(dst[:, at_k:at_k + k1 - k0, :], rows(A[w][l, k0 * P:k1 * P, cols])).then_inc(half_loaded[s], 16)
                    continue
                if name == "down":
                    dst, src = raw[:, s, :].rearrange("p (k n) -> p k n", k=2), rows(A["w_down"][l, (2 * c + h) * 2 * P:(2 * c + h + 1) * 2 * P, :])
                    sp.dma_start(dst, src).then_inc(half_loaded[s], 16)
                    continue
                w = A[{"in": "w_in", "o": "w_o", "up": "w_up", "ada": "w_ada_2", "in2": "w_in_2", "out2": "w_out_2"}[name]][l]
                a, b = IN2[c] if name == "in2" else (c * 512, (c + 1) * 512)
                if by_features(key):
                    for q in range(2):
                        f = a + (2 * h + q) * P
                        sp.dma_start(raw[:, s, q * QUARTER:(q + 1) * QUARTER].rearrange("p (k n) -> p k n", k=KD),
                                     rows(w[:, f:f + P])).then_inc(half_loaded[s], 16)
                else:
                    dst = raw[:, s, 0:4 * (b - a)].rearrange("p (k n) -> p k n", k=4)
                    sp.dma_start(dst, rows(w[4 * h * P:4 * (h + 1) * P, a:b])).then_inc(half_loaded[s], 16)
            sp.wait_ge(*x_added.at(6))
            sp.dma_start(out.rearrange("(t p) n -> p t n", p=P), X[:, 0:TILES, :]).then_inc(out_stored, 16)
            sp.wait_ge(out_stored, 16)


INPUTS = ["x", "norm_mix", "w_in", "w_out_a", "w_out_b", "w_out_c", "w_o", "norm_mlp", "w_up", "w_down", "norm_final",
          "c_2", "ctx_2", "c_ctx_2", "norm_g_2", "w_ada_2", "b_ada_2", "w_in_2", "w_out_2", "glob_q_norm_2",
          "glob_k_norm_2", "hy_conv_w_2", "hy_conv_b_2", "hy_w1_2", "hy_b1_2", "hy_w2_2", "hy_b2_2", "hy_freq_2",
          "hy_w3_2", "hy_skip_2", "win_q_norm_2", "win_k_norm_2", "win_sink_2", "nat_q_norm_2", "nat_k_norm_2",
          "nat_rpb_2"]


def kernel(**inputs):
    import concourse.bacc as bacc
    from concourse.bass_utils import run_bass_kernel_spmd

    nc = bacc.Bacc("TRN2", target_bir_lowering=False, num_devices=1)
    arrays, A, C = {}, {}, {}
    for name in INPUTS:
        arrays["in_" + name] = np.ascontiguousarray(inputs[name])
        A[name] = nc.dram_tensor("in_" + name, arrays["in_" + name].shape, F32, kind="ExternalInput").ap()
    for name, a in constants().items():
        arrays["const_" + name] = a
        C[name] = nc.dram_tensor("const_" + name, a.shape, F32, kind="ExternalInput").ap()
    out = nc.dram_tensor("out_dram", (SEQ, D), F32, kind="ExternalOutput").ap()
    two_blocks(nc, A, C, out)
    r = run_bass_kernel_spmd(nc, [arrays], core_ids=[0])
    return np.asarray(r.results[0]["out_dram"]).reshape(1, SEQ, D)
```

```python
import math
from contextlib import ExitStack

import numpy as np

import concourse.bass as bass
from concourse import mybir

F32 = mybir.dt.float32
F32R = mybir.dt.float32r
ACT = mybir.ActivationFunctionType
ALU = mybir.AluOpType
AX_X = mybir.AxisListType.X

P = 128
SEQ = 256
D = 1024
KD = D // P
TILES = SEQ // P
DH = 64
SCALE = DH ** -0.5
EPS = 1e-6
NEG = -1e30
LAYERS = 2
HEADS = 24
MIX = HEADS * DH
ROT = 18
ROPE = 16
N_A, N_B, N_C = 4, 6, 6
GROUPS_A = ((128, 1), (512, 4), (2048, 16))
G_A = len(GROUPS_A)
FF = 4096
CTX = 256
T4 = (SEQ + CTX) // P
N4 = T4 * P
QH = 8
KVH = 2
GW = QH * DH
IN2 = [(0, 512), (512, 768), (768, 1280), (1280, 1792), (1792, 2304), (2304, 2816), (2816, 3328)]
HY = 512
HY_CH = 3 * HY // P
HID, EMB = 64, 33
NA_ROWS, NA_COLS, GRID_W = 8, 16, 64
ROWS = SEQ // GRID_W
REL_R, REL_C = 2 * NA_ROWS - 1, 2 * NA_COLS - 1
TWO_PI = 2.0 * math.pi
TWO_PI_HI = float(np.float32(6.28125))
TWO_PI_LO = float(np.float32(TWO_PI - 6.28125))
ROUND = 1.5 * 2.0 ** 23
PI_IN = float(np.nextafter(np.float32(math.pi), np.float32(0)))

HALF, QUARTER = 2048, 1024
SLOTS = 4
SPLITS = 4
BANKS = 8
ANY_BANK = tuple(range(BANKS))
ATTENTION_BANKS = (0, 1, 2, 3, 4)
GATE_BANKS = (5, 6, 7)
CONSTS = 8 + 5 + 2 + 6 + 4 + 3
BIASES = ROWS + 2


def constants():
    f = np.float32
    i = np.arange(P)
    c = {"ident": np.eye(P, dtype=f)}
    c["tri"] = (i[:, None] >= i[None, :]).astype(f)
    off = i[:, None] + P - i[None, :]
    on = i[:, None] - i[None, :]
    mask_a = np.zeros((P, G_A, 2, P), f)
    for g, (w, d) in enumerate(GROUPS_A):
        for b, dist in enumerate((off, on)):
            ok = (dist >= 0) & (dist <= w) & (dist % d == 0)
            mask_a[:, g, b] = np.where(ok, 0, NEG)
    c["mask_a"] = mask_a.reshape(P, -1)
    causal = np.where(on >= 0, 0, NEG)
    c["mask_b"] = np.concatenate([np.zeros((P, P)), causal], 1).astype(f)
    strict = np.where(i[None, :] > i[:, None], 0, NEG)
    c["mask_c"] = np.concatenate([strict, np.zeros((P, P)), strict], 1).astype(f)
    pos = np.arange(SEQ, dtype=f)
    inv = np.exp(f(-math.log(500000.0)) * np.arange(0, ROPE, 2, dtype=f) / f(ROPE)).astype(f)
    ang = (pos[:, None] * inv).astype(f).astype(np.float64)
    table = np.concatenate([np.cos(ang), np.sin(ang)], 1).astype(f)
    c["rope_a"] = np.concatenate([table[:P], table[P:]], 1)
    row, col = (np.arange(SEQ) // GRID_W).astype(f), (np.arange(SEQ) % GRID_W).astype(f)
    inv = (f(10000.0) ** (-np.arange(16, dtype=f) / f(16))).astype(f)
    ang = np.concatenate([row[:, None] * inv, col[:, None] * inv], 1).astype(f).astype(np.float64)
    table = np.concatenate([np.cos(ang), np.sin(ang)], 1).astype(f)
    c["rope_b"] = np.concatenate([table[:P], table[P:]], 1)
    sel = np.zeros((2, 2, P), f)
    sel[0, 0] = sel[1, 1] = 1
    c["select"] = sel.reshape(2, -1)
    near0 = np.where(i[None, :] <= i[:, None], 0, NEG)
    near1 = np.where(i[:, None] <= i[None, :], 0, NEG)
    z = np.zeros((P, P))
    c["mask_w"] = np.concatenate([z, near0, near1, z], 1).astype(f)
    gc = i % GRID_W
    c0 = np.clip(gc - NA_COLS // 2, 0, GRID_W - NA_COLS)
    k = np.arange(GRID_W)
    c["mask_n"] = np.where((k >= c0[:, None]) & (k < c0[:, None] + NA_COLS), 0, NEG).astype(f)
    t = np.arange(SEQ)
    theta = TWO_PI * ((t[:, None] * t[None, :]) % (2 * SEQ)) / (2 * SEQ)
    alt = np.where(t % 2, -1.0, 1.0)
    fc, fs = np.cos(theta), -np.sin(theta)
    fs[:, 0] = alt
    gcos, gsin = 2 * np.cos(theta) / (2 * SEQ), -2 * np.sin(theta) / (2 * SEQ)
    gcos[0] /= 2
    gsin[0] = alt / (2 * SEQ)
    c["fourier"] = np.concatenate([m[h * P:(h + 1) * P] for m in (fc, fs, gcos, gsin) for h in (0, 1)], 1).astype(f)
    tt = np.linspace(0.0, 1.0, SEQ, dtype=f)[:, None]
    bands = (EMB - 1) // 2
    w = (f(TWO_PI) * np.arange(SEQ, dtype=f)[:, None] / f(SEQ)).astype(f)
    fr = np.linspace(1e-4, bands - 1, bands, dtype=f)[None]
    a = (fr * w).astype(f).astype(np.float64)
    c["positions"] = np.ascontiguousarray(np.concatenate([tt, np.cos(a), -np.sin(a)], 1).astype(f).T)
    deltas = np.linspace(math.log(1e-2) / 1.5, math.log(1e-2) / 0.3, HY, dtype=f)
    decay = np.exp((-tt * np.abs(deltas)).astype(f)).astype(f)
    c["decay"] = np.concatenate([decay[:P], decay[P:]], 1)
    return {n: np.ascontiguousarray(a.astype(f)) for n, a in c.items()}


def units_of_block1():
    soft = [("A", s, t) for s in range(N_A) for t in range(TILES)]
    soft += [("B", b, t) for b in range(N_B) for t in range(TILES)]
    return soft + [("C", c, 0) for c in range(N_C)]


def units_of_block2(layer):
    if layer == 0:
        return [("G", h, t) for h in range(QH) for t in range(T4)]
    return [(k, h, t) for k in ("W", "N") for h in range(QH) for t in range(TILES)]


def half_list():
    slabs = []
    for l in range(LAYERS):
        slabs += [("in", l, c) for c in range(15)]
        slabs += [("out", l, c) for c in range(2)] + [("o", l, c) for c in range(2)]
        slabs += [("up", l, c) for c in range(8)] + [("down", l, c) for c in range(8)]
    for l in range(LAYERS):
        slabs += [("ada", l, c) for c in range(6)] + [("in2", l, c) for c in range(7)]
        slabs += [("out2", l, c) for c in range(2)]
    return [s + (h,) for s in slabs for h in range(2)]


def by_features(key):
    return key[0] == "up" or (key[0] == "in2" and key[2] >= (2 if key[1] == 0 else 5))


class Signal:

    def __init__(self, sem, keys):
        self.sem = sem
        self.value = {k: n + 1 for n, k in enumerate(keys)}
        self.count = 0

    def at(self, *key):
        return self.sem, self.value[key]

    def by(self, *key):
        self.count += 1
        assert self.value[key] == self.count, (self.sem, key)
        return self.sem, self.count


class Steps:

    def __init__(self, eng, sem):
        self.eng, self.sem, self.n, self.last = eng, sem, 0, None

    def __call__(self, instruction, signal=None):
        if signal is None:
            self.n += 1
            signal = (self.sem, self.n)
        instruction.then_inc(signal[0], 1)
        self.last = signal

    def settle(self):
        self.eng.wait_ge(*self.last)


def two_blocks(nc, A, C, out):
    ctx = ExitStack()
    with ctx:
        def sb(name, shape):
            return ctx.enter_context(nc.sbuf_tensor(name, shape, F32))

        def sem(name):
            return ctx.enter_context(nc.semaphore(name))

        raw = sb("raw", [P, SLOTS, HALF])
        w_high = ctx.enter_context(nc.sbuf_tensor("w_high", [P, SPLITS, QUARTER], F32R))
        w_low = ctx.enter_context(nc.sbuf_tensor("w_low", [P, SPLITS, QUARTER], F32R))
        X = sb("X", [P, T4, D])
        ident = sb("ident", [P, P])
        ones = sb("ones", [P, P])
        rope_a = sb("rope_a", [P, TILES, ROPE])
        g_cols = sb("g_cols", [P, 3, LAYERS, KD])
        stat = sb("stat", [P, 4, 4, 8])
        nstat = sb("nstat", [P, 4, 64])
        small = sb("small", [P, 64])
        rope_b = sb("rope_b", [P, TILES, DH])
        select = sb("select", [2, 2, P])
        eps_col = sb("eps_col", [P, 2])
        ada_t = sb("ada_t", [P, 16, 2])
        gain = sb("gain", [P, KD, 2])
        cond = sb("cond", [P, KD, 2])
        cond_e = sb("cond_e", [P, KD, 2])
        sink = sb("sink", [P, QH])
        sink_neg = sb("sink_neg", [P, QH])
        head_gain = sb("head_gain", [P, 6, DH])
        conv_w = sb("conv_w", [P, 4, HY_CH])
        hid = sb("hid", [HID, 8])
        arena_cols = 31000
        arena_at = (nc.sbuf_base + 31) // 32 * 32
        arena = sb("arena", [P, arena_cols])
        scores_cols, acts_cols = 4 * 768, 4 * KD * SEQ
        acts_r = nc.alloc_sbuf_tensor_at("acts_r", [P, acts_cols], F32R, offset=arena_at + 4 * scores_cols)
        hidden_r = nc.alloc_sbuf_tensor_at("hidden_r", [P, 2 * FF // P * SEQ], F32R,
                                           offset=arena_at + 4 * (scores_cols + acts_cols))
        rel_rows = nc.dram_tensor("rel_rows", (GRID_W, QH * REL_R, GRID_W), F32, kind="Internal").ap()

        def carve(at, *shape, of=arena, start=0):
            n = int(np.prod(shape))
            assert at[0] + n <= arena_cols, (at[0] + n)
            v = of[:, at[0] - start:at[0] - start + n]
            at[0] += n
            if len(shape) == 2:
                v = v.rearrange("p (a b) -> p a b", a=shape[0])
            elif len(shape) == 3:
                v = v.rearrange("p (a b c) -> p a b c", a=shape[0], b=shape[1])
            elif len(shape) == 4:
                v = v.rearrange("p (a b c d) -> p a b c d", a=shape[0], b=shape[1], c=shape[2])
            return v

        at = [0]
        S = carve(at, 2, 768)
        PT = carve(at, 2, 768)
        work = arena[:, 0:2048]
        base = at[0]
        hT = carve(at, 2, KD, SEQ, of=acts_r, start=base)
        o_tok = carve([at[0] + KD * SEQ], TILES, D)
        oT = carve(at, 2, KD, SEQ, of=acts_r, start=base)
        qkv_at = at[0]
        qkv = carve(at, 3, TILES, MIX)
        qT_at = at[0]
        qkT = carve(at, 2, MIX // P, SEQ)
        at = [qkv_at + 2 * FF // P * SEQ]
        mask_a = carve(at, G_A, SEQ)
        mask_b = carve(at, SEQ)
        mask_c = carve(at, 3, P)
        tri = carve(at, P)
        up_tmp = carve([0], 2, 2, 512)
        gates = carve([qkv_at], TILES, 3, D)
        uT = carve([qkv_at], 2, FF // P, SEQ, of=hidden_r, start=qkv_at)
        xn1 = carve([qT_at], TILES, D)
        rope_tmp = carve([qT_at + 4 * D], 4, TILES, ROT, ROPE // 2)
        merged = carve([qT_at + 2 * D], TILES, D)
        gated = carve([qT_at + 4 * D], 2, 512)
        final_g = carve([base + 4 * D], D)
        assert qT_at + 2 * MIX // P * SEQ <= qkv_at + 2 * FF // P * SEQ
        gate_log = carve(at, 2, 512)
        rel_pad = carve([at[0] - 2 * GRID_W], 2 * GRID_W)
        rel_toep = carve([qT_at + 2 * D], GRID_W, GRID_W)
        at = [base]
        hT2 = carve(at, 2, KD, N4, of=acts_r, start=base)
        q_at = at[0]
        q2 = carve(at, T4, GW)
        kv2 = carve(at, T4, 2 * KVH * DH)
        k2d = carve(at, T4, KVH, 2 * DH)
        qT2 = carve(at, QH // 2, N4)
        kT2 = carve(at, KVH, N4)
        uc_at = at[0]
        uc = carve(at, HY_CH, N4)
        ag_at = at[0]
        ag = carve(at, 4, N4)
        hg = carve(at, 4, N4)
        gate_row_at = at[0]
        gate_row = carve(at, D)
        fourier_at = at[0]
        fourier_fwd = carve(at, 2, 2, SEQ)
        o2_tok = carve([q_at], T4, GW)
        oT2 = carve([base], QH // 2, N4)
        xn2 = carve([uc_at], T4, D)
        mod_tmp = carve([uc_at + 4 * D], 2, N4)
        ada_bias = carve([uc_at + 5 * D], 3 * D)
        ada_row = carve([uc_at + 8 * D], 2 * D)
        at = [base]
        Z = carve(at, T4, HY)
        G1 = carve(at, T4, HY)
        taps = carve([base], 2, 2, HY)
        taps_sd = carve([base + 2048], 2, 2, HY)
        yThr = carve([base], 2, 4, N4, of=acts_r, start=base)
        oT2r = carve([base + 4096], 2, 4, N4, of=acts_r, start=base)
        at = [q_at]
        spec_a = carve(at, 2, 2, HY)
        spec_b = carve(at, 2, 2, HY)
        positions = carve([N4], SEQ)[0:EMB, :]
        hyena_w1 = carve([768 + N4], HID)[0:EMB, :]
        hyena_w2 = carve([768 + N4 + HID], HID)[0:HID, :]
        hidden = carve(at, 2, SEQ)
        decay = carve(at, 2, HY)
        fourier_inv = carve(at, 2, 2, SEQ)
        assert at[0] <= q_at + 7 * D
        y_tmp = carve([q_at + 2 * D], 2, N4)
        w3 = carve([ag_at], 2, 2, HY)
        Y1 = carve([ag_at], 4, HY)
        skip_b = carve([ag_at + 2048], 2, HY)
        spec_c = carve([ag_at + 3072], 2, HY)
        Y = carve([0], 4, HY)
        rn = carve([2048], 2, HY)
        spec_tmp = carve([2048], 2, HY)
        gate_b0 = carve([uc_at], 2, D)

        def spectrum(s):
            return (Y, Y1)[s]

        at = [base + 8 * D]
        wq_at = at[0]
        wq = carve(at, TILES, GW)
        nq = carve(at, TILES, GW)
        kv3 = carve(at, T4, 2 * KVH * DH)
        k3d = carve(at, T4, KVH, 2 * DH)
        nk_at = at[0]
        nk = carve(at, T4, GW)
        nv = carve(at, T4, GW)
        wqT = carve(at, QH // 2, SEQ)
        nqT = carve(at, QH // 2, SEQ)
        wkT = carve(at, KVH, N4)
        nkT = carve(at, QH // 2, N4)
        wgT = carve([nk_at], 4, SEQ)
        ngT = carve([nk_at + 1024], 4, SEQ)
        gate_b1 = carve(at, 1, D)
        bias_at = at[0]
        rel_bias = carve(at, TILES, QH, SEQ)
        mask_w = carve(at, TILES, SEQ)
        mask_n = carve(at, GRID_W)
        no_mask = carve(at, SEQ)
        o3_tok = carve([wq_at], TILES, GW)
        y3_tok = carve([wq_at + 1024], TILES, GW)
        oT3 = carve([base + 4096], 4, SEQ)
        yT3 = carve([base + 5120], 4, SEQ)
        oT3r = carve([base], 2, 4, SEQ, of=acts_r, start=base)
        yT3r = carve([base + 2048], 2, 4, SEQ, of=acts_r, start=base)
        xn3 = carve([bias_at], T4, D)
        mod_tmp3 = carve([wq_at], 2, N4)
        ada_row3 = carve([nk_at], 3 * D)
        ada_bias3 = carve([uc_at + 2 * D], 3 * D)

        banks = [ctx.enter_context(nc.psum_tensor(f"bank{b}", [P, 512], F32)) for b in range(BANKS)]

        bank_filled = [sem(f"bank_filled{b}") for b in range(BANKS)]
        bank_emptied = [sem(f"bank_emptied{b}") for b in range(BANKS)]
        half_loaded = [sem(f"half_loaded{s}") for s in range(SLOTS)]
        high_ready = sem("high_ready")
        split_ready = sem("split_ready")
        quarter_used = sem("quarter_used")
        high_taken = sem("high_taken")
        x_loaded = sem("x_loaded")
        context_loaded = sem("context_loaded")
        first_loaded = sem("first_loaded")
        consts_loaded = sem("consts_loaded")
        fourier_loaded = sem("fourier_loaded")
        ada_loaded = sem("ada_loaded")
        final_g_loaded = sem("final_g_loaded")
        hidden_loaded = sem("hidden_loaded")
        tables_loaded = sem("tables_loaded")
        w3_loaded = sem("w3_loaded")
        skip_loaded = sem("skip_loaded")
        bias_loaded = sem("bias_loaded")
        ada_bias_loaded = sem("ada_bias_loaded")
        rel_loaded = sem("rel_loaded")
        rel_stored = sem("rel_stored")
        out_stored = sem("out_stored")
        vector_step = sem("vector_step")
        scalar_step = sem("scalar_step")
        NORMS = range(7)
        b1u = [(l, u) for l in range(LAYERS) for u in range(len(units_of_block1()))]
        b2u = [(2 + l, u) for l in range(LAYERS) for u in range(len(units_of_block2(l)))]
        kinds = {(l, u): units_of_block1()[u][0] for l, u in b1u}
        kinds |= {(l, u): units_of_block2(l - 2)[u][0] for l, u in b2u}
        softs = [k for k in b1u + b2u if kinds[k] != "C"]
        sticks = [k for k in b1u if kinds[k] == "C"]
        ones_set = sem("ones_set")
        x_added = Signal(sem("x_added"), [(n,) for n in range(8)])
        rstd_ready = Signal(sem("rstd_ready"), [(n,) for n in NORMS])
        xn_by_vector = Signal(sem("xn_by_vector"), [(n,) for n in NORMS if n != 4])
        qk_roped = Signal(sem("qk_roped"), [(l, j) for l in range(LAYERS) for j in range(2)])
        bias_ready = Signal(sem("bias_ready"), softs)
        sum_inverted = Signal(sem("sum_inverted"), softs)
        stick_summed = Signal(sem("stick_summed"), sticks)
        merged_ready = Signal(sem("merged_ready"), [(l, c) for l in range(LAYERS) for c in range(2)])
        heads_squared = Signal(sem("heads_squared"), [(l, j) for l, n in ((0, 2), (1, 4)) for j in range(n)])
        heads_ready = Signal(sem("heads_ready"), [(l, j) for l, n in ((0, 2), (1, 4)) for j in range(n)])
        cond_ready = sem("cond_ready")
        cond_ready_s = Signal(cond_ready, [("sum",), ("done",)])
        ada_ready = Signal(sem("ada_ready"), [(l,) for l in range(LAYERS)])
        sin_in_range = Signal(sem("sin_in_range"), [(0,), (1,)])
        taps_squared = Signal(sem("taps_squared"), [(0,), (1,)])
        taps_mixed = Signal(sem("taps_mixed"), [(0,), (1,)])
        spectra_ready = Signal(sem("spectra_ready"), [(0,), (1,)])
        silu_used = Signal(sem("silu_used"), [(0,)])
        pool_step = sem("pool_step")
        bias_masked = sem("bias_masked")
        spectrum_ready = Signal(sem("spectrum_ready"), [(o, s) for o in range(2) for s in range(2)])
        rsqrt_guess = Signal(sem("rsqrt_guess"), [(n,) for n in NORMS])
        xn_by_scalar = Signal(sem("xn_by_scalar"), [(n,) for n in NORMS if n != 4])
        probs_ready = Signal(sem("probs_ready"), [k for k in softs if kinds[k] != "G"])
        softplus_part = Signal(sem("softplus_part"), sticks)
        stick_weights = Signal(sem("stick_weights"), sticks)
        heads_guess = Signal(sem("heads_guess"), [(l, j) for l, n in ((0, 2), (1, 4)) for j in range(n)])
        cond_exp = Signal(sem("cond_exp"), [(0,)])
        sin_ready = Signal(sem("sin_ready"), [(0,), (1,)])
        taps_guess = Signal(sem("taps_guess"), [(0,), (1,)])
        conv_begun = Signal(sem("conv_begun"), [(c,) for c in range(HY_CH)])
        silu_exp = Signal(sem("silu_exp"), [(l, c) for l in range(LAYERS) for c in range(8)])
        gates_of = [(l, n) for l in range(LAYERS) for n in range(6 * TILES)]
        gate_logged = Signal(sem("gate_logged"), gates_of)
        gates_ready = Signal(sem("gates_ready"), gates_of)
        gate_exponent = Signal(sem("gate_exponent"), gates_of)
        up_ready = Signal(sem("up_ready"), [(l, m) for l in range(LAYERS) for m in range(16)])
        low_ready = Signal(sem("low_ready"), [("o2",), ("y",), ("o3",), ("y3",)])
        out_gated = Signal(sem("out_gated"), [("o2",), ("y", 0, 0), ("y", 0, 1), ("y", 1, 0), ("y", 1, 1), ("o3",), ("y3",)])

        number = {}
        uses = [0] * BANKS
        opened = [-1] * BANKS
        HALVES = half_list()
        half_at = {k: n for n, k in enumerate(HALVES)}
        loads_of = [2 if k[0] == "out" or by_features(k) else 1 for k in HALVES]
        quarters = [k + (q,) for k in HALVES if k[0] != "ada" for q in range(2)]
        quarter_at = {k: n for n, k in enumerate(quarters)}
        last_use = {}
        half_used = {}
        ended_in = {}
        logged_by = {}
        high_done = {}
        position = {}

        def bank(*key):
            return banks[number[key][0]]

        def filled(*key):
            b, n = number[key]
            return bank_filled[b], n + 1

        def emptied(*key):
            b, n = number[key]
            return bank_emptied[b], n + 1

        def x_group(name, l, t, c):
            return (name, l, c, t) if name == "wo" else (name, l, t, c)

        def half_is_loaded(n):
            return half_loaded[n % SLOTS], 16 * sum(loads_of[m] for m in range(n % SLOTS, n + 1, SLOTS))

        def probs_at(l, u):
            return emptied("s", l, u) if kinds[l, u] == "G" else probs_ready.at(l, u)

        def raw_quarter(n):
            key = quarters[n]
            h, q = half_at[key[:4]], key[4]
            width = 512 if key[0] == "in2" and key[2] == 1 else QUARTER
            return raw[:, h % SLOTS, q * width:(q + 1) * width], w_high[:, n % SPLITS, 0:width], w_low[:, n % SPLITS, 0:width]

        class Splits:

            def __init__(self, one):
                self.one, self.n = one, 0

            def due(self, *key, ahead=0):
                p = position[key] + ahead
                while self.n < len(quarters) and (self.n < SPLITS or position[self.n - SPLITS] <= p):
                    name, l = quarters[self.n][:2]
                    if name == "in2" and position["ada", l, 5] >= p:
                        return
                    self.one(self.n)
                    self.n += 1

        block = ctx.enter_context(nc.Block())

        @block.tensor
        def _(pe):
            mm, tr = nc.tensor.matmul, nc.tensor.transpose

            counts = {"used": 0, "order": 0}

            def open_bank(*key, among=ANY_BANK):
                b = min(among, key=lambda x: opened[x])
                number[key] = (b, uses[b])
                if uses[b]:
                    pe.wait_ge(bank_emptied[b], uses[b])
                uses[b] += 1
                opened[b] = max(opened) + 1
                return banks[b]

            def close_bank(ins, *key):
                ins.then_inc(filled(*key)[0], 1)
                counts["order"] += 1
                position[key] = counts["order"]

            def split(*key):
                n = quarter_at[key]
                pe.wait_ge(split_ready, n + 1)
                return w_high[:, n % SPLITS, :], w_low[:, n % SPLITS, :]

            def end_quarter(key, ins, *group):
                n = quarter_at[key]
                if group:
                    last_use[n] = filled(*group)
                else:
                    ins.then_inc(quarter_used, 1)
                    counts["used"] += 1
                    last_use[n] = (quarter_used, counts["used"])
                counts["order"] += 1
                position[n] = counts["order"]

            def product(o, left, right, start, stop):
                (lh, ll), (rh, rl) = left, right
                mm(o, lh, rh, start=start, stop=False)
                mm(o, lh, rl, start=False, stop=False)
                return mm(o, ll, rh, start=False, stop=stop)

            def tiles_of(x, width=P):
                return lambda k, t: (x[:, 0, k, t * P:(t + 1) * P], x[:, 1, k, t * P:(t + 1) * P])

            def norm_transposes(n, xn, tiles, per_bank):
                pe.wait_ge(*xn_by_vector.at(n))
                pe.wait_ge(*xn_by_scalar.at(n))
                for b in range(KD // per_bank):
                    o = open_bank("hT", n, b)
                    for kk in range(per_bank):
                        k = b * per_bank + kk
                        for t in range(tiles):
                            c = (kk * tiles + t) * P
                            ins = tr(o[:, c:c + P], xn[:, t, k * P:(k + 1) * P], ident[:, :])
                    close_bank(ins, "hT", n, b)

            def tokens_by_features(slab, name, acts, tiles, width=512, among=ANY_BANK, ready=None):
                group = (name,) + slab[1:]
                o = {}
                for k in range(KD):
                    key = slab + (k // 4, k // 2 % 2)
                    if k % 2 == 0:
                        wh, wl = (w.rearrange("p (k n) -> p k n", k=2) for w in (x[:, 0:2 * width] for x in split(*key)))
                    if ready:
                        pe.wait_ge(*ready(k))
                    for t in tiles:
                        if k == 0:
                            o[t] = open_bank(*group, t, among=among)
                        ins = product(o[t][:, 0:width], acts(k, t), (wh[:, k % 2, :], wl[:, k % 2, :]), k == 0, k == KD - 1)
                        if k == KD - 1:
                            close_bank(ins, *group, t)
                            if name == "gate":
                                ended_in[(slab[1], "at")].append(group + (t,))
                        if k % 2 and t == tiles[-1]:
                            end_quarter(key, ins, *(group + (t,) if k == KD - 1 else ()))
                        yield

            def run(steps):
                for _ in steps:
                    pass

            def advance(steps, n):
                for _ in range(n):
                    if next(steps, "end") == "end":
                        return

            pe.wait_ge(first_loaded, 2 * 16)
            pe.wait_ge(ones_set, 1)
            for l in range(LAYERS):
                norm_transposes(2 * l, xn1, TILES, 2)
                turned = [("qT", l, 0, b) for b in range(6)] + [("qT", l, 1, b) for b in range(6)]
                for c in range(9):
                    turned_token = (lambda k: emptied("hT", 2 * l, k // 2)) if c == 0 else None
                    steps = tokens_by_features(("in", l, c), "qkv", tiles_of(hT), range(TILES), ready=turned_token)
                    if c < 6:
                        run(steps)
                        continue
                    for _ in range(4):
                        advance(steps, 4)
                        key = turned.pop(0)
                        j, b = key[2], key[3]
                        pe.wait_ge(*qk_roped.at(l, j))
                        o = open_bank(*key)
                        for m in range(4):
                            ch, tt = 2 * b + m // 2, m % 2
                            ins = tr(o[:, m * P:(m + 1) * P], qkv[:, j, tt, ch * P:(ch + 1) * P], ident[:, :])
                        close_bank(ins, *key)
                for c in range(6, 9):
                    for t in range(TILES):
                        pe.wait_ge(*emptied("qkv", l, c, t))
                for j in range(2):
                    for b in range(6):
                        pe.wait_ge(*emptied("qT", l, j, b))

                if l == 0:
                    pe.wait_ge(consts_loaded, CONSTS * 16)

                def gate_groups():
                    for c in range(9, 15):
                        yield from tokens_by_features(("in", l, c), "gate", tiles_of(hT), range(TILES), among=GATE_BANKS)

                def head(j, h, cols):
                    half = DH * (h % 2)
                    return qkT[half:half + DH, j, h // 2, cols]

                def scores(u):
                    kind, h, t = U[u]
                    q = slice(t * P, (t + 1) * P)
                    if kind == "A":
                        span = (t + 1) * P
                        o = open_bank("s", l, u, among=ATTENTION_BANKS)
                        for g in range(G_A):
                            hd = g * N_A + h
                            if g == 2 and t == 1:
                                close_bank(ins, "s", l, u)
                                o = open_bank("s2", l, u, among=ATTENTION_BANKS)
                            c = g * span if not (g == 2 and t == 1) else 0
                            ins = mm(o[:, c:c + span], head(0, hd, q), head(1, hd, slice(0, span)), start=True, stop=True)
                        close_bank(ins, "s2" if t else "s", l, u)
                    elif kind == "B":
                        o = open_bank("s", l, u, among=ATTENTION_BANKS)
                        hd = 12 + h
                        ins = mm(o[:, 0:(t + 1) * P], head(0, hd, q), head(1, hd, slice(0, (t + 1) * P)), start=True, stop=True)
                        close_bank(ins, "s", l, u)
                    else:
                        hd = ROT + h
                        o = open_bank("s", l, u, among=ATTENTION_BANKS)
                        mm(o[:, 0:SEQ], head(1, hd, slice(0, P)), head(0, hd, slice(0, SEQ)), start=True, stop=True)
                        ins = mm(o[:, SEQ:SEQ + P], head(1, hd, slice(P, SEQ)), head(0, hd, slice(P, SEQ)), start=True, stop=True)
                        close_bank(ins, "s", l, u)

                def second(u):
                    kind, h, t = U[u]
                    if kind == "C":
                        pe.wait_ge(*stick_summed.at(l, u))
                        sp = PT[:, u % 2, 384:768]
                        o = open_bank("p", l, u, 0, among=ATTENTION_BANKS)
                        mm(o[:, 0:SEQ], tri, sp[:, 0:SEQ], start=True, stop=False)
                        mm(o[:, P:SEQ], ones[:, :], sp[:, SEQ:SEQ + P], start=False, stop=True)
                        ins = mm(o[:, SEQ:SEQ + P], tri, sp[:, SEQ:SEQ + P], start=True, stop=True)
                        close_bank(ins, "p", l, u, 0)
                        return
                    pe.wait_ge(*probs_ready.at(l, u))
                    blocks = (G_A if kind == "A" else 1) * (t + 1)
                    for b0 in range(0, blocks, 4):
                        o = open_bank("p", l, u, b0 // 4, among=ATTENTION_BANKS)
                        for b in range(b0, min(blocks, b0 + 4)):
                            ins = tr(o[:, (b - b0) * P:(b - b0 + 1) * P], S[:, u % 2, b * P:(b + 1) * P], ident[:, :])
                        close_bank(ins, "p", l, u, b0 // 4)

                def values(u):
                    kind, h, t = U[u]
                    v = lambda hd, jt: qkv[:, 2, jt, hd * DH:(hd + 1) * DH]
                    o = None
                    if kind == "C":
                        pe.wait_ge(*stick_weights.at(l, u))
                        o = open_bank("o", l, u, among=ATTENTION_BANKS)
                        a = PT[:, u % 2, 0:384]
                        mm(o[:, 0:DH], a[:, 0:P], v(ROT + h, 0), start=True, stop=True)
                        mm(o[:, DH:2 * DH], a[:, P:SEQ], v(ROT + h, 0), start=True, stop=False)
                        ins = mm(o[:, DH:2 * DH], a[:, SEQ:SEQ + P], v(ROT + h, 1), start=False, stop=True)
                        close_bank(ins, "o", l, u)
                        return
                    blocks = (G_A if kind == "A" else 1) * (t + 1)
                    for b0 in range(0, blocks, 4):
                        pe.wait_ge(*emptied("p", l, u, b0 // 4))
                    o = open_bank("o", l, u, among=ATTENTION_BANKS)
                    for b in range(blocks):
                        g, jt = b // (t + 1), b % (t + 1)
                        hd = g * N_A + h if kind == "A" else 12 + h
                        ins = mm(o[:, 0:DH], PT[:, u % 2, b * P:(b + 1) * P], v(hd, jt), start=b == 0, stop=b == blocks - 1)
                    close_bank(ins, "o", l, u)

                U = units_of_block1()
                filler = gate_groups()
                for u in range(len(U) + 2):
                    ended_in[(l, "at")] = []
                    if u < len(U):
                        scores(u)
                    if 1 <= u <= len(U):
                        second(u - 1)
                    advance(filler, 1000 if u >= len(U) else 3 if U[u][0] == "A" else 4)
                    if u >= 2:
                        values(u - 2)
                    ended_in[(l, u)] = ended_in[(l, "at")]

                for u in range(len(U)):
                    pe.wait_ge(*emptied("o", l, u))
                for b in range(4):
                    o = open_bank("oT", l, b)
                    for m in range(4):
                        k, t = 2 * b + m // 2, m % 2
                        ins = tr(o[:, m * P:(m + 1) * P], o_tok[:, t, k * P:(k + 1) * P], ident[:, :])
                    close_bank(ins, "oT", l, b)
                kinds_k = (range(0, 2), range(2, 5), range(5, 8))

                def turn_merged(c):
                    pe.wait_ge(*merged_ready.at(l, c))
                    for b in range(2 * c, 2 * c + 2):
                        o = open_bank("mT", l, b)
                        for m in range(4):
                            k, t = 2 * b + m // 2, m % 2
                            ins = tr(o[:, m * P:(m + 1) * P], merged[:, t, k * P:(k + 1) * P], ident[:, :])
                        close_bank(ins, "mT", l, b)

                def merged_turned(k):
                    if k == 4:
                        turn_merged(1)
                    return emptied("mT", l, k // 2)

                for c in range(2):
                    for k in range(KD):
                        br = [k in ks for ks in kinds_k].index(True)
                        if c == 0:
                            pe.wait_ge(*emptied("oT", l, k // 2))
                        elif k == 5:
                            turn_merged(0)
                        key = ("out", l, c, k // 4, k // 2 % 2)
                        if k % 2 == 0:
                            wh, wl = (w.rearrange("p (k n) -> p k n", k=2) for w in split(*key))
                        for t in range(TILES):
                            group = ("y", l, c, t, br)
                            first, end = k == kinds_k[br][0], k == kinds_k[br][-1]
                            if first:
                                open_bank(*group)
                            ins = product(bank(*group)[:, :], tiles_of(oT)(k, t), (wh[:, k % 2, :], wl[:, k % 2, :]), first, end)
                            if end:
                                close_bank(ins, *group)
                        if k % 2:
                            end_quarter(key, ins, *(group if end else ()))
                for c in range(2):
                    run(tokens_by_features(("o", l, c), "wo", tiles_of(hT), range(TILES), ready=None if c else merged_turned))

                norm_transposes(2 * l + 1, xn1, TILES, 2)
                for m in range(16):
                    o = open_bank("up", l, m)
                    for j in range(2):
                        key = ("up", l, m // 2, m % 2, j)
                        wh, wl = (w.rearrange("p (k n) -> p k n", k=KD) for w in split(*key))
                        for k in range(KD):
                            if m + j == 0:
                                pe.wait_ge(*emptied("hT", 2 * l + 1, k // 2))
                            ins = product(o[:, j * SEQ:(j + 1) * SEQ], (wh[:, k, :], wl[:, k, :]),
                                          (hT[:, 0, k, :], hT[:, 1, k, :]), k == 0, k == KD - 1)
                        if j:
                            close_bank(ins, "up", l, m)
                        end_quarter(key, ins, *(("up", l, m) if j else ()))
                accs = {(t, c): open_bank("down", l, t, c) for t in range(TILES) for c in range(2)}
                for k in range(FF // P):
                    key = ("down", l, k // 4, k // 2 % 2, k % 2)
                    wh, wl = split(*key)
                    if k % 2 == 0:
                        pe.wait_ge(*up_ready.at(l, k // 2))
                    for t in range(TILES):
                        for c in range(2):
                            cols = slice(c * 512, (c + 1) * 512)
                            ins = product(accs[t, c][:, :], tiles_of(uT)(k, t), (wh[:, cols], wl[:, cols]), k == 0, k == FF // P - 1)
                            if k == FF // P - 1:
                                close_bank(ins, "down", l, t, c)
                    end_quarter(key, ins, *(("down", l, 1, 1) if k == FF // P - 1 else ()))

            def modulation(l, row):
                pe.wait_ge(*cond_ready_s.at("done"))
                for c in range(6):
                    o = open_bank("ada", l, c)
                    for k in range(KD):
                        n = half_at["ada", l, c, k // 4]
                        if k % 4 == 0:
                            pe.wait_ge(*half_is_loaded(n))
                        w = raw[:, n % SLOTS, k % 4 * 512:(k % 4 + 1) * 512]
                        ins = mm(o[0:2, :], cond[:, k, :], w, start=k == 0, stop=k == KD - 1)
                    close_bank(ins, "ada", l, c)
                    half_used[half_at["ada", l, c, 0]] = half_used[half_at["ada", l, c, 1]] = filled("ada", l, c)
                for c in range(6):
                    pe.wait_ge(*emptied("ada", l, c))
                o = open_bank("adaT", l)
                for k in range(16):
                    ins = tr(o[:, 2 * k:2 * k + 2], row[0:2, k * P:(k + 1) * P], ident[0:2, 0:2])
                close_bank(ins, "adaT", l)

            def gate_rows(l, row, sequences):
                for s in range(sequences):
                    for c in range(2):
                        o = open_bank("gateB", l, s, c)
                        ins = mm(o[:, :], select[:, s, :], row[0:2, c * 512:(c + 1) * 512], start=True, stop=True)
                        close_bank(ins, "gateB", l, s, c)

            def project2(l, j, tiles):
                turned_token = (lambda k: emptied("hT", 5 + l, k)) if j == 0 else None
                run(tokens_by_features(("in2", l, j), "in2", tiles_of(hT2), tiles, width=IN2[j][1] - IN2[j][0], ready=turned_token))

            def feature_groups(l, j, n):
                for c in range(4):
                    group, key = ("in2f", l, 4 * (j - 2) + c), ("in2", l, j, c // 2, c % 2)
                    o = open_bank(*group, among=GATE_BANKS)
                    wh, wl = (w.rearrange("p (k n) -> p k n", k=KD) for w in split(*key))
                    for k in range(KD):
                        ins = product(o[:, 0:n], (wh[:, k, :], wl[:, k, :]), (hT2[:, 0, k, 0:n], hT2[:, 1, k, 0:n]),
                                      k == 0, k == KD - 1)
                        if k == KD - 1:
                            close_bank(ins, *group)
                            end_quarter(key, ins, *group)
                            ended_in.setdefault((2 + l, "at"), []).append(group)
                        yield

            def turn_heads(l, j, src, chunks, tiles, per_bank):
                pe.wait_ge(*heads_ready.at(l, j))
                for b in range(chunks // per_bank):
                    o = open_bank("heads", l, j, b)
                    for m in range(per_bank):
                        for t in range(tiles):
                            ins = tr(o[:, (m * tiles + t) * P:(m * tiles + t + 1) * P], src(b * per_bank + m, t), ident[:, :])
                    close_bank(ins, "heads", l, j, b)

            def attention2(l, filler, per_unit):
                U = units_of_block2(l)

                def scores(u):
                    kind, h, t = U[u]
                    half = DH * (h % 2)
                    first = SEQ if kind == "G" and t >= TILES else 0
                    if kind == "G":
                        q, k = qT2, kT2[half:half + DH, h // 4, first:N4]
                    elif kind == "W":
                        q, k = wqT, wkT[half:half + DH, h // 4, :]
                    else:
                        q, k = nqT, nkT[half:half + DH, h // 2, :]
                    o = open_bank("s", 2 + l, u, among=ATTENTION_BANKS)
                    ins = mm(o[:, 0:N4 - first], q[half:half + DH, h // 2, t * P:(t + 1) * P], k, start=True, stop=True)
                    close_bank(ins, "s", 2 + l, u)

                def blocks_of(u):
                    kind, h, t = U[u]
                    return range(2, 4) if kind == "G" and t >= TILES else range(4)

                def second(u):
                    pe.wait_ge(*probs_at(2 + l, u))
                    o = open_bank("p", 2 + l, u, 0, among=ATTENTION_BANKS)
                    for n, _ in enumerate(blocks_of(u)):
                        ins = tr(o[:, n * P:(n + 1) * P], S[:, u % 2, n * P:(n + 1) * P], ident[:, :])
                    close_bank(ins, "p", 2 + l, u, 0)

                def values(u):
                    kind, h, t = U[u]
                    pe.wait_ge(*emptied("p", 2 + l, u, 0))
                    o = open_bank("o", 2 + l, u, among=ATTENTION_BANKS)
                    blocks = blocks_of(u)
                    for n, b in enumerate(blocks):
                        if kind == "G":
                            v = kv2[:, b, (KVH + h // 4) * DH:(KVH + h // 4 + 1) * DH]
                        elif kind == "W":
                            v = kv3[:, b, (KVH + h // 4) * DH:(KVH + h // 4 + 1) * DH]
                        else:
                            v = nv[:, b, h * DH:(h + 1) * DH]
                        ins = mm(o[:, 0:DH], PT[:, u % 2, n * P:(n + 1) * P], v, start=n == 0, stop=n == len(blocks) - 1)
                    close_bank(ins, "o", 2 + l, u)

                for u in range(len(U) + 2):
                    ended_in[(2 + l, "at")] = []
                    if u < len(U):
                        scores(u)
                    if 1 <= u <= len(U):
                        second(u - 1)
                    advance(filler, per_unit(u) if u < len(U) else 1000)
                    if u >= 2:
                        values(u - 2)
                    ended_in[(2 + l, u)] = ended_in[(2 + l, "at")]

            def turn_outputs(l):
                for u in range(len(units_of_block2(l))):
                    pe.wait_ge(*emptied("o", 2 + l, u))
                for b in range(4):
                    o = open_bank("oT", 2 + l, b)
                    for m in range(4):
                        if l == 0:
                            src = o2_tok[:, m, b * P:(b + 1) * P]
                        else:
                            k = 2 * (b % 2) + m // 2
                            src = (o3_tok, y3_tok)[b // 2][:, m % 2, k * P:(k + 1) * P]
                        ins = tr(o[:, m * P:(m + 1) * P], src, ident[:, :])
                    close_bank(ins, "oT", 2 + l, b)

            def out2(l, tiles, first, second, ready=None):
                acts = lambda k, t: tiles_of(first)(k, t) if k < 4 else tiles_of(second)(k - 4, t)
                for c in range(2):
                    run(tokens_by_features(("out2", l, c), "out2", acts, tiles, ready=None if c else ready))

            modulation(0, ada_row)
            norm_transposes(5, xn2, T4, 1)
            project2(0, 0, range(T4))
            project2(0, 1, range(T4))

            def fill0():
                for j in range(2, 7):
                    yield from feature_groups(0, j, N4)

            filler = fill0()
            ended_in[(2, "at")] = []
            advance(filler, 24)
            ended_in[(2, "before")] = ended_in[(2, "at")]
            turn_heads(0, 0, lambda c, t: q2[:, t, c * P:(c + 1) * P], 4, T4, 1)
            turn_heads(0, 1, lambda c, t: k2d[:, t, c, :], KVH, T4, 1)
            for b in range(4):
                pe.wait_ge(*emptied("heads", 0, 0, b))
            for b in range(KVH):
                pe.wait_ge(*emptied("heads", 0, 1, b))
            for t in range(T4):
                pe.wait_ge(*emptied("in2", 0, 1, t))
            attention2(0, filler, lambda u: 4)
            pe.wait_ge(hidden_loaded, 3 * 16)
            o = open_bank("f", 0)
            close_bank(mm(o[0:HID, 0:SEQ], hyena_w1, positions, start=True, stop=True), "f", 0)
            turn_outputs(0)

            pe.wait_ge(*sin_ready.at(0))
            o = open_bank("f", 1)
            close_bank(mm(o[0:HID, 0:SEQ], hyena_w2, hidden[0:HID, 0, :], start=True, stop=True), "f", 1)
            pe.wait_ge(*sin_ready.at(1))
            pe.wait_ge(w3_loaded, 16)
            pe.wait_ge(fourier_loaded, 16)
            pe.wait_ge(tables_loaded, 2 * 16)
            for od in range(2):
                for d in range(2):
                    for t in range(TILES):
                        o = open_bank("tap", od, d, t)
                        ins = mm(o[:, :], hidden[0:HID, 1, t * P:(t + 1) * P], w3[0:HID, od, d, :], start=True, stop=True)
                        close_bank(ins, "tap", od, d, t)
                pe.wait_ge(*taps_squared.at(od))
                o = open_bank("energy", od)
                for n in range(4):
                    ins = mm(o[:, :], ones[:, :], work.rearrange("p (a n) -> p a n", a=4)[:, n, :], start=n == 0, stop=n == 3)
                close_bank(ins, "energy", od)
                pe.wait_ge(*taps_mixed.at(od))
                for m in range(2):
                    for which in range(2):
                        o = open_bank("spec", od, m, which)
                        for t in range(TILES):
                            ins = mm(o[:, :], fourier_fwd[:, which, t, m * P:(m + 1) * P], taps_sd[:, which, t, :], start=t == 0, stop=t == 1)
                        close_bank(ins, "spec", od, m, which)
                o = open_bank("nyq", od)
                for t in range(TILES):
                    ins = mm(o[0:1, :], fourier_fwd[:, 1, t, 0:1], taps_sd[:, 0, t, :], start=t == 0, stop=t == 1)
                close_bank(ins, "nyq", od)
            for c in range(HY_CH):
                pe.wait_ge(*emptied("in2f", 0, c))
            for c in range(8):
                o = open_bank("zg", c)
                for t in range(T4):
                    ins = tr(o[:, t * P:(t + 1) * P], uc[:, c, t * P:(t + 1) * P], ident[:, :])
                close_bank(ins, "zg", c)
            for c in range(8):
                pe.wait_ge(*emptied("zg", c))
            for od in range(2):
                for s in range(2):
                    if od == 1:
                        for t in range(TILES):
                            pe.wait_ge(*emptied("z1", s, t))
                    for m in range(2):
                        for which in range(2):
                            o = open_bank("zf", od, s, m, which)
                            for t in range(TILES):
                                ins = mm(o[:, :], fourier_fwd[:, which, t, m * P:(m + 1) * P], Z[:, 2 * s + t, :], start=t == 0, stop=t == 1)
                            close_bank(ins, "zf", od, s, m, which)
                    if s == 1:
                        inverse_now = (0, 1)
                    else:
                        inverse_now = ()
                    for ss in inverse_now:
                        pe.wait_ge(*spectrum_ready.at(od, ss))
                        if od == 0:
                            for t in range(TILES):
                                o = open_bank("z1", ss, t)
                                for kk in range(4):
                                    ins = mm(o[:, :], fourier_inv[:, kk // 2, kk % 2, t * P:(t + 1) * P], spectrum(ss)[:, kk, :],
                                             start=kk == 0, stop=kk == 3)
                                close_bank(ins, "z1", ss, t)
                        else:
                            for c2 in range(2):
                                o = open_bank("y2", ss, c2)
                                for cc in range(2):
                                    c = 2 * c2 + cc
                                    for kk in range(4):
                                        ins = mm(o[:, cc * SEQ:(cc + 1) * SEQ], spectrum(ss)[:, kk, c * P:(c + 1) * P],
                                                 fourier_inv[:, kk // 2, kk % 2, :], start=kk == 0, stop=kk == 3)
                                close_bank(ins, "y2", ss, c2)
            gate_rows(0, gate_row, 2)
            pe.wait_ge(*low_ready.at("o2"))
            pe.wait_ge(*low_ready.at("y"))
            out2(0, range(T4), oT2r, yThr)

            modulation(1, ada_row3)
            gate_rows(1, ada_row3[:, 2 * D:3 * D], 1)
            norm_transposes(6, xn3, T4, 1)
            project2(1, 0, range(TILES))
            project2(1, 1, range(T4))
            project2(1, 2, range(TILES))
            project2(1, 3, range(T4))
            turn_heads(1, 0, lambda c, t: wq[:, t, c * P:(c + 1) * P], 4, TILES, 2)
            turn_heads(1, 1, lambda c, t: k3d[:, t, c, :], KVH, T4, 1)
            project2(1, 4, range(T4))
            turn_heads(1, 2, lambda c, t: nq[:, t, c * P:(c + 1) * P], 4, TILES, 2)
            turn_heads(1, 3, lambda c, t: nk[:, t, c * P:(c + 1) * P], 4, T4, 1)
            for j, n in ((0, 2), (1, 2), (2, 2), (3, 4)):
                for b in range(n):
                    pe.wait_ge(*emptied("heads", 1, j, b))
            for j in (1, 4):
                for t in range(T4):
                    pe.wait_ge(*emptied("in2", 1, j, t))

            def fill1():
                for j in (5, 6):
                    yield from feature_groups(1, j, SEQ)

            attention2(1, fill1(), lambda u: 2)
            turn_outputs(1)
            pe.wait_ge(*low_ready.at("o3"))
            out2(1, range(TILES), oT3r, yT3r, lambda k: low_ready.at("o3" if k < 4 else "y3"))

        @block.scalar
        def _(act):
            run = Steps(act, scalar_step)
            A_ = nc.scalar.activation
            act.preload_act_table_set("natural_log_exp_and_others")

            def norm_guess(n, tiles, xn, added=None):
                for t in range(tiles):
                    if added:
                        for c in range(2):
                            act.wait_ge(*emptied(*x_group(*added, t, c)))
                    run(A_(xn[:, t, :], X[:, t, :], ACT.Square, accum_out=nstat[:, 0, t:t + 1]))
                run.settle()
                run(A_(nstat[:, 1, 0:tiles], nstat[:, 0, 0:tiles], ACT.Ln, bias=eps_col[:, 0:1], scale=1.0 / D))
                run.settle()
                run(A_(nstat[:, 2, 0:tiles], nstat[:, 1, 0:tiles], ACT.Exp, scale=-0.5), rsqrt_guess.by(n))

            def norm_scale(n, tiles, xn):
                act.wait_ge(*rstd_ready.at(n))
                run.settle()
                for t in range(1, tiles, 2):
                    last = t + 2 > tiles
                    run(A_(xn[:, t, :], X[:, t, :], ACT.Copy, scale=nstat[:, 2, t:t + 1]),
                        xn_by_scalar.by(n) if last else None)

            def round_weights(n):
                src, high, _ = raw_quarter(n)
                act.wait_ge(*half_is_loaded(half_at[quarters[n][:4]]))
                if n >= SPLITS:
                    act.wait_ge(*last_use[n - SPLITS])
                run(A_(high, src, ACT.Copy), (high_ready, n + 1))

            splits = Splits(round_weights)

            def copy_out(dst, src, *key):
                splits.due(*key)
                act.wait_ge(*filled(*key))
                run(A_(dst, src, ACT.Copy), emptied(*key))

            taken = [0]

            def take_high(ins, *key):
                taken[0] += 1
                run(ins, (high_taken, taken[0]))
                high_done[key] = (high_taken, taken[0])

            def norm_evacuate(n, which, l):
                for b in range(4):
                    splits.due("hT", n, b)
                    act.wait_ge(*filled("hT", n, b))
                    for kk in range(2):
                        k = 2 * b + kk
                        ins = A_(hT[:, 0, k, :], bank("hT", n, b)[:, kk * SEQ:(kk + 1) * SEQ], ACT.Copy,
                                 scale=g_cols[:, which, l, k:k + 1])
                        take_high(ins, "hT", n, b) if kk else run(ins)

            def softmax_exp(l, u, width, src, kind, scale):
                act.wait_ge(*bias_ready.at(l, u))
                if kind in "WN":
                    if kind == "W":
                        h = units_of_block2(l - 2)[u][1]
                        run(A_(stat[:, u % 4, 3, 1:2], sink[:, h:h + 1], ACT.Exp, bias=stat[:, u % 4, 1, 0:1]))
                run(A_(S[:, u % 2, 0:width], src, ACT.Exp, bias=stat[:, u % 4, 1, 0:1], scale=scale,
                       accum_out=stat[:, u % 4, 2, 0:1]), probs_ready.by(l, u))

            act.wait_ge(x_loaded, 16)
            act.wait_ge(ones_set, 1)
            for l in range(LAYERS):
                norm_guess(2 * l, TILES, xn1, ("down", l - 1) if l else None)
                norm_scale(2 * l, TILES, xn1)
                if l == 0:
                    act.wait_ge(first_loaded, 2 * 16)
                norm_evacuate(2 * l, 0, l)
                if l == 0:
                    act.wait_ge(consts_loaded, CONSTS * 16)
                    run(A_(cond_e[:, :, :], cond[:, :, :], ACT.Exp, scale=-1.0), cond_exp.by(0))
                for c in range(9):
                    if c >= 6:
                        for n in range((c - 6) * 4 + 1, (c - 6) * 4 + 4, 2):
                            j, b = n // 6, n % 6
                            copy_out(qkT[:, j, 2 * b:2 * b + 2, :], bank("qT", l, j, b)[:, :].rearrange("p (a n) -> p a n", a=2), "qT", l, j, b)
                    for t in range(TILES):
                        copy_out(qkv[:, c // 3, t, c % 3 * 512:(c % 3 + 1) * 512], bank("qkv", l, c, t)[:, :], "qkv", l, c, t)
                U = units_of_block1()

                def take_second(u):
                    kind, h, t = U[u]
                    if u >= 2:
                        act.wait_ge(*filled("o", l, u - 2))
                    if kind == "C":
                        act.wait_ge(*emptied("p", l, u, 0))
                        run(A_(PT[:, u % 2, 0:384], S[:, u % 2, 384:768], ACT.Exp, scale=SCALE), stick_weights.by(l, u))
                        return
                    blocks = (G_A if kind == "A" else 1) * (t + 1)
                    for b0 in range(0, blocks, 4):
                        n = min(4, blocks - b0) * P
                        copy_out(PT[:, u % 2, b0 * P:b0 * P + n], bank("p", l, u, b0 // 4)[:, 0:n], "p", l, u, b0 // 4)

                def take_values(u):
                    kind, h, t = U[u]
                    first = {"A": 0, "B": 2, "C": 5}[kind] * P + h * DH
                    act.wait_ge(*filled("o", l, u))
                    if kind == "C":
                        run(A_(o_tok[:, :, first:first + DH], bank("o", l, u)[:, 0:2 * DH].rearrange("p (t n) -> p t n", t=TILES),
                               ACT.Copy), emptied("o", l, u))
                    else:
                        act.wait_ge(*sum_inverted.at(l, u))
                        run(A_(o_tok[:, t, first:first + DH], bank("o", l, u)[:, 0:DH], ACT.Copy, scale=stat[:, u % 4, 2, 1:2]),
                            emptied("o", l, u))

                copied, logs, done, ready = [], [], [], 0

                def copy_gate(key):
                    _, _, c, t = key
                    c -= 9
                    copied.append(gates[:, t, c // 2, c % 2 * 512:(c % 2 + 1) * 512])
                    splits.due(*key)
                    act.wait_ge(*filled(*key))
                    run(A_(copied[-1], bank(*key)[:, :], ACT.Copy))
                    n = len(copied) - 1
                    if n >= 2:
                        act.wait_ge(*gate_exponent.at(l, n - 2))
                    run(A_(gate_log[:, n % 2, :], bank(*key)[:, :], ACT.Abs), emptied(*key))

                def gate_log_step():
                    n = len(logs)
                    logs.append(n)
                    x = gate_log[:, n % 2, :]
                    act.wait_ge(*emptied("gate", l, 9 + n // TILES, n % TILES))
                    run(A_(x, x, ACT.Exp, scale=-1.0))
                    run.settle()
                    run(A_(x, x, ACT.Ln, bias=eps_col[:, 1:2]), gate_logged.by(l, n))

                def gate_exp_step():
                    n = len(done)
                    done.append(n)
                    act.wait_ge(*gate_exponent.at(l, n))
                    run(A_(copied[n], copied[n], ACT.Exp), gates_ready.by(l, n))

                for u in range(len(U) + 2):
                    if 1 <= u <= len(U):
                        take_second(u - 1)
                    if u < len(U):
                        splits.due("s", l, u)
                        kind, h, t = U[u]
                        if kind == "C":
                            act.wait_ge(*emptied("s", l, u))
                            s = S[:, u % 2, 384:768]
                            run(A_(s, S[:, u % 2, 0:384], ACT.Abs))
                            run.settle()
                            run(A_(s, s, ACT.Exp, scale=-SCALE))
                            run.settle()
                            run(A_(s, s, ACT.Ln, bias=eps_col[:, 1:2]), softplus_part.by(l, u))
                        else:
                            w = (G_A if kind == "A" else 1) * (t + 1) * P
                            softmax_exp(l, u, w, S[:, u % 2, 0:w], kind, SCALE)
                    if u >= 2:
                        take_values(u - 2)
                    if len(done) < ready:
                        gate_exp_step()
                    ready = logged_by[(l, u)] = len(logs)
                    if len(logs) < len(copied):
                        gate_log_step()
                    for key in ended_in[(l, u)]:
                        copy_gate(key)
                while len(done) < len(copied):
                    if len(logs) < len(copied):
                        gate_log_step()
                    gate_exp_step()
                for b in range(4):
                    splits.due("oT", l, b)
                    act.wait_ge(*filled("oT", l, b))
                    take_high(A_(oT[:, 0, 2 * b:2 * b + 2, :], bank("oT", l, b)[:, :].rearrange("p (a n) -> p a n", a=2), ACT.Copy),
                              "oT", l, b)
                for b in range(4):
                    splits.due("mT", l, b)
                    act.wait_ge(*filled("mT", l, b))
                    take_high(A_(hT[:, 0, 2 * b:2 * b + 2, :], bank("mT", l, b)[:, :].rearrange("p (a n) -> p a n", a=2), ACT.Copy),
                              "mT", l, b)
                splits.due("wo", l, 1, 1)
                norm_guess(2 * l + 1, TILES, xn1, ("wo", l))
                norm_scale(2 * l + 1, TILES, xn1)
                norm_evacuate(2 * l + 1, 1, l)
                for m in range(16):
                    splits.due("up", l, m)
                    if m >= 2:
                        act.wait_ge(*up_ready.at(l, m - 2))
                    act.wait_ge(*filled("up", l, m))
                    run(A_(up_tmp[:, m % 2, 0, :], bank("up", l, m)[:, :], ACT.Relu), emptied("up", l, m))
                    run.settle()
                    take_high(A_(uT[:, 0, 2 * m:2 * m + 2, :], up_tmp[:, m % 2, 0, :].rearrange("p (a n) -> p a n", a=2), ACT.Square),
                              "up", l, m)
                splits.due("down", l, 1, 1)
            norm_guess(4, TILES, xn1, ("down", 1))

            def modulated_evacuate(n, l):
                for k in range(KD):
                    splits.due("hT", n, k)
                    act.wait_ge(*filled("hT", n, k))
                    if k == 0:
                        act.wait_ge(*ada_ready.at(l))
                    for s in range(2):
                        cols = slice(s * SEQ, (s + 1) * SEQ)
                        ins = A_(hT2[:, 0, k, cols], bank("hT", n, k)[:, cols], ACT.Identity,
                                 scale=gain[:, k, s:s + 1], bias=ada_t[:, k, s:s + 1])
                        take_high(ins, "hT", n, k) if s else run(ins)

            def gate_rows(l, dst, sequences):
                for s in range(sequences):
                    for c in range(2):
                        copy_out(dst[:, s, c * 512:(c + 1) * 512], bank("gateB", l, s, c)[:, :], "gateB", l, s, c)

            def heads_rsqrt(l, j, n):
                act.wait_ge(*heads_squared.at(l, j))
                run(A_(nstat[:, 1, 0:n], nstat[:, 0, 0:n], ACT.Ln, bias=eps_col[:, 0:1], scale=1.0 / DH))
                run.settle()
                run(A_(nstat[:, 2, 0:n], nstat[:, 1, 0:n], ACT.Exp, scale=-0.5), heads_guess.by(l, j))

            def take_features(l, key):
                c = key[2]
                splits.due(*key)
                if l == 0 and c < HY_CH:
                    act.wait_ge(*filled(*key))
                    run(A_(uc[:, c, :], bank(*key)[:, :], ACT.Identity, scale=conv_w[:, 1, c:c + 1], bias=conv_w[:, 3, c:c + 1]),
                        conv_begun.by(c))
                else:
                    n, dst = (N4, (ag, hg)) if l == 0 else (SEQ, (wgT, ngT))
                    c -= HY_CH
                    act.wait_ge(*filled(*key))
                    run(A_(dst[c // 4][:, c % 4, :], bank(*key)[:, 0:n], ACT.Exp, scale=-1.0), silu_exp.by(l, c))

            def attention2(l):
                U = units_of_block2(l)
                for u in range(len(U) + 2):
                    if 1 <= u <= len(U):
                        n = (2 if U[u - 1][0] == "G" and U[u - 1][2] >= TILES else 4) * P
                        if u >= 3:
                            act.wait_ge(*filled("o", 2 + l, u - 3))
                        copy_out(PT[:, (u - 1) % 2, 0:n], bank("p", 2 + l, u - 1, 0)[:, 0:n], "p", 2 + l, u - 1, 0)
                    if u < len(U):
                        splits.due("s", 2 + l, u)
                        kind, h, t = U[u]
                        n = SEQ if kind == "G" and t >= TILES else N4
                        if kind == "G":
                            act.wait_ge(*bias_ready.at(2, u))
                            if u >= 2:
                                act.wait_ge(*filled("p", 2 + l, u - 2, 0))
                            run(A_(S[:, u % 2, 0:n], bank("s", 2, u)[:, 0:n], ACT.Exp, bias=stat[:, u % 4, 1, 0:1],
                                   scale=SCALE, accum_out=stat[:, u % 4, 2, 0:1]), emptied("s", 2, u))
                        else:
                            softmax_exp(2 + l, u, n, S[:, u % 2, 0:n], kind, SCALE)
                    for key in ended_in[(2 + l, u)]:
                        take_features(l, key)
                    if u >= 2:
                        kind, h, t = U[u - 2]
                        dst = {"G": o2_tok, "W": o3_tok, "N": y3_tok}[kind]
                        key = ("o", 2 + l, u - 2)
                        splits.due(*key)
                        act.wait_ge(*filled(*key))
                        act.wait_ge(*sum_inverted.at(*key[1:]))
                        run(A_(dst[:, t, h * DH:(h + 1) * DH], bank(*key)[:, 0:DH], ACT.Copy, scale=stat[:, (u - 2) % 4, 2, 1:2]),
                            emptied(*key))

            act.wait_ge(*x_added.at(4))
            act.wait_ge(context_loaded, 16)
            norm_guess(5, T4, xn2)
            norm_scale(5, T4, xn2)
            modulated_evacuate(5, 0)
            for t in range(T4):
                copy_out(q2[:, t, :], bank("in2", 0, 0, t)[:, :], "in2", 0, 0, t)
            splits.due("in2", 0, 0, T4 - 1, ahead=1)
            heads_rsqrt(0, 0, T4 * QH)
            for t in range(T4):
                copy_out(kv2[:, t, :], bank("in2", 0, 1, t)[:, 0:256], "in2", 0, 1, t)
            splits.due("in2", 0, 1, T4 - 1, ahead=1)
            heads_rsqrt(0, 1, T4 * KVH)
            for key in ended_in[(2, "before")]:
                take_features(0, key)
            for b in range(4):
                copy_out(qT2[:, b, :], bank("heads", 0, 0, b)[:, :], "heads", 0, 0, b)
            for b in range(KVH):
                copy_out(kT2[:, b, :], bank("heads", 0, 1, b)[:, :], "heads", 0, 1, b)
            attention2(0)
            for n in range(2):
                act.wait_ge(*sin_in_range.at(n))
                run(A_(hidden[0:HID, n, :], hidden[0:HID, n, :], ACT.Sin), sin_ready.by(n))
            act.wait_ge(*out_gated.at("o2"))
            take_high(A_(oT2r[:, 0], oT2, ACT.Copy), "o2")
            act.preload_act_table_set("natural_log_exp_and_others")
            for od in range(2):
                act.wait_ge(*filled("energy", od))
                run(A_(rn[:, 0, :], bank("energy", od)[:, :], ACT.Ln, bias=eps_col[:, 0:1]))
                run.settle()
                run(A_(rn[:, 0, :], rn[:, 0, :], ACT.Exp, scale=-0.5), taps_guess.by(od))
            act.wait_ge(*spectra_ready.at(1))
            for c in range(8):
                if c % 2:
                    dst = (Z, G1)[c // 4][:, :, c % 4 * P:(c % 4 + 1) * P]
                    copy_out(dst, bank("zg", c)[:, :].rearrange("p (t n) -> p t n", t=T4), "zg", c)
            for s in range(2):
                for c2 in range(2):
                    cols = slice(s * SEQ, (s + 1) * SEQ)
                    act.wait_ge(*out_gated.at("y", s, c2))
                    take_high(A_(yThr[:, 0, 2 * c2:2 * c2 + 2, cols], y_tmp[:, c2, :].rearrange("p (a n) -> p a n", a=2), ACT.Copy), "y", s, c2)
            gate_rows(0, gate_b0, 2)
            splits.due("out2", 0, 1, T4 - 1)
            act.wait_ge(*x_added.at(5))
            norm_guess(6, T4, xn3)
            norm_scale(6, T4, xn3)
            gate_rows(1, gate_b1, 1)
            modulated_evacuate(6, 1)
            for t in range(TILES):
                copy_out(wq[:, t, :], bank("in2", 1, 0, t)[:, :], "in2", 1, 0, t)
            splits.due("in2", 1, 0, TILES - 1, ahead=1)
            heads_rsqrt(1, 0, TILES * QH)
            for t in range(T4):
                copy_out(kv3[:, t, :], bank("in2", 1, 1, t)[:, 0:256], "in2", 1, 1, t)
            splits.due("in2", 1, 1, T4 - 1, ahead=1)
            heads_rsqrt(1, 1, T4 * KVH)
            for t in range(TILES):
                copy_out(nq[:, t, :], bank("in2", 1, 2, t)[:, :], "in2", 1, 2, t)
            splits.due("in2", 1, 2, TILES - 1, ahead=1)
            heads_rsqrt(1, 2, TILES * QH)
            for t in range(T4):
                copy_out(nk[:, t, :], bank("in2", 1, 3, t)[:, :], "in2", 1, 3, t)
            for b in range(2):
                copy_out(wqT[:, 2 * b:2 * b + 2, :], bank("heads", 1, 0, b)[:, :].rearrange("p (a n) -> p a n", a=2), "heads", 1, 0, b)
            for b in range(KVH):
                copy_out(wkT[:, b, :], bank("heads", 1, 1, b)[:, :], "heads", 1, 1, b)
            heads_rsqrt(1, 3, T4 * QH)
            for t in range(T4):
                copy_out(nv[:, t, :], bank("in2", 1, 4, t)[:, :], "in2", 1, 4, t)
            for b in range(2):
                copy_out(nqT[:, 2 * b:2 * b + 2, :], bank("heads", 1, 2, b)[:, :].rearrange("p (a n) -> p a n", a=2), "heads", 1, 2, b)
            for b in range(4):
                copy_out(nkT[:, b, :], bank("heads", 1, 3, b)[:, :], "heads", 1, 3, b)
            attention2(1)
            act.wait_ge(*out_gated.at("o3"))
            take_high(A_(oT3r[:, 0], oT3, ACT.Copy), "o3")
            act.wait_ge(*out_gated.at("y3"))
            take_high(A_(yT3r[:, 0], yT3, ACT.Copy), "y3")
            splits.due("out2", 1, 1, 1)

        @block.vector
        def _(dve):
            run = Steps(dve, vector_step)
            V = nc.vector

            def newton(v, y, t, width=None):
                run(V.tensor_tensor(t, y, y, ALU.mult))
                run.settle()
                run(V.tensor_tensor(t, t, v, ALU.mult))
                run.settle()
                run(V.tensor_scalar(t, t, -0.5, 1.5, ALU.mult, ALU.add))
                run.settle()

            def norm_finish(n, tiles, xn):
                dve.wait_ge(*rsqrt_guess.at(n))
                v, y, t = nstat[:, 0, 0:tiles], nstat[:, 2, 0:tiles], nstat[:, 3, 0:tiles]
                run(V.tensor_scalar(v, v, 1.0 / D, EPS, ALU.mult, ALU.add))
                run.settle()
                newton(v, y, t)
                run(V.tensor_tensor(y, y, t, ALU.mult), rstd_ready.by(n))
                run.settle()
                if xn is None:
                    return
                for tt in range(0, tiles, 2):
                    run(V.tensor_scalar(xn[:, tt, :], X[:, tt, :], nstat[:, 2, tt:tt + 1], None, ALU.mult),
                        xn_by_vector.by(n) if tt + 2 >= tiles else None)

            def subtract_high(n):
                src, high, low = raw_quarter(n)
                dve.wait_ge(high_ready, n + 1)
                run(V.tensor_tensor(low, src, high.bitcast(F32), ALU.subtract), (split_ready, n + 1))

            splits = Splits(subtract_high)

            def take_low(x, k, value, signal, *key):
                dve.wait_ge(*high_done[key])
                run(V.tensor_tensor(x[:, 1][k], value, x[:, 0][k].bitcast(F32), ALU.subtract), signal)

            def norm_evacuate(n, which, l):
                for b in range(4):
                    splits.due("hT", n, b)
                    dve.wait_ge(*high_done["hT", n, b])
                    for kk in range(2):
                        k = 2 * b + kk
                        run(V.scalar_tensor_tensor(out=hT[:, 1, k, :], in0=bank("hT", n, b)[:, kk * SEQ:(kk + 1) * SEQ],
                                                   scalar=g_cols[:, which, l, k:k + 1], in1=hT[:, 0, k, :].bitcast(F32),
                                                   op0=ALU.mult, op1=ALU.subtract), emptied("hT", n, b) if kk else None)

            run(V.memset(ones[:, :], 1.0))
            run(V.memset(eps_col[:, 0:1], EPS))
            V.memset(eps_col[:, 1:2], 1.0).then_inc(ones_set, 1)
            dve.wait_ge(ones_set, 1)
            dve.wait_ge(x_loaded, 16)
            for l in range(LAYERS):
                norm_finish(2 * l, TILES, xn1)
                if l == 0:
                    dve.wait_ge(first_loaded, 2 * 16)
                norm_evacuate(2 * l, 0, l)
                if l == 0:
                    splits.due("qkv", 0, 0, 1)
                    dve.wait_ge(consts_loaded, CONSTS * 16)
                    dve.wait_ge(*cond_exp.at(0))
                    run(V.tensor_scalar(cond_e[:, :, :], cond_e[:, :, :], 1.0, None, ALU.add), cond_ready_s.by("sum"))
                    run.settle()
                    run(V.reciprocal(cond_e[:, :, :], cond_e[:, :, :]))
                    run.settle()
                    run(V.tensor_tensor(cond[:, :, :], cond[:, :, :], cond_e[:, :, :], ALU.mult), cond_ready_s.by("done"))
                for j in range(2):
                    for c in range(3 * j, 3 * j + 3):
                        for t in range(TILES):
                            splits.due("qkv", l, c, t)
                            dve.wait_ge(*emptied("qkv", l, c, t))
                    if l + j == 0:
                        dve.wait_ge(rel_stored, 16)
                    h3 = ROPE // 2
                    for t in range(TILES):
                        hd = qkv[:, j, t, 0:ROT * DH].rearrange("p (h d) -> p h d", h=ROT)
                        x1, x2 = hd[:, :, 0:h3], hd[:, :, h3:ROPE]
                        cos = rope_a[:, t, 0:h3].unsqueeze(1).to_broadcast([P, ROT, h3])
                        sin = rope_a[:, t, h3:ROPE].unsqueeze(1).to_broadcast([P, ROT, h3])
                        r = [rope_tmp[:, n, t, :, :] for n in range(4)]
                        run(V.tensor_tensor(r[0], x1, cos, ALU.mult))
                        run(V.tensor_tensor(r[1], x2, sin, ALU.mult))
                        run(V.tensor_tensor(r[2], x2, cos, ALU.mult))
                        run(V.tensor_tensor(r[3], x1, sin, ALU.mult))
                        run.settle()
                        run(V.tensor_tensor(x1, r[0], r[1], ALU.subtract))
                        run(V.tensor_tensor(x2, r[2], r[3], ALU.add), qk_roped.by(l, j) if t else None)
                    run.settle()
                for n in range(0, 12, 2):
                    j, b = n // 6, n % 6
                    splits.due("qT", l, j, b)
                    dve.wait_ge(*filled("qT", l, j, b))
                    run(V.tensor_copy(qkT[:, j, 2 * b:2 * b + 2, :], bank("qT", l, j, b)[:, :].rearrange("p (a n) -> p a n", a=2)),
                        emptied("qT", l, j, b))

                U = units_of_block1()
                last_p = lambda u: filled("p", l, u, 1 if U[u][0] == "A" and U[u][2] else 0)

                def invert_sum(u):
                    if U[u][0] != "C":
                        st = stat[:, u % 4, :, :]
                        dve.wait_ge(*probs_ready.at(l, u))
                        run(V.reciprocal(st[:, 2, 1:2], st[:, 2, 0:1]), sum_inverted.by(l, u))

                exponents = 0

                def gate_exponents(until):
                    for n in range(exponents, until):
                        g = gates[:, n % TILES, n // TILES // 2, n // TILES % 2 * 512:(n // TILES % 2 + 1) * 512]
                        dve.wait_ge(*gate_logged.at(l, n))
                        run(V.scalar_tensor_tensor(out=g, in0=g, scalar=0.0, in1=gate_log[:, n % 2, :], op0=ALU.min, op1=ALU.subtract),
                            gate_exponent.by(l, n))
                    return until

                for u in range(len(U) + 1):
                    if u < len(U):
                        kind, h, t = U[u]
                        st = stat[:, u % 4, :, :]
                        if u >= 2:
                            dve.wait_ge(*last_p(u - 2))
                        dve.wait_ge(*filled("s", l, u))
                        if kind == "C":
                            run(V.tensor_tensor(S[:, u % 2, 0:384], bank("s", l, u)[:, 0:384], mask_c.rearrange("p a n -> p (a n)"), ALU.add),
                                emptied("s", l, u))
                        elif kind == "A":
                            n = G_A if t == 0 else 2
                            w = (t + 1) * P
                            run(V.tensor_tensor_reduce(
                                S[:, u % 2, 0:n * w].rearrange("p (g n) -> p g n", g=n),
                                bank("s", l, u)[:, 0:n * w].rearrange("p (g n) -> p g n", g=n),
                                mask_a[:, 0:n, SEQ - w:SEQ], 1.0, -3e38, ALU.add, ALU.max, st[:, 0, 0:1]), emptied("s", l, u))
                            if t:
                                dve.wait_ge(*filled("s2", l, u))
                                run(V.tensor_tensor_reduce(S[:, u % 2, 512:768], bank("s2", l, u)[:, 0:w], mask_a[:, 2, :],
                                                           1.0, -3e38, ALU.add, ALU.max, st[:, 0, 1:2]), emptied("s2", l, u))
                                run.settle()
                                run(V.tensor_tensor(st[:, 0, 0:1], st[:, 0, 0:1], st[:, 0, 1:2], ALU.max))
                        else:
                            w = (t + 1) * P
                            run(V.tensor_tensor_reduce(S[:, u % 2, 0:w], bank("s", l, u)[:, 0:w], mask_b[:, SEQ - w:SEQ],
                                                       1.0, -3e38, ALU.add, ALU.max, st[:, 0, 0:1]), emptied("s", l, u))
                        if kind != "C":
                            run.settle()
                            run(V.tensor_scalar(st[:, 1, 0:1], st[:, 0, 0:1], -SCALE, None, ALU.mult), bias_ready.by(l, u))
                    if u >= 1 and U[u - 1][0] == "C":
                        dve.wait_ge(*filled("p", l, u - 1, 0))
                        s = S[:, (u - 1) % 2, :]
                        run(V.tensor_tensor(s[:, 384:768], s[:, 0:384], bank("p", l, u - 1, 0)[:, 0:384], ALU.subtract),
                            emptied("p", l, u - 1, 0))
                    splits.due("s", l, min(u, len(U) - 1))
                    if u >= 1:
                        invert_sum(u - 1)
                        exponents = gate_exponents(logged_by[(l, u)])
                    if u < len(U):
                        if kind == "C":
                            sp = PT[:, u % 2, 384:768]
                            dve.wait_ge(*emptied("s", l, u))
                            if u >= 2:
                                dve.wait_ge(*filled("o", l, u - 2))
                            run(V.tensor_scalar(sp, S[:, u % 2, 0:384], 0.0, None, ALU.max))
                            run.settle()
                            dve.wait_ge(*softplus_part.at(l, u))
                            run(V.scalar_tensor_tensor(out=sp, in0=S[:, u % 2, 384:768], scalar=1.0 / SCALE, in1=sp,
                                                       op0=ALU.mult, op1=ALU.add), stick_summed.by(l, u))
                gate_exponents(6 * TILES)
                for b in range(4):
                    splits.due("oT", l, b)
                    dve.wait_ge(*filled("oT", l, 3))
                    dve.wait_ge(*high_done["oT", l, b])
                    k = slice(2 * b, 2 * b + 2)
                    run(V.tensor_tensor(oT[:, 1, k, :], bank("oT", l, b)[:, :].rearrange("p (a n) -> p a n", a=2),
                                        oT[:, 0, k, :].bitcast(F32), ALU.subtract), emptied("oT", l, b))

                def take_merged(c):
                    for b in range(2 * c, 2 * c + 2):
                        splits.due("mT", l, b)
                        dve.wait_ge(*high_done["mT", l, b])
                        k = slice(2 * b, 2 * b + 2)
                        run(V.tensor_tensor(hT[:, 1, k, :], bank("mT", l, b)[:, :].rearrange("p (a n) -> p a n", a=2),
                                            hT[:, 0, k, :].bitcast(F32), ALU.subtract), emptied("mT", l, b))

                dve.wait_ge(*gates_ready.at(l, 6 * TILES - 1))
                run.settle()
                for c in range(2):
                    cols = slice(c * 512, (c + 1) * 512)
                    for br in range(3):
                        for t in range(TILES):
                            key = ("y", l, c, t, br)
                            splits.due(*key)
                            dve.wait_ge(*filled(*key))
                            dst = merged[:, t, cols] if br == 0 else gated[:, t, :]
                            run(V.tensor_tensor(dst, bank(*key)[:, :], gates[:, t, br, cols], ALU.mult), emptied(*key))
                            run.settle()
                            if br:
                                run(V.tensor_tensor(merged[:, t, cols], merged[:, t, cols], gated[:, t, :], ALU.add),
                                    merged_ready.by(l, c) if t and br == 2 else None)
                                run.settle()
                    if c == 0:
                        take_merged(0)

                def add_to_x(name, n):
                    for t in range(TILES):
                        for c in range(2):
                            key = x_group(name, l, t, c)
                            splits.due(*key)
                            dve.wait_ge(*filled(*key))
                            x = X[:, t, c * 512:(c + 1) * 512]
                            run(V.tensor_tensor(x, x, bank(*key)[:, :], ALU.add), emptied(*key))
                    run.settle()
                    run(V.tensor_copy(small[:, 2:3], X[:, 1, D - 1:D]), x_added.by(n))
                    run.settle()

                take_merged(1)
                add_to_x("wo", 2 * l)
                norm_finish(2 * l + 1, TILES, xn1)
                norm_evacuate(2 * l + 1, 1, l)
                for m in range(16):
                    splits.due("up", l, m)
                    t, v = up_tmp[:, m % 2, 0, :], up_tmp[:, m % 2, 1, :]
                    dve.wait_ge(*high_done["up", l, m])
                    run(V.tensor_tensor(v, t, t, ALU.mult))
                    run.settle()
                    k = slice(2 * m, 2 * m + 2)
                    run(V.tensor_tensor(uT[:, 1, k, :], v.rearrange("p (a n) -> p a n", a=2), uT[:, 0, k, :].bitcast(F32),
                                        ALU.subtract), up_ready.by(l, m))
                add_to_x("down", 2 * l + 1)

            norm_finish(4, TILES, None)
            dve.wait_ge(final_g_loaded, 16)
            for t in range(TILES):
                run(V.scalar_tensor_tensor(out=X[:, t, :], in0=X[:, t, :], scalar=nstat[:, 2, t:t + 1], in1=final_g,
                                           op0=ALU.mult, op1=ALU.mult), x_added.by(4) if t else None)

            def modulation(l, row, gate, bias):
                dve.wait_ge(ada_loaded, 16)
                if l:
                    dve.wait_ge(ada_bias_loaded, 16)
                for c in range(6):
                    cols = slice(c * 512, (c + 1) * 512)
                    dst = row[0:2, cols] if c < 4 else gate[0:2, (c - 4) * 512:(c - 3) * 512]
                    splits.due("ada", l, c)
                    dve.wait_ge(*filled("ada", l, c))
                    run(V.tensor_tensor(dst, bank("ada", l, c)[0:2, :], bias[0:2, cols], ALU.add), emptied("ada", l, c))
                dve.wait_ge(*filled("adaT", l))
                run(V.tensor_copy(ada_t[:, :, :], bank("adaT", l)[:, 0:32].rearrange("p (k s) -> p k s", k=16)), emptied("adaT", l))
                run.settle()
                run(V.tensor_scalar(gain[:, :, :], ada_t[:, KD:2 * KD, :], 1.0, None, ALU.add))
                run.settle()
                g = g_cols[:, 2, l, :].unsqueeze(2).to_broadcast([P, KD, 2])
                run(V.tensor_tensor(gain[:, :, :], gain[:, :, :], g, ALU.mult), ada_ready.by(l))

            def modulated_evacuate(n, tmp):
                run.settle()
                for k in range(KD):
                    splits.due("hT", n, k)
                    dve.wait_ge(*high_done["hT", n, k])
                    b = bank("hT", n, k)
                    for s in range(2):
                        cols = slice(s * SEQ, (s + 1) * SEQ)
                        run(V.tensor_scalar(tmp[:, k % 2, cols], b[:, cols], gain[:, k, s:s + 1], ada_t[:, k, s:s + 1], ALU.mult, ALU.add))
                    run.settle()
                    run(V.tensor_tensor(hT2[:, 1, k, :], tmp[:, k % 2, :], hT2[:, 0, k, :].bitcast(F32), ALU.subtract), emptied("hT", n, k))

            def heads_norm(l, j, x, tiles, heads, g, rope, dup, ready, during=None):
                n = tiles * heads
                for key in ready:
                    splits.due(*key)
                    dve.wait_ge(*emptied(*key))
                splits.due(*ready[-1], ahead=1)
                x3 = x.rearrange("p t (h d) -> p t h d", h=heads)
                sq = work[:, 0:n * DH].rearrange("p (t h d) -> p t h d", t=tiles, h=heads)
                for t in range(tiles):
                    run(V.tensor_tensor(sq[:, t], x3[:, t], x3[:, t], ALU.mult))
                run.settle()
                run(V.tensor_reduce(nstat[:, 0, 0:n], work[:, 0:n * DH].rearrange("p (a d) -> p a d", d=DH), AX_X, ALU.add),
                    heads_squared.by(l, j))
                v, y, t_ = nstat[:, 0, 0:n], nstat[:, 2, 0:n], nstat[:, 3, 0:n]
                dve.wait_ge(*heads_guess.at(l, j))
                run(V.tensor_scalar(v, v, 1.0 / DH, EPS, ALU.mult, ALU.add))
                run.settle()
                newton(v, y, t_)
                run(V.tensor_tensor(y, y, t_, ALU.mult))
                run.settle()
                if during:
                    splits.due(*during)
                for t in range(tiles):
                    r = y[:, t * heads:(t + 1) * heads].unsqueeze(2).to_broadcast([P, heads, DH])
                    run(V.tensor_tensor(x3[:, t], x3[:, t], r, ALU.mult))
                run.settle()
                gb = head_gain[:, g, :].unsqueeze(1).to_broadcast([P, heads, DH])
                for t in range(tiles):
                    run(V.tensor_tensor(x3[:, t], x3[:, t], gb, ALU.mult))
                run.settle()
                if rope:
                    hd = DH // 2
                    for t in range(TILES):
                        x0, x1 = x3[:, t, :, 0:DH:2], x3[:, t, :, 1:DH:2]
                        cos = rope_b[:, t, 0:hd].unsqueeze(1).to_broadcast([P, heads, hd])
                        sin = rope_b[:, t, hd:DH].unsqueeze(1).to_broadcast([P, heads, hd])
                        r = [work[:, (4 * t + m) * 256:(4 * t + m) * 256 + heads * hd].rearrange("p (h d) -> p h d", h=heads)
                             for m in range(4)]
                        run(V.tensor_tensor(r[0], x0, cos, ALU.mult))
                        run(V.tensor_tensor(r[1], x1, sin, ALU.mult))
                        run(V.tensor_tensor(r[2], x0, sin, ALU.mult))
                        run(V.tensor_tensor(r[3], x1, cos, ALU.mult))
                        run.settle()
                        run(V.tensor_tensor(x0, r[0], r[1], ALU.subtract))
                        run(V.tensor_tensor(x1, r[2], r[3], ALU.add))
                    run.settle()
                if dup is not None:
                    for half in range(2):
                        ins = V.tensor_copy(dup.rearrange("p t h (a d) -> p t h a d", a=2)[:, :, :, half, :], x3)
                        run(ins, heads_ready.by(l, j) if half else None)
                else:
                    run(V.tensor_copy(small[:, 3:4], small[:, 3:4]), heads_ready.by(l, j))
                run.settle()

            def silu_finish(l, key):
                c = key[2] - HY_CH
                n, dst = (N4, (ag, hg)) if l == 0 else (SEQ, (wgT, ngT))
                g = dst[c // 4][:, c % 4, :]
                dve.wait_ge(*silu_exp.at(l, c))
                run(V.tensor_scalar(g, g, 1.0, None, ALU.add))
                run.settle()
                run(V.reciprocal(g, g))
                run.settle()
                run(V.tensor_tensor(g, g, bank(*key)[:, 0:n], ALU.mult), emptied(*key))

            def take_features(l, key):
                splits.due(*key)
                c = key[2]
                if l or c >= HY_CH:
                    return silu_finish(l, key)
                dve.wait_ge(*conv_begun.at(c))
                b = bank(*key)[:, :].rearrange("p (s n) -> p s n", s=2)
                u = uc[:, c, :].rearrange("p (s n) -> p s n", s=2)
                for s in range(2):
                    run(V.scalar_tensor_tensor(out=u[:, s, 1:SEQ], in0=b[:, s, 0:SEQ - 1], scalar=conv_w[:, 0, c:c + 1],
                                               in1=u[:, s, 1:SEQ], op0=ALU.mult, op1=ALU.add))
                run.settle()
                for s in range(2):
                    run(V.scalar_tensor_tensor(out=u[:, s, 0:SEQ - 1], in0=b[:, s, 1:SEQ], scalar=conv_w[:, 2, c:c + 1],
                                               in1=u[:, s, 0:SEQ - 1], op0=ALU.mult, op1=ALU.add), emptied(*key) if s else None)

            def attention2(l):
                U = units_of_block2(l)

                def invert_sum(u):
                    st = stat[:, u % 4, :, :]
                    dve.wait_ge(*probs_at(2 + l, u))
                    if U[u][0] == "W":
                        run(V.tensor_tensor(st[:, 2, 0:1], st[:, 2, 0:1], st[:, 3, 1:2], ALU.add))
                        run.settle()
                    run(V.reciprocal(st[:, 2, 1:2], st[:, 2, 0:1]), sum_inverted.by(2 + l, u))

                for u in range(len(U) + 1):
                    splits.due("s", 2 + l, min(u, len(U) - 1))
                    if u < len(U):
                        kind, h, t = U[u]
                        st = stat[:, u % 4, :, :]
                        n = SEQ if kind == "G" and t >= TILES else N4
                        b = bank("s", 2 + l, u)
                        dve.wait_ge(*filled("s", 2 + l, u))
                        if kind == "G":
                            run(V.tensor_reduce(st[:, 0, 0:1], b[:, 0:n], AX_X, ALU.max))
                            run.settle()
                            run(V.tensor_scalar(st[:, 1, 0:1], st[:, 0, 0:1], -SCALE, None, ALU.mult), bias_ready.by(2 + l, u))
                        else:
                            if u >= 2:
                                dve.wait_ge(*filled("p", 2 + l, u - 2, 0))
                            m = mask_w[:, t, :] if kind == "W" else rel_bias[:, t, h, :]
                            run(V.tensor_tensor_reduce(S[:, u % 2, 0:SEQ], b[:, 0:SEQ], m, 1.0, -3e38, ALU.add, ALU.max, st[:, 0, 0:1]))
                            run(V.tensor_tensor_reduce(S[:, u % 2, SEQ:N4], b[:, SEQ:N4], no_mask, 1.0, -3e38, ALU.add, ALU.max,
                                                       st[:, 0, 1:2]), emptied("s", 2 + l, u))
                            run.settle()
                            run(V.tensor_tensor(st[:, 0, 0:1], st[:, 0, 0:1], st[:, 0, 1:2], ALU.max))
                            run.settle()
                            if kind == "W":
                                run(V.scalar_tensor_tensor(out=st[:, 1, 0:1], in0=st[:, 0, 0:1], scalar=-SCALE, in1=sink_neg[:, h:h + 1],
                                                           op0=ALU.mult, op1=ALU.min), bias_ready.by(2 + l, u))
                            else:
                                run(V.tensor_scalar(st[:, 1, 0:1], st[:, 0, 0:1], -SCALE, None, ALU.mult), bias_ready.by(2 + l, u))
                    if u >= 1:
                        invert_sum(u - 1)
                        for key in ended_in[(2 + l, u - 1)]:
                            take_features(l, key)
                for key in ended_in[(2 + l, len(U))]:
                    take_features(l, key)

            def add_gated(l, n, tiles, gate_b):
                for c in range(2):
                    for t in tiles:
                        key = ("out2", l, c, t)
                        splits.due(*key)
                        cols = slice(c * 512, (c + 1) * 512)
                        dve.wait_ge(*filled(*key))
                        w = work[:, t * 512:(t + 1) * 512]
                        run(V.tensor_tensor(w, bank(*key)[:, :], gate_b[:, t // 2, cols], ALU.mult), emptied(*key))
                        run.settle()
                        run(V.tensor_tensor(X[:, t, cols], X[:, t, cols], w, ALU.add),
                            x_added.by(n) if c and t == tiles[-1] else None)

            run(V.memset(small[:, 3:5], 0.0))
            run(V.tensor_scalar(sink_neg[:, :], sink[:, :], -1.0, None, ALU.mult))
            modulation(0, ada_row, gate_row, ada_bias)
            norm_finish(5, T4, xn2)
            modulated_evacuate(5, mod_tmp)
            heads_norm(0, 0, q2, T4, QH, 0, True, None, [("in2", 0, 0, t) for t in range(T4)], ("in2", 0, 1, T4 - 1))
            heads_norm(0, 1, kv2[:, :, 0:KVH * DH], T4, KVH, 1, True, k2d, [("in2", 0, 1, t) for t in range(T4)])
            for key in ended_in[(2, "before")]:
                take_features(0, key)
            attention2(0)
            def hidden_layer(n):
                a, k = hidden[0:HID, n, :], work[0:HID, 0:SEQ]
                dve.wait_ge(*filled("f", n))
                run(V.tensor_scalar(a, bank("f", n)[0:HID, 0:SEQ], hid[:, n:n + 1], hid[:, 2:3], ALU.add, ALU.mult), emptied("f", n))
                run.settle()
                run(V.tensor_scalar(k, a, 1.0 / TWO_PI, ROUND, ALU.mult, ALU.add))
                run.settle()
                run(V.tensor_scalar(k, k, ROUND, None, ALU.subtract))
                run.settle()
                run(V.scalar_tensor_tensor(out=a, in0=k, scalar=-TWO_PI_HI, in1=a, op0=ALU.mult, op1=ALU.add))
                run.settle()
                run(V.scalar_tensor_tensor(out=a, in0=k, scalar=-TWO_PI_LO, in1=a, op0=ALU.mult, op1=ALU.add))
                run.settle()
                run(V.tensor_scalar(a, a, PI_IN, -PI_IN, ALU.min, ALU.max), sin_in_range.by(n))
                run.settle()

            hidden_layer(0)
            for b in range(4):
                dve.wait_ge(*filled("oT", 2, b))
                run(V.tensor_tensor(oT2[:, b, :], bank("oT", 2, b)[:, :], ag[:, b, :], ALU.mult), emptied("oT", 2, b))
            run.settle()
            run(V.tensor_copy(small[:, 5:6], small[:, 4:5]), out_gated.by("o2"))
            hidden_layer(1)
            take_low(oT2r, slice(None), oT2, low_ready.by("o2"), "o2")
            run.settle()

            sq = work.rearrange("p (a n) -> p a n", a=4)
            dve.wait_ge(tables_loaded, 2 * 16)
            for od in range(2):
                for d in range(2):
                    for t in range(TILES):
                        dve.wait_ge(*filled("tap", od, d, t))
                        run(V.tensor_tensor(taps[:, d, t, :], bank("tap", od, d, t)[:, :], decay[:, t, :], ALU.mult), emptied("tap", od, d, t))
                run.settle()
                run(V.memset(taps[0:1, 1, 0, :], 0.0))
                run.settle()
                if od:
                    dve.wait_ge(*filled("energy", 0))
                    dve.wait_ge(*filled("nyq", 0))
                for d in range(2):
                    for t in range(TILES):
                        run(V.tensor_tensor(sq[:, 2 * d + t, :], taps[:, d, t, :], taps[:, d, t, :], ALU.mult),
                            taps_squared.by(od) if d and t else None)
                run(V.tensor_tensor(taps_sd[:, 0], taps[:, 0], taps[:, 1], ALU.add))
                run(V.tensor_tensor(taps_sd[:, 1], taps[:, 0], taps[:, 1], ALU.subtract), taps_mixed.by(od))
                if od == 0:
                    run(V.tensor_tensor(uc[:, 8:12, :], uc[:, 8:12, :], hg, ALU.mult), silu_used.by(0))
                dve.wait_ge(*taps_guess.at(od))
                v, y, t_ = rn[:, 1, :], rn[:, 0, :], taps[:, 0, 0, :]
                run.settle()
                run(V.tensor_scalar(v, bank("energy", od)[:, :], EPS, None, ALU.add), emptied("energy", od))
                run.settle()
                newton(v, y, t_)
                run(V.tensor_tensor(y, y, t_, ALU.mult))
                run.settle()
                if od == 0:
                    dve.wait_ge(skip_loaded, 16)
                for m in range(2):
                    dve.wait_ge(*filled("spec", od, m, 0))
                    run(V.tensor_tensor(spec_a[:, od, m, :], bank("spec", od, m, 0)[:, :], y, ALU.mult), emptied("spec", od, m, 0))
                    dve.wait_ge(*filled("spec", od, m, 1))
                    run(V.tensor_tensor(spec_b[:, od, m, :], bank("spec", od, m, 1)[:, :], y, ALU.mult), emptied("spec", od, m, 1))
                    run.settle()
                    run(V.tensor_tensor(spec_a[:, od, m, :], spec_a[:, od, m, :], skip_b[:, od, :], ALU.add))
                run(V.memset(spec_b[0:1, od, 0, :], 0.0))
                dve.wait_ge(*filled("nyq", od))
                run(V.tensor_tensor(spec_c[0:1, od, :], bank("nyq", od)[0:1, :], y[0:1, :], ALU.mult), emptied("nyq", od))
                run.settle()
                run(V.tensor_tensor(spec_c[0:1, od, :], spec_c[0:1, od, :], skip_b[0:1, od, :], ALU.add), spectra_ready.by(od))
                run.settle()
            for c in range(0, 8, 2):
                dst = (Z, G1)[c // 4][:, :, c % 4 * P:(c % 4 + 1) * P]
                dve.wait_ge(*filled("zg", c))
                run(V.tensor_copy(dst, bank("zg", c)[:, :].rearrange("p (t n) -> p t n", t=T4)), emptied("zg", c))

            for od in range(2):
                for s in range(2):
                    y = spectrum(s)
                    if od:
                        for n in range(2):
                            dve.wait_ge(*filled("z1", s, n))
                    for m in range(2):
                        zr, zi = bank("zf", od, s, m, 0), bank("zf", od, s, m, 1)
                        a, b = spec_a[:, od, m, :], spec_b[:, od, m, :]
                        re, im = y[:, m, :], y[:, 2 + m, :]
                        t0, t1 = spec_tmp[:, 0, :], spec_tmp[:, 1, :]
                        dve.wait_ge(*filled("zf", od, s, m, 0))
                        dve.wait_ge(*filled("zf", od, s, m, 1))
                        run(V.tensor_tensor(re, zr[:, :], a, ALU.mult))
                        run(V.tensor_tensor(im, zr[:, :], b, ALU.mult), emptied("zf", od, s, m, 0))
                        run(V.tensor_tensor(t0, zi[:, :], b, ALU.mult))
                        run(V.tensor_tensor(t1, zi[:, :], a, ALU.mult))
                        run.settle()
                        run(V.tensor_tensor(re, re, t0, ALU.subtract))
                        run(V.tensor_tensor(im, im, t1, ALU.add))
                        run.settle()
                        if m == 0:
                            run(V.tensor_tensor(im[0:1, :], zi[0:1, :], spec_c[0:1, od, :], ALU.mult), emptied("zf", od, s, m, 1))
                            run.settle()
                        else:
                            run(V.tensor_copy(small[:, 5:6], zi[:, 0:1]), emptied("zf", od, s, m, 1))
                            run.settle()
                    run(V.tensor_copy(small[:, 5:6], small[:, 4:5]), spectrum_ready.by(od, s))
                for s in range(2):
                    if od == 0:
                        for t in range(TILES):
                            dve.wait_ge(*filled("z1", s, t))
                            run(V.tensor_tensor(Z[:, 2 * s + t, :], bank("z1", s, t)[:, :], G1[:, 2 * s + t, :], ALU.mult), emptied("z1", s, t))
                    else:
                        for c2 in range(2):
                            cols = slice(s * SEQ, (s + 1) * SEQ)
                            dve.wait_ge(*filled("y2", s, c2))
                            y3 = y_tmp[:, c2, :].rearrange("p (a n) -> p a n", a=2)
                            run(V.tensor_tensor(y3, bank("y2", s, c2)[:, :].rearrange("p (a n) -> p a n", a=2),
                                                uc[:, 8 + 2 * c2:10 + 2 * c2, cols], ALU.mult), emptied("y2", s, c2))
                            run.settle()
                            run(V.tensor_copy(small[:, 5:6], small[:, 4:5]), out_gated.by("y", s, c2))
                        for c2 in range(2):
                            y3 = y_tmp[:, c2, :].rearrange("p (a n) -> p a n", a=2)
                            k = slice(2 * c2, 2 * c2 + 2)
                            dve.wait_ge(*high_done["y", s, c2])
                            run(V.tensor_tensor(yThr[:, 1, k, cols], y3, yThr[:, 0, k, cols].bitcast(F32), ALU.subtract),
                                low_ready.by("y") if s and c2 else None)
                        run.settle()
            add_gated(0, 5, list(range(T4)), gate_b0)
            run.settle()

            modulation(1, ada_row3, ada_row3[:, 2 * D:3 * D], ada_bias3)
            norm_finish(6, T4, xn3)
            modulated_evacuate(6, mod_tmp3)
            heads_norm(1, 0, wq, TILES, QH, 2, True, None, [("in2", 1, 0, t) for t in range(TILES)], ("in2", 1, 1, T4 - 1))
            heads_norm(1, 1, kv3[:, :, 0:KVH * DH], T4, KVH, 3, True, k3d, [("in2", 1, 1, t) for t in range(T4)], ("in2", 1, 2, TILES - 1))
            heads_norm(1, 2, nq, TILES, QH, 4, False, None, [("in2", 1, 2, t) for t in range(TILES)], ("in2", 1, 3, T4 - 1))
            heads_norm(1, 3, nk, T4, QH, 5, False, None, [("in2", 1, 3, t) for t in range(T4)])
            dve.wait_ge(bias_loaded, BIASES * 16)
            dve.wait_ge(bias_masked, 1)
            run(V.memset(no_mask, 0.0))
            run.settle()
            attention2(1)
            for n, (key, x, gate) in enumerate((("o3", oT3, wgT), ("y3", yT3, ngT))):
                for b in range(2):
                    dve.wait_ge(*filled("oT", 3, 2 * n + b))
                    run(V.tensor_tensor(x[:, 2 * b:2 * b + 2, :], bank("oT", 3, 2 * n + b)[:, :].rearrange("p (a n) -> p a n", a=2),
                                        gate[:, 2 * b:2 * b + 2, :], ALU.mult), emptied("oT", 3, 2 * n + b))
                run.settle()
                run(V.tensor_copy(small[:, 5:6], small[:, 4:5]), out_gated.by(key))
            for key, x, xr in (("o3", oT3, oT3r), ("y3", yT3, yT3r)):
                dve.wait_ge(*high_done[key,])
                run(V.tensor_tensor(xr[:, 1], x, xr[:, 0].bitcast(F32), ALU.subtract), low_ready.by(key))
            add_gated(1, 6, [0, 1], gate_b1)

        @block.gpsimd
        def _(pool):
            run = Steps(pool, pool_step)
            G = nc.gpsimd
            n = QH * REL_R
            run(G.memset(rel_pad[0:n, :], 0.0))
            run.settle()
            pool.dma_start(rel_pad[0:n, GRID_W - NA_COLS:GRID_W - NA_COLS + REL_C],
                           A["nat_rpb_2"][0].rearrange("h r c -> (h r) c")).then_inc(rel_loaded, 16)
            pool.wait_ge(rel_loaded, 16)
            run(G.tensor_scalar(rel_pad[0:n, :], rel_pad[0:n, :], 1.0 / SCALE, None, ALU.mult))
            run.settle()
            for c in range(GRID_W):
                run(G.tensor_copy(rel_toep[0:n, c, :], rel_pad[0:n, GRID_W - 1 - c:2 * GRID_W - 1 - c]))
            run.settle()
            pool.dma_start(rel_rows.rearrange("c n k -> n c k"), rel_toep[0:n, :, :]).then_inc(rel_stored, 16)
            pool.wait_ge(rel_stored, 16)
            pool.wait_ge(*merged_ready.at(1, 1))
            pool.dma_start(final_g, A["norm_final"].partition_broadcast(P)).then_inc(final_g_loaded, 16)
            pool.dma_start(fourier_fwd.rearrange("p a b n -> p (a b n)"), C["fourier"][:, 0:4 * SEQ]).then_inc(fourier_loaded, 16)
            pool.wait_ge(*x_added.at(3))
            pool.dma_start(ada_bias[0:2, :], A["b_ada_2"][0].partition_broadcast(2)).then_inc(ada_loaded, 16)
            pool.wait_ge(*heads_ready.at(0, 1))
            for dst, src in ((positions, C["positions"]), (hyena_w1, A["hy_w1_2"][0]), (hyena_w2, A["hy_w2_2"][0])):
                pool.dma_start(dst, src).then_inc(hidden_loaded, 16)
            for u in range(len(units_of_block2(0))):
                pool.wait_ge(*filled("o", 2, u))
            for dst, src in ((decay.rearrange("p t n -> p (t n)"), C["decay"]),
                             (fourier_inv.rearrange("p a b n -> p (a b n)"), C["fourier"][:, 4 * SEQ:8 * SEQ])):
                pool.dma_start(dst, src).then_inc(tables_loaded, 16)
            pool.wait_ge(*out_gated.at("o2"))
            pool.dma_start(w3[0:HID, :, :, :].rearrange("k o d n -> k (o d n)"), A["hy_w3_2"][0]).then_inc(w3_loaded, 16)
            pool.wait_ge(*silu_used.at(0))
            pool.dma_start(skip_b.rearrange("p o n -> p (o n)"),
                           A["hy_skip_2"][0].rearrange("o n -> (o n)").partition_broadcast(P)).then_inc(skip_loaded, 16)
            for s in range(2):
                for c2 in range(2):
                    pool.wait_ge(*emptied("y2", s, c2))
            pool.dma_start(ada_bias3[0:2, :], A["b_ada_2"][1].partition_broadcast(2)).then_inc(ada_bias_loaded, 16)
            pool.wait_ge(*filled("hT", 6, 7))
            for r in range(ROWS):
                part = slice(r % 2 * GRID_W, (r % 2 + 1) * GRID_W)
                src = rel_rows.rearrange("c (h r) k -> c h r k", h=QH)[:, :, NA_ROWS - 1 - r:NA_ROWS - 1 - r + ROWS, :]
                pool.dma_start(rel_bias[part, r // 2, :, :], src.rearrange("c h r k -> c h (r k)")).then_inc(bias_loaded, 16)
            pool.dma_start(mask_w.rearrange("p t n -> p (t n)"), C["mask_w"]).then_inc(bias_loaded, 16)
            pool.dma_start(mask_n, C["mask_n"]).then_inc(bias_loaded, 16)
            pool.wait_ge(bias_loaded, BIASES * 16)
            for t in range(TILES):
                for h in range(QH):
                    b = rel_bias[:, t, h, :].rearrange("p (r c) -> p r c", r=ROWS)
                    ins = G.tensor_tensor(b, b, mask_n.unsqueeze(1).to_broadcast([P, ROWS, GRID_W]), ALU.add)
            ins.then_inc(bias_masked, 1)

        @block.sync
        def _(sp):
            x_rows = A["x"][0].rearrange("(t p) n -> p t n", p=P)
            sp.dma_start(X[:, 0:TILES, :], x_rows).then_inc(x_loaded, 16)
            sp.dma_start(ident[:, :], C["ident"]).then_inc(first_loaded, 16)
            loads = [(tri, C["tri"]), (rope_a[:, :, :].rearrange("p t n -> p (t n)"), C["rope_a"]),
                     (mask_a.rearrange("p g n -> p (g n)"), C["mask_a"]), (mask_b, C["mask_b"]),
                     (mask_c.rearrange("p a n -> p (a n)"), C["mask_c"]),
                     (rope_b[:, :, :].rearrange("p t n -> p (t n)"), C["rope_b"]),
                     (select[:, :, :].rearrange("p t n -> p (t n)"), C["select"]),
                     (sink[:, :], A["win_sink_2"][0].partition_broadcast(P))]
            for n, name in enumerate(("norm_mix", "norm_mlp", "norm_g_2")):
                for l in range(LAYERS):
                    loads.append((g_cols[:, n, l, :], A[name][l].rearrange("(k p) -> p k", p=P)))
            first_gain = loads.pop(8)
            loads.append((cond[:, :, 0], A["c_2"][0].rearrange("(k p) -> p k", p=P)))
            loads.append((cond[:, :, 1], A["c_ctx_2"].rearrange("(k p) -> p k", p=P)))
            for n, name in enumerate(("glob_q", "glob_k", "win_q", "win_k", "nat_q", "nat_k")):
                loads.append((head_gain[:, n, :], A[name + "_norm_2"][0].partition_broadcast(P)))
            for n in range(3):
                loads.append((conv_w[:, n, :], A["hy_conv_w_2"][0, n].rearrange("(c p) -> p c", p=P)))
            loads.append((conv_w[:, 3, :], A["hy_conv_b_2"][0].rearrange("(c p) -> p c", p=P)))
            for n, name in enumerate(("hy_b1_2", "hy_b2_2", "hy_freq_2")):
                loads.append((hid[:, n:n + 1], A[name].rearrange("a n -> n a")))
            assert len(loads) == CONSTS, len(loads)
            with nc.allow_non_contiguous_dma("small vectors, once"):
                sp.dma_start(*first_gain).then_inc(first_loaded, 16)
            rows = lambda w: w.rearrange("(k p) n -> p k n", p=P)
            for n, key in enumerate(HALVES):
                name, l, c, h = key
                s = n % SLOTS
                if n == SLOTS:
                    with nc.allow_non_contiguous_dma("small vectors, once"):
                        for dst, src in loads:
                            sp.dma_start(dst, src).then_inc(consts_loaded, 16)
                    sp.dma_start(X[:, TILES:T4, :], A["ctx_2"][0].rearrange("(t p) n -> p t n", p=P)).then_inc(context_loaded, 16)
                if n >= SLOTS:
                    m = n - SLOTS
                    if m in half_used:
                        sp.wait_ge(*half_used[m])
                    else:
                        sp.wait_ge(split_ready, quarter_at[HALVES[m] + (1,)] + 1)
                cols = slice(c * 512, (c + 1) * 512)
                dst = raw[:, s, :].rearrange("p (k n) -> p k n", k=4)
                if name == "out":
                    parts = ((("w_out_a", 0, 2, 0), ("w_out_b", 0, 2, 2)), (("w_out_b", 2, 3, 0), ("w_out_c", 0, 3, 1)))[h]
                    for w, k0, k1, at_k in parts:
                        sp.dma_start(dst[:, at_k:at_k + k1 - k0, :], rows(A[w][l, k0 * P:k1 * P, cols])).then_inc(half_loaded[s], 16)
                    continue
                if name == "down":
                    dst, src = raw[:, s, :].rearrange("p (k n) -> p k n", k=2), rows(A["w_down"][l, (2 * c + h) * 2 * P:(2 * c + h + 1) * 2 * P, :])
                    sp.dma_start(dst, src).then_inc(half_loaded[s], 16)
                    continue
                w = A[{"in": "w_in", "o": "w_o", "up": "w_up", "ada": "w_ada_2", "in2": "w_in_2", "out2": "w_out_2"}[name]][l]
                a, b = IN2[c] if name == "in2" else (c * 512, (c + 1) * 512)
                if by_features(key):
                    for q in range(2):
                        f = a + (2 * h + q) * P
                        sp.dma_start(raw[:, s, q * QUARTER:(q + 1) * QUARTER].rearrange("p (k n) -> p k n", k=KD),
                                     rows(w[:, f:f + P])).then_inc(half_loaded[s], 16)
                else:
                    dst = raw[:, s, 0:4 * (b - a)].rearrange("p (k n) -> p k n", k=4)
                    sp.dma_start(dst, rows(w[4 * h * P:4 * (h + 1) * P, a:b])).then_inc(half_loaded[s], 16)
            sp.wait_ge(*x_added.at(6))
            sp.dma_start(out.rearrange("(t p) n -> p t n", p=P), X[:, 0:TILES, :]).then_inc(out_stored, 16)
            sp.wait_ge(out_stored, 16)


INPUTS = ["x", "norm_mix", "w_in", "w_out_a", "w_out_b", "w_out_c", "w_o", "norm_mlp", "w_up", "w_down", "norm_final",
          "c_2", "ctx_2", "c_ctx_2", "norm_g_2", "w_ada_2", "b_ada_2", "w_in_2", "w_out_2", "glob_q_norm_2",
          "glob_k_norm_2", "hy_conv_w_2", "hy_conv_b_2", "hy_w1_2", "hy_b1_2", "hy_w2_2", "hy_b2_2", "hy_freq_2",
          "hy_w3_2", "hy_skip_2", "win_q_norm_2", "win_k_norm_2", "win_sink_2", "nat_q_norm_2", "nat_k_norm_2",
          "nat_rpb_2"]


def kernel(**inputs):
    import concourse.bacc as bacc
    from concourse.bass_utils import run_bass_kernel_spmd

    nc = bacc.Bacc("TRN2", target_bir_lowering=False, num_devices=1)
    arrays, A, C = {}, {}, {}
    for name in INPUTS:
        arrays["in_" + name] = np.ascontiguousarray(inputs[name])
        A[name] = nc.dram_tensor("in_" + name, arrays["in_" + name].shape, F32, kind="ExternalInput").ap()
    for name, a in constants().items():
        arrays["const_" + name] = a
        C[name] = nc.dram_tensor("const_" + name, a.shape, F32, kind="ExternalInput").ap()
    out = nc.dram_tensor("out_dram", (SEQ, D), F32, kind="ExternalOutput").ap()
    two_blocks(nc, A, C, out)
    r = run_bass_kernel_spmd(nc, [arrays], core_ids=[0])
    return np.asarray(r.results[0]["out_dram"]).reshape(1, SEQ, D)
```
